# Optimizing a Trainium2 kernel written in Bass

```python
import jax, jax.numpy as jnp
from jax import lax
import numpy as np
import math

D_MODEL = 1024
BATCH = 1
SEQ = 256
DEPTH = 1

NORM_EPS = 1e-6

RWKV_HEAD = 64
RWKV_HEADS = D_MODEL // RWKV_HEAD
RWKV_DIM = RWKV_HEADS * RWKV_HEAD
DECAY_LORA = 64
ICLR_LORA = 64
GATE_LORA = 160
GN_EPS = 64e-5
RWKV_SPLIT = (RWKV_DIM, RWKV_DIM, RWKV_DIM, DECAY_LORA, ICLR_LORA, GATE_LORA)
RWKV_COLS = sum(RWKV_SPLIT)

NSA_HEAD = 64
NSA_HEADS = D_MODEL // NSA_HEAD
NSA_GROUPS = 4
NSA_HPG = NSA_HEADS // NSA_GROUPS
NSA_KV = NSA_GROUPS * NSA_HEAD
CMP_BLOCK = 32
CMP_STRIDE = 16
CMP_HIDDEN = 128
SLC_BLOCK = 64
N_SELECT = 16
WINDOW = 512
Q_BLOCK = 128
NSA_SPLIT = (NSA_HEADS * NSA_HEAD,) + (NSA_KV,) * 6 + (3 * NSA_HEADS,)
NSA_COLS = sum(NSA_SPLIT)

GATE_COLS = 2 * D_MODEL
IN_COLS = RWKV_COLS + NSA_COLS + GATE_COLS

D_FF = ((8 * D_MODEL // 3 + 255) // 256) * 256
CONV_W = 3

NEG_INF = -1e30
TINY = 1e-30
FORCE = 1e9


def rms_norm(x, g):
    xf = x.astype(jnp.float32)
    y = xf * lax.rsqrt(jnp.mean(xf * xf, axis=-1, keepdims=True) + NORM_EPS)
    return (y * g.astype(jnp.float32)).astype(x.dtype)

def masked_softmax(s, mask, axis):
    s = jnp.where(mask, s, NEG_INF)
    e = jnp.where(mask, jnp.exp(s - jnp.max(s, axis=axis, keepdims=True)), 0.0)
    return e / jnp.maximum(jnp.sum(e, axis=axis, keepdims=True), TINY)

def alibi_slopes():
    h = jnp.arange(1, NSA_HEADS + 1, dtype=jnp.float32)
    return jnp.exp2(-8.0 * h / NSA_HEADS).reshape(NSA_GROUPS, NSA_HPG)

def split_cols(z, widths):
    return jnp.split(z, [int(c) for c in np.cumsum(widths)[:-1]], axis=-1)

def wkv7_scan(r, w, k, v, a, b):
    B, _, H, N = r.shape

    def step(state, inp):
        r_t, w_t, k_t, v_t, a_t, b_t = inp
        sa = jnp.einsum('bhvk,bhk->bhv', state, a_t)
        state = (state * w_t[:, :, None, :] + sa[..., None] * b_t[:, :, None, :]
                 + v_t[..., None] * k_t[:, :, None, :])
        return state, jnp.einsum('bhvk,bhk->bhv', state, r_t)

    tm = lambda t: jnp.moveaxis(t, 1, 0)
    state0 = jnp.zeros((B, H, N, N), jnp.float32)
    _, y = lax.scan(step, state0, (tm(r), tm(w), tm(k), tm(v), tm(a), tm(b)))
    return jnp.moveaxis(y, 0, 1)

def rwkv7_time_mix(z, mu, w0, w2, a0, a2, g2, k_k, k_a, r_k, ln_w, ln_b):
    B, S, _ = z.shape
    f32 = jnp.float32
    prev = jnp.pad(z, ((0, 0), (1, 0), (0, 0)))[:, :-1]
    z = z + (prev - z) * mu
    r, k, v, wd, ad, gd = split_cols(z, RWKV_SPLIT)
    w_log = -jax.nn.softplus(-(w0 + jnp.tanh(wd) @ w2)) - 0.5
    decay = jnp.exp(-jnp.exp(w_log.astype(f32)))
    a = jax.nn.sigmoid(a0 + ad @ a2)
    g = jax.nn.sigmoid(gd) @ g2
    heads = lambda t: t.reshape(B, S, RWKV_HEADS, RWKV_HEAD).astype(f32)
    kk = heads(k * k_k)
    kk = kk / jnp.maximum(jnp.sqrt(jnp.sum(kk * kk, axis=-1, keepdims=True)), 1e-12)
    k = k * (1.0 + (a - 1.0) * k_a)
    r_h, k_h, v_h, a_h = heads(r), heads(k), heads(v), heads(a)
    y = wkv7_scan(r_h, heads(decay), k_h, v_h, -kk, kk * a_h)
    mean = jnp.mean(y, axis=-1, keepdims=True)
    var = jnp.mean(jnp.square(y - mean), axis=-1, keepdims=True)
    y = ((y - mean) * lax.rsqrt(var + GN_EPS)).reshape(B, S, RWKV_DIM)
    y = y * ln_w.astype(f32) + ln_b.astype(f32)
    bonus = jnp.sum(r_h * k_h * r_k.astype(f32), axis=-1, keepdims=True) * v_h
    y = y + bonus.reshape(B, S, RWKV_DIM)
    return (y * g.astype(f32)).astype(z.dtype)

def nsa_attention(z, cmp_pos_k, cmp_w1_k, cmp_w2_k, cmp_pos_v, cmp_w1_v, cmp_w2_v):
    B, S, _ = z.shape
    f32 = jnp.float32
    G, HG, DH = NSA_GROUPS, NSA_HPG, NSA_HEAD
    q, kc, vc, ks, vs, kw, vw, gl = split_cols(z, NSA_SPLIT)
    q = (q.astype(f32) * DH ** -0.5).reshape(B, S, G, HG, DH).transpose(0, 2, 3, 1, 4)
    gates = jax.nn.sigmoid(gl.astype(f32)).reshape(B, S, G, HG, 3).transpose(0, 2, 3, 1, 4)
    kv = lambda t: t.astype(f32).reshape(B, S, G, DH).transpose(0, 2, 1, 3)

    n_cmp = (S - CMP_BLOCK) // CMP_STRIDE + 1
    cidx = np.arange(n_cmp)[:, None] * CMP_STRIDE + np.arange(CMP_BLOCK)[None, :]

    def compress(t, pos, w1, w2):
        blk = kv(t)[:, :, cidx] + pos.astype(f32)
        hid = jax.nn.gelu(blk.reshape(B, G, n_cmp, CMP_BLOCK * DH) @ w1.astype(f32))
        return hid @ w2.astype(f32)

    k_cmp = compress(kc, cmp_pos_k, cmp_w1_k, cmp_w2_k)
    v_cmp = compress(vc, cmp_pos_v, cmp_w1_v, cmp_w2_v)
    cmp_end = jnp.asarray(cidx[:, -1], jnp.int32)
    cmp_mid = jnp.asarray(cidx.mean(axis=1), jnp.float32)

    n_sel = S // SLC_BLOCK
    top = min(N_SELECT, n_sel)
    k_slc = kv(ks).reshape(B, G, n_sel, SLC_BLOCK, DH)
    v_slc = kv(vs).reshape(B, G, n_sel, SLC_BLOCK, DH)
    r1, r2 = SLC_BLOCK // CMP_STRIDE, CMP_BLOCK // CMP_STRIDE
    off = np.array([m - n for m in range(r1) for n in range(r2)])
    imap_np = np.arange(n_sel)[:, None] * r1 + off[None, :]
    imap_ok = jnp.asarray((imap_np >= 0) & (imap_np < n_cmp))
    imap = jnp.asarray(np.clip(imap_np, 0, n_cmp - 1), jnp.int32)
    bi = jnp.arange(B)[:, None, None, None]
    gi = jnp.arange(G)[None, :, None, None]

    k_win = jnp.pad(kv(kw), ((0, 0), (0, 0), (WINDOW, 0), (0, 0)))
    v_win = jnp.pad(kv(vw), ((0, 0), (0, 0), (WINDOW, 0), (0, 0)))

    slopes = alibi_slopes()[None, :, :, None, None]

    def block(i):
        t0 = i * Q_BLOCK
        qb = lax.dynamic_slice_in_dim(q, t0, Q_BLOCK, axis=3)
        gb = lax.dynamic_slice_in_dim(gates, t0, Q_BLOCK, axis=3)
        t = t0 + jnp.arange(Q_BLOCK, dtype=jnp.int32)
        tf = t.astype(f32)

        s_c = jnp.einsum('bghtd,bgnd->bghtn', qb, k_cmp) - slopes * (tf[:, None] - cmp_mid[None, :])
        p_c = masked_softmax(s_c, cmp_end[None, :] <= t[:, None], -1)
        o_c = jnp.einsum('bghtn,bgnd->bghtd', p_c, v_cmp)

        imp_c = jnp.sum(p_c, axis=2)
        imp = jnp.sum(jnp.where(imap_ok, imp_c[..., imap], 0.0), axis=-1)
        cur = (t // SLC_BLOCK)[:, None]
        jb = jnp.arange(n_sel, dtype=jnp.int32)[None, :]
        forced = (jb == 0) | (jb == cur) | (jb == cur - 1)
        score = jnp.where(jb <= cur, jnp.where(forced, FORCE, imp), NEG_INF)
        vals, idx = lax.top_k(score, top)
        kg = k_slc[bi, gi, idx]
        vg = v_slc[bi, gi, idx]
        pos = idx[..., None] * SLC_BLOCK + jnp.arange(SLC_BLOCK, dtype=jnp.int32)
        dist_s = t[:, None, None] - pos
        mask_s = ((vals > 0.5 * NEG_INF)[..., None] & (dist_s >= 0))[:, :, None]
        s_s = (jnp.einsum('bghtd,bgtnld->bghtnl', qb, kg)
               - slopes[..., None] * dist_s.astype(f32)[:, :, None])
        p_s = masked_softmax(s_s, mask_s, (-2, -1))
        o_s = jnp.einsum('bghtnl,bgtnld->bghtd', p_s, vg)

        kwb = lax.dynamic_slice_in_dim(k_win, t0, Q_BLOCK + WINDOW, axis=2)
        vwb = lax.dynamic_slice_in_dim(v_win, t0, Q_BLOCK + WINDOW, axis=2)
        spos = t0 - WINDOW + jnp.arange(Q_BLOCK + WINDOW, dtype=jnp.int32)
        dist_w = t[:, None] - spos[None, :]
        mask_w = (spos[None, :] >= 0) & (dist_w >= 0) & (dist_w < WINDOW)
        s_w = jnp.einsum('bghtd,bgsd->bghts', qb, kwb) - slopes * dist_w.astype(f32)
        p_w = masked_softmax(s_w, mask_w, -1)
        o_w = jnp.einsum('bghts,bgsd->bghtd', p_w, vwb)

        return gb[..., 0:1] * o_c + gb[..., 1:2] * o_s + gb[..., 2:3] * o_w

    out = lax.map(block, jnp.arange(S // Q_BLOCK, dtype=jnp.int32))
    out = out.transpose(1, 0, 4, 2, 3, 5).reshape(B, S, NSA_HEADS * DH)
    return out.astype(z.dtype)

def causal_dwconv(u, w, b):
    C = u.shape[-1]
    y = lax.conv_general_dilated(u, w[:, None, :].astype(u.dtype), window_strides=(1,),
                                 padding=[(CONV_W - 1, 0)],
                                 dimension_numbers=('NWC', 'WIO', 'NWC'),
                                 feature_group_count=C)
    return y + b

def first_inputs(seed: int = 0) -> dict:
    key = jax.random.key(seed)
    ks = jax.random.split(key, 32)
    f32 = jnp.float32
    L = DEPTH
    nrm = lambda k, shape, scale: jax.random.normal(k, shape, f32) * scale
    gain = lambda k, n: 1.0 + 0.05 * jax.random.normal(k, (L, n), f32)
    return {
        "x": jax.random.normal(ks[0], (BATCH, SEQ, D_MODEL), f32),
        "norm_mix_pre": gain(ks[1], D_MODEL),
        "norm_mix_post": gain(ks[2], D_MODEL),
        "norm_ffn_pre": gain(ks[3], D_MODEL),
        "norm_ffn_post": gain(ks[4], D_MODEL),
        "w_in": nrm(ks[5], (L, D_MODEL, IN_COLS), D_MODEL ** -0.5),
        "rwkv_mu": jax.random.uniform(ks[6], (L, RWKV_COLS), f32),
        "rwkv_w0": jax.random.uniform(ks[7], (L, RWKV_DIM), f32, minval=-6.0, maxval=0.0),
        "rwkv_w2": nrm(ks[8], (L, DECAY_LORA, RWKV_DIM), DECAY_LORA ** -0.5),
        "rwkv_a0": nrm(ks[9], (L, RWKV_DIM), 0.1),
        "rwkv_a2": nrm(ks[10], (L, ICLR_LORA, RWKV_DIM), ICLR_LORA ** -0.5),
        "rwkv_g2": nrm(ks[11], (L, GATE_LORA, RWKV_DIM), GATE_LORA ** -0.5),
        "rwkv_k_k": 0.85 + nrm(ks[12], (L, RWKV_DIM), 0.05),
        "rwkv_k_a": 1.0 + nrm(ks[13], (L, RWKV_DIM), 0.05),
        "rwkv_r_k": nrm(ks[14], (L, RWKV_HEADS, RWKV_HEAD), 0.1),
        "rwkv_ln_w": gain(ks[15], RWKV_DIM),
        "rwkv_ln_b": nrm(ks[16], (L, RWKV_DIM), 0.02),
        "cmp_pos_k": nrm(ks[17], (L, CMP_BLOCK, NSA_HEAD), 0.1),
        "cmp_w1_k": nrm(ks[18], (L, CMP_BLOCK * NSA_HEAD, CMP_HIDDEN), (CMP_BLOCK * NSA_HEAD) ** -0.5),
        "cmp_w2_k": nrm(ks[19], (L, CMP_HIDDEN, NSA_HEAD), CMP_HIDDEN ** -0.5),
        "cmp_pos_v": nrm(ks[20], (L, CMP_BLOCK, NSA_HEAD), 0.1),
        "cmp_w1_v": nrm(ks[21], (L, CMP_BLOCK * NSA_HEAD, CMP_HIDDEN), (CMP_BLOCK * NSA_HEAD) ** -0.5),
        "cmp_w2_v": nrm(ks[22], (L, CMP_HIDDEN, NSA_HEAD), CMP_HIDDEN ** -0.5),
        "w_branch_rwkv": nrm(ks[23], (L, RWKV_DIM, D_MODEL), RWKV_DIM ** -0.5),
        "w_branch_nsa": nrm(ks[24], (L, NSA_HEADS * NSA_HEAD, D_MODEL), (NSA_HEADS * NSA_HEAD) ** -0.5),
        "w_out": nrm(ks[25], (L, D_MODEL, D_MODEL), D_MODEL ** -0.5),
        "ffn_up": nrm(ks[26], (L, D_MODEL, 2 * D_FF), D_MODEL ** -0.5),
        "ffn_conv_w": nrm(ks[27], (L, CONV_W, 2 * D_FF), CONV_W ** -0.5),
        "ffn_conv_b": nrm(ks[28], (L, 2 * D_FF), 0.02),
        "ffn_down": nrm(ks[29], (L, D_FF, D_MODEL), D_FF ** -0.5),
    }

def first_block(x, norm_mix_pre, norm_mix_post, norm_ffn_pre, norm_ffn_post, w_in,
              rwkv_mu, rwkv_w0, rwkv_w2, rwkv_a0, rwkv_a2, rwkv_g2, rwkv_k_k, rwkv_k_a,
              rwkv_r_k, rwkv_ln_w, rwkv_ln_b,
              cmp_pos_k, cmp_w1_k, cmp_w2_k, cmp_pos_v, cmp_w1_v, cmp_w2_v,
              w_branch_rwkv, w_branch_nsa, w_out,
              ffn_up, ffn_conv_w, ffn_conv_b, ffn_down):
    for l in range(DEPTH):
        h = rms_norm(x, norm_mix_pre[l])
        z = h @ w_in[l]
        z_rwkv, z_nsa, z_gate = jnp.split(z, [RWKV_COLS, RWKV_COLS + NSA_COLS], axis=-1)
        o_a = rwkv7_time_mix(z_rwkv, rwkv_mu[l], rwkv_w0[l], rwkv_w2[l], rwkv_a0[l],
                             rwkv_a2[l], rwkv_g2[l], rwkv_k_k[l], rwkv_k_a[l],
                             rwkv_r_k[l], rwkv_ln_w[l], rwkv_ln_b[l])
        o_b = nsa_attention(z_nsa, cmp_pos_k[l], cmp_w1_k[l], cmp_w2_k[l],
                            cmp_pos_v[l], cmp_w1_v[l], cmp_w2_v[l])
        g_a, g_b = jnp.split(jax.nn.sigmoid(z_gate), 2, axis=-1)
        m = g_a * (o_a @ w_branch_rwkv[l]) + g_b * (o_b @ w_branch_nsa[l])
        x = x + rms_norm(m @ w_out[l], norm_mix_post[l])
        h = rms_norm(x, norm_ffn_pre[l])
        u = causal_dwconv(h @ ffn_up[l], ffn_conv_w[l], ffn_conv_b[l])
        u_gate, u_val = jnp.split(u, 2, axis=-1)
        x = x + rms_norm((jax.nn.silu(u_gate) * u_val) @ ffn_down[l], norm_ffn_post[l])
    return x


DEPTH_2 = 2

BLOCK = 128
EPS = 1e-6
HEAD_DIM = 64
SB_HEADS = 8
SW_HEADS = 8
SW_KV_HEADS = 2
SW_GROUP = SW_HEADS // SW_KV_HEADS
WINDOW_2 = 128
SB_WIDTH = SB_HEADS * HEAD_DIM
SW_Q_WIDTH = SW_HEADS * HEAD_DIM
SW_KV_WIDTH = SW_KV_HEADS * HEAD_DIM
EVEN_SPLITS = [SB_WIDTH, SB_WIDTH, SB_WIDTH, SW_Q_WIDTH, SW_KV_WIDTH, SW_KV_WIDTH]
EVEN_IN_WIDTH = sum(EVEN_SPLITS)
EVEN_OUT_WIDTH = SB_WIDTH + SW_Q_WIDTH
REL_BUCKETS = 32
REL_MAX_DIST = 128
MLA_HEADS = 16
MLA_NOPE_DIM = 64
MLA_ROPE_DIM = 32
MLA_V_DIM = 64
MLA_Q_RANK = 384
MLA_KV_RANK = 256
MLA_DOWN_WIDTH = MLA_Q_RANK + MLA_KV_RANK + MLA_ROPE_DIM
ROPE_THETA = 10000.0
FFN_HIDDEN = -(-8 * D_MODEL // (3 * 256)) * 256
N_EVEN = (DEPTH_2 + 1) // 2
N_ODD = DEPTH_2 // 2


F32 = jnp.float32

def rmsnorm(x, g):
    xf = x.astype(F32)
    y = xf * lax.rsqrt(jnp.mean(xf * xf, axis=-1, keepdims=True) + EPS)
    return (y * g.astype(F32)).astype(x.dtype)

def t5_bucket(rel):
    max_exact = REL_BUCKETS // 2
    rel = jnp.maximum(rel, 0)
    relf = jnp.maximum(rel, 1).astype(F32)
    large = max_exact + (jnp.log(relf / max_exact) / math.log(REL_MAX_DIST / max_exact)
                         * (REL_BUCKETS - max_exact)).astype(jnp.int32)
    large = jnp.minimum(large, REL_BUCKETS - 1)
    return jnp.where(rel < max_exact, rel, large)

def stick_breaking_attention(q, k, v):
    B_, S, H, d = q.shape
    nb = S // BLOCK
    scale = d ** -0.5
    qb = q.reshape(B_, nb, BLOCK, H, d).transpose(1, 0, 3, 2, 4)
    key_pos = jnp.arange(S)

    def one_block(args):
        q_blk, i = args
        z = jnp.einsum('bhqd,bshd->bhqs', q_blk, k, preferred_element_type=F32) * scale
        q_pos = i * BLOCK + jnp.arange(BLOCK)
        causal = key_pos[None, :] < q_pos[:, None]
        log_beta = jax.nn.log_sigmoid(z)
        log_1m_beta = jnp.where(causal, jax.nn.log_sigmoid(-z), 0.0)
        between = lax.cumsum(log_1m_beta, axis=3, reverse=True) - log_1m_beta
        w = jnp.where(causal, jnp.exp(log_beta + between), 0.0)
        return jnp.einsum('bhqs,bshd->bqhd', w.astype(v.dtype), v)

    out = lax.map(one_block, (qb, jnp.arange(nb)))
    return out.transpose(1, 0, 2, 3, 4).reshape(B_, S, H * d)

def sliding_window_attention(q, k, v, sinks, rel_bias_table):
    B_, S, Hq, d = q.shape
    Hkv = k.shape[2]
    G = Hq // Hkv
    nb = S // BLOCK
    qb = q.reshape(B_, nb, BLOCK, Hkv, G, d)

    def banded(t):
        tb = t.reshape(B_, nb, BLOCK, Hkv, d)
        prev = jnp.concatenate([jnp.zeros_like(tb[:, :1]), tb[:, :-1]], axis=1)
        return jnp.concatenate([prev, tb], axis=2)

    kb, vb = banded(k), banded(v)
    logits = jnp.einsum('bnqkgd,bnskd->bnkgqs', qb, kb, preferred_element_type=F32) * d ** -0.5
    rel = BLOCK + jnp.arange(BLOCK)[:, None] - jnp.arange(2 * BLOCK)[None, :]
    in_window = (rel >= 0) & (rel < WINDOW_2)
    key_pos = (jnp.arange(nb)[:, None] - 1) * BLOCK + jnp.arange(2 * BLOCK)[None, :]
    valid = in_window[None] & (key_pos >= 0)[:, None, :]
    bias = rel_bias_table.astype(F32)[t5_bucket(rel)]
    bias = bias.transpose(2, 0, 1).reshape(Hkv, G, BLOCK, 2 * BLOCK)
    logits = jnp.where(valid[None, :, None, None], logits + bias, -jnp.inf)
    sink = sinks.astype(F32).reshape(Hkv, G)[:, :, None, None]
    m = jnp.maximum(jnp.max(logits, axis=-1, keepdims=True), sink)
    p = jnp.exp(logits - m)
    p = p / (jnp.sum(p, axis=-1, keepdims=True) + jnp.exp(sink - m))
    out = jnp.einsum('bnkgqs,bnskd->bnqkgd', p.astype(v.dtype), vb)
    return out.reshape(B_, S, Hq * d)

def rope(x, positions):
    half = x.shape[-1] // 2
    freqs = ROPE_THETA ** (-jnp.arange(half, dtype=F32) / half)
    ang = positions.astype(F32)[..., None] * freqs
    cos = jnp.cos(ang)[:, :, None, :]
    sin = jnp.sin(ang)[:, :, None, :]
    x1 = x[..., :half].astype(F32)
    x2 = x[..., half:].astype(F32)
    return jnp.concatenate([x1 * cos - x2 * sin, x2 * cos + x1 * sin], axis=-1).astype(x.dtype)

def mla_attention(q_nope, q_rope, k_nope, k_rope, v):
    B_, S, H, _ = q_nope.shape
    nb = S // BLOCK
    scale = (MLA_NOPE_DIM + MLA_ROPE_DIM) ** -0.5
    qn = q_nope.reshape(B_, nb, BLOCK, H, MLA_NOPE_DIM).transpose(1, 0, 2, 3, 4)
    qr = q_rope.reshape(B_, nb, BLOCK, H, MLA_ROPE_DIM).transpose(1, 0, 2, 3, 4)
    key_pos = jnp.arange(S)

    def one_block(args):
        qn_blk, qr_blk, i = args
        s = (jnp.einsum('bqhd,bshd->bhqs', qn_blk, k_nope, preferred_element_type=F32)
             + jnp.einsum('bqhr,bsr->bhqs', qr_blk, k_rope, preferred_element_type=F32)) * scale
        q_pos = i * BLOCK + jnp.arange(BLOCK)
        s = jnp.where(key_pos[None, :] <= q_pos[:, None], s, -jnp.inf)
        p = jax.nn.softmax(s, axis=-1)
        return jnp.einsum('bhqs,bshd->bqhd', p.astype(v.dtype), v)

    out = lax.map(one_block, (qn, qr, jnp.arange(nb)))
    return out.transpose(1, 0, 2, 3, 4).reshape(B_, S, H * MLA_V_DIM)

def even_mixer(h, w_in, sinks, rel_bias_table, w_out):
    B_, S, _ = h.shape
    proj = h @ w_in
    q_a, k_a, v_a, q_b, k_b, v_b = jnp.split(proj, list(np.cumsum(EVEN_SPLITS)[:-1]), axis=-1)
    hd = lambda t, n: t.reshape(B_, S, n, HEAD_DIM)
    o_a = stick_breaking_attention(hd(q_a, SB_HEADS), hd(k_a, SB_HEADS), hd(v_a, SB_HEADS))
    o_b = sliding_window_attention(hd(q_b, SW_HEADS), hd(k_b, SW_KV_HEADS), hd(v_b, SW_KV_HEADS),
                                   sinks, rel_bias_table)
    return jnp.concatenate([o_a, o_b], axis=-1) @ w_out

def mla_mixer(h, positions, w_down, q_norm, w_uq, kv_norm, w_ukv, w_o):
    B_, S, _ = h.shape
    down = h @ w_down
    c_q = down[..., :MLA_Q_RANK]
    c_kv = down[..., MLA_Q_RANK:MLA_Q_RANK + MLA_KV_RANK]
    k_rope = down[..., MLA_Q_RANK + MLA_KV_RANK:]
    q = (rmsnorm(c_q, q_norm) @ w_uq).reshape(B_, S, MLA_HEADS, MLA_NOPE_DIM + MLA_ROPE_DIM)
    q_nope = q[..., :MLA_NOPE_DIM]
    q_rope = rope(q[..., MLA_NOPE_DIM:], positions)
    kv = (rmsnorm(c_kv, kv_norm) @ w_ukv).reshape(B_, S, MLA_HEADS, MLA_NOPE_DIM + MLA_V_DIM)
    k_nope = kv[..., :MLA_NOPE_DIM]
    v = kv[..., MLA_NOPE_DIM:]
    k_rope = rope(k_rope[:, :, None, :], positions)[:, :, 0, :]
    return mla_attention(q_nope, q_rope, k_nope, k_rope, v) @ w_o

def swiglu(h, w_gate, w_up, w_down):
    return (jax.nn.silu(h @ w_gate) * (h @ w_up)) @ w_down

def second_inputs(seed: int = 0) -> dict:
    key = jax.random.key(seed)
    ks = jax.random.split(key, 20)
    nrm = lambda k, shape, fan_in: jax.random.normal(k, shape, F32) * fan_in ** -0.5
    gain = lambda k, shape: 1.0 + 0.02 * jax.random.normal(k, shape, F32)
    x = jax.random.normal(ks[0], (BATCH, SEQ, D_MODEL), F32)
    offsets = jax.random.randint(ks[1], (BATCH, 1), 0, 1024, dtype=jnp.int32)
    positions = (jnp.arange(SEQ, dtype=jnp.int32)[None, :] + offsets).astype(jnp.int32)
    return {
        "x": x,
        "positions": positions,
        "attn_norm": gain(ks[2], (DEPTH_2, D_MODEL)),
        "ffn_norm": gain(ks[3], (DEPTH_2, D_MODEL)),
        "even_w_in": nrm(ks[4], (N_EVEN, D_MODEL, EVEN_IN_WIDTH), D_MODEL),
        "even_sinks": 0.5 * jax.random.normal(ks[5], (N_EVEN, SW_HEADS), F32),
        "even_w_out": nrm(ks[6], (N_EVEN, EVEN_OUT_WIDTH, D_MODEL), EVEN_OUT_WIDTH),
        "rel_bias_table": 0.5 * jax.random.normal(ks[7], (REL_BUCKETS, SW_HEADS), F32),
        "mla_w_down": nrm(ks[8], (N_ODD, D_MODEL, MLA_DOWN_WIDTH), D_MODEL),
        "mla_q_norm": gain(ks[9], (N_ODD, MLA_Q_RANK)),
        "mla_w_uq": nrm(ks[10], (N_ODD, MLA_Q_RANK, MLA_HEADS * (MLA_NOPE_DIM + MLA_ROPE_DIM)), MLA_Q_RANK),
        "mla_kv_norm": gain(ks[11], (N_ODD, MLA_KV_RANK)),
        "mla_w_ukv": nrm(ks[12], (N_ODD, MLA_KV_RANK, MLA_HEADS * (MLA_NOPE_DIM + MLA_V_DIM)), MLA_KV_RANK),
        "mla_w_o": nrm(ks[13], (N_ODD, MLA_HEADS * MLA_V_DIM, D_MODEL), MLA_HEADS * MLA_V_DIM),
        "ffn_w_gate": nrm(ks[14], (DEPTH_2, D_MODEL, FFN_HIDDEN), D_MODEL),
        "ffn_w_up": nrm(ks[15], (DEPTH_2, D_MODEL, FFN_HIDDEN), D_MODEL),
        "ffn_w_down": nrm(ks[16], (DEPTH_2, FFN_HIDDEN, D_MODEL), FFN_HIDDEN),
        "final_norm": gain(ks[17], (D_MODEL,)),
    }

def second_block(x, positions, attn_norm, ffn_norm, even_w_in, even_sinks, even_w_out, rel_bias_table,
              mla_w_down, mla_q_norm, mla_w_uq, mla_kv_norm, mla_w_ukv, mla_w_o,
              ffn_w_gate, ffn_w_up, ffn_w_down, final_norm):
    for layer in range(DEPTH_2):
        h = rmsnorm(x, attn_norm[layer])
        if layer % 2 == 0:
            e = layer // 2
            x = x + even_mixer(h, even_w_in[e], even_sinks[e], rel_bias_table, even_w_out[e])
        else:
            o = layer // 2
            x = x + mla_mixer(h, positions, mla_w_down[o], mla_q_norm[o], mla_w_uq[o],
                              mla_kv_norm[o], mla_w_ukv[o], mla_w_o[o])
        h = rmsnorm(x, ffn_norm[layer])
        x = x + swiglu(h, ffn_w_gate[layer], ffn_w_up[layer], ffn_w_down[layer])
    return rmsnorm(x, final_norm)


def setup_inputs(seed=0):
    out = dict(first_inputs(seed))
    for name, value in second_inputs(seed + 1).items():
        if name != "x":
            out[name + "_2"] = value
    return out


def reference(
    x, norm_mix_pre, norm_mix_post, norm_ffn_pre, norm_ffn_post, w_in, rwkv_mu, rwkv_w0,
    rwkv_w2, rwkv_a0, rwkv_a2, rwkv_g2, rwkv_k_k, rwkv_k_a, rwkv_r_k, rwkv_ln_w, rwkv_ln_b,
    cmp_pos_k, cmp_w1_k, cmp_w2_k, cmp_pos_v, cmp_w1_v, cmp_w2_v, w_branch_rwkv, w_branch_nsa,
    w_out, ffn_up, ffn_conv_w, ffn_conv_b, ffn_down, positions_2, attn_norm_2, ffn_norm_2,
    even_w_in_2, even_sinks_2, even_w_out_2, rel_bias_table_2, mla_w_down_2, mla_q_norm_2,
    mla_w_uq_2, mla_kv_norm_2, mla_w_ukv_2, mla_w_o_2, ffn_w_gate_2, ffn_w_up_2, ffn_w_down_2,
    final_norm_2,
):
    x = first_block(
        x, norm_mix_pre, norm_mix_post, norm_ffn_pre, norm_ffn_post, w_in, rwkv_mu, rwkv_w0,
        rwkv_w2, rwkv_a0, rwkv_a2, rwkv_g2, rwkv_k_k, rwkv_k_a, rwkv_r_k, rwkv_ln_w, rwkv_ln_b,
        cmp_pos_k, cmp_w1_k, cmp_w2_k, cmp_pos_v, cmp_w1_v, cmp_w2_v, w_branch_rwkv,
        w_branch_nsa, w_out, ffn_up, ffn_conv_w, ffn_conv_b, ffn_down,
    )
    return second_block(
        x, positions_2, attn_norm_2, ffn_norm_2, even_w_in_2, even_sinks_2, even_w_out_2,
        rel_bias_table_2, mla_w_down_2, mla_q_norm_2, mla_w_uq_2, mla_kv_norm_2, mla_w_ukv_2,
        mla_w_o_2, ffn_w_gate_2, ffn_w_up_2, ffn_w_down_2, final_norm_2,
    )


_drawn_inputs = setup_inputs


def setup_inputs(seed=0):
    import zlib

    import numpy as np

    out = dict(_drawn_inputs(seed))
    spreads = {}
    factors = {'rwkv_ln_b': 3.568,
     'cmp_pos_k': 8.0,
     'ffn_conv_b': 3.046,
     'attn_norm_2': 6.861,
     'ffn_norm_2': 4.414,
     'even_sinks_2': 8.0,
     'mla_q_norm_2': 8.0,
     'mla_kv_norm_2': 8.0,
     'final_norm_2': 2.842}
    for name, (base, spread) in spreads.items():
        noise = np.random.default_rng([zlib.crc32(name.encode()), seed]).standard_normal(out[name].shape)
        drawn = base * np.exp(spread * noise) if base else spread * noise
        out[name] = __import__('jax').numpy.asarray(drawn.astype(out[name].dtype))
    for name, factor in factors.items():
        out[name] = (out[name] * factor).astype(out[name].dtype)
    return out
```

```python
from contextlib import ExitStack
import math

import numpy as np
import concourse.bass as bass
from concourse import mybir

F32 = mybir.dt.float32
I32 = mybir.dt.int32
ALU = mybir.AluOpType
ACT = mybir.ActivationFunctionType
AX = mybir.AxisListType.X

P = 128
S = 256
D = 1024
KT = D // P
NB = S // P
HD = 64
H = D // HD
PAIRS = H // 2
CH = 64
NC = S // CH
GROUPS = 4
HPG = H // GROUPS
N_CMP = (S - 32) // 16 + 1
SB_HEADS = 8
SW_HEADS = 8
Q_RANK, KV_RANK, ROPE = 384, 256, 32
F_FF = 2816
FT = F_FF // P
RING = 4
UNIT = 2048
BIG = 1e30
C_DECAY = math.exp(-0.5)
SCALE = HD ** -0.5
MLA_SCALE = (HD + ROPE) ** -0.5
KEYS = P + S

PLAN = [("lora", 1), ("rwkv", 16), ("nsa_q", 4), ("nsa_k", 4), ("nsa_v", 2), ("cmp", 2),
        ("gate_b", 4), ("branch", 8), ("w_out", 4), ("up0", FT), ("down0", FT // 2),
        ("even_f", 6), ("even_kv", 1), ("even_v", 2), ("even_out", 4),
        ("up1", FT), ("down1", FT // 2),
        ("mla_down", 3), ("mla_uq", 4), ("mla_uk", 1), ("mla_uv", 1), ("mla_out", 4),
        ("up2", FT), ("down2", FT // 2)]
U = {}
N_UNITS = 0
for _name, _n in PLAN:
    U[_name] = N_UNITS
    N_UNITS += _n

CONST = [("ident", 128), ("headsum", 128), ("ones", 128), ("chunk", 256), ("tri", 128),
         ("dist", KEYS), ("causal", KEYS), ("strict", KEYS), ("nstrict", KEYS),
         ("cmpbias", GROUPS * 8 * N_CMP), ("slope", H), ("rope", 3)]
CO = {}
N_CONST = 0
for _name, _n in CONST:
    CO[_name] = (N_CONST, N_CONST + _n)
    N_CONST += _n

SMALL = [("w_small", KT * 80), ("mu_lora", 3), ("g_mix", KT), ("g_ffn", KT), ("g_attn2", 2 * KT),
         ("g_ffn2", 2 * KT), ("g_q", 3), ("g_kv", 2), ("conv", FT * 8), ("cmp_w2", 128),
         ("cmp_pos", 64), ("sinks", 8)]
SO = {}
N_SMALL = 0
for _name, _n in SMALL:
    SO[_name] = (N_SMALL, N_SMALL + _n)
    N_SMALL += _n

_P1 = float(np.float32(6.28125))
_P2 = float(np.float32(round((2 * math.pi - _P1) * 2 ** 20) / 2 ** 20))
TWO_PI = (_P1, _P2, 2 * math.pi - _P1 - _P2)

AUX = 384 + 16
(MU_R, MU_K, MU_V, W0, A0, K_K, K_A, R_K, LN_W, LN_B) = range(384, 394)


def build(nc, ins, out):
    weights, aux_d, const_d, small_d, rows_d, swbias_d, x_d, pos_d = ins
    with ExitStack() as ctx:
        def sb(name, shape, dt=F32):
            return ctx.enter_context(nc.sbuf_tensor(name, shape, dt))

        def sem(name):
            return ctx.enter_context(nc.semaphore(name))

        ps = [ctx.enter_context(nc.psum_tensor(f"ps{i}", [P, 512], F32)) for i in range(8)]
        ring = sb("ring", [P, RING, UNIT])
        x = sb("x", [P, NB, D])
        xn = sb("xn", [P, NB, D])
        hT = sb("hT", [P, KT, S])
        oT = sb("oT", [P, KT, S])
        cst = sb("cst", [P, N_CONST])
        sml = sb("sml", [P, N_SMALL])
        grow = sb("grow", [P, D])
        pos_i = sb("pos_i", [P, S], I32)
        stat = sb("stat", [P, 8])
        gates = sb("gates", [P, NB, 48])
        q_st = sb("q_st", [P, 2, S])
        b_st = sb("b_st", [P, 2, KEYS])
        sc = sb("sc", [P, 2, KEYS])
        pT = sb("pT", [P, 2, KEYS])
        mx = sb("mx", [P, 2, 8])
        mx2 = sb("mx2", [P, 2, 8])
        sink_st = sb("sink_st", [P, 2])
        arena = sb("arena", [P, 28400])
        top = [0]

        def carve(*shape):
            n = int(np.prod(shape))
            a = arena[:, top[0]:top[0] + n]
            top[0] += n
            assert top[0] <= 28400, top[0]
            if len(shape) == 1:
                return a
            names = "abcd"[:len(shape)]
            pat = f"p ({' '.join(names)}) -> p {' '.join(names)}"
            return a.rearrange(pat, **{k: v for k, v in zip(names, shape)})

        def const(name):
            return cst[:, CO[name][0]:CO[name][1]]

        def small(name):
            return sml[:, SO[name][0]:SO[name][1]]

        ident = const("ident")
        headsum = const("headsum")
        ones = const("ones")
        chunk_keep = const("chunk")
        tri = const("tri")
        dist = const("dist")
        w_small = small("w_small").rearrange("p (k c) -> p k c", k=KT)
        conv_p = small("conv").rearrange("p (f c) -> p f c", f=FT)
        cmp_w2 = small("cmp_w2")
        cmp_pos = small("cmp_pos").rearrange("p (w l) -> p w l", w=2)

        oaT = carve(PAIRS, S)
        gaT = carve(KT, S)
        gbT = carve(KT, S)
        mT = carve(KT, S)
        first_top = top[0]
        aux = carve(PAIRS, AUX)
        ast = carve(2, AUX)
        half = carve(2, 2)
        lz = carve(3, S + 1)
        lora = carve(3, S)
        zs = carve(3, S + 1)
        dz = carve(3, S)
        r_f, k_f = carve(S), carve(S)
        v_pad = carve(CH + S)
        th_w, th_a = carve(S), carve(S)
        g_f, bonus = carve(2, S), q_st
        ln_st = carve(2)
        ld, cum, cum1 = carve(S), carve(S), carve(S)
        e1, e2, e3 = carve(S), carve(S), carve(S)
        kk, kk2, km, rk, nrm = carve(S), carve(S), carve(S), carve(S), carve(S)
        BK = carve(NC, 2, CH)
        AR = carve(NC, 2, CH)
        RH = carve(NC, 2, CH)
        LR = carve(NC, 2, CH)
        GR = carve(NC, 2, CH)
        UV = carve(NC, 2, CH)
        SV = carve(NC, 2, CH)
        BKT = carve(NC, 2, CH)
        Rs = carve(2, CH)
        Sw = carve(2, CH)
        Wc = carve(NC, 2)
        P0 = carve(4, P)
        Pp = [carve(4, P), carve(4, P)]
        Qp = [carve(4, P), carve(4, P)]
        Zp = [carve(4, P), carve(4, P)]
        y_f, yq = pT[:, 0, 0:S], pT[:, 1, 0:S]
        vroot, vrec = sc[:, 0, 0:S], sc[:, 1, 0:S]
        top[0] = first_top
        qT = carve(H, S)
        kcT, vcT, ksT, kwT = (carve(GROUPS, S) for _ in range(4))
        v_sw = carve(NB, 512)
        blk = [carve(16, GROUPS * N_CMP), carve(16, GROUPS * N_CMP)]
        hid = [carve(GROUPS * N_CMP) for _ in range(2)]
        ga_, gb_ = carve(GROUPS * N_CMP), carve(GROUPS * N_CMP)
        xg = carve(2, GROUPS * N_CMP)
        kcmp = carve(GROUPS * N_CMP)
        Vblk = carve(GROUPS, 4 * HD)
        cs = carve(8, N_CMP)
        cp_ = carve(8, 32)
        cpT = carve(NB, P)
        cst8 = carve(4, 8)
        top[0] = 0
        actT = carve(FT, S)
        uz = [carve(2, S + 2), carve(2, S + 2)]
        uc = [carve(2, S), carve(2, S)]
        ut = [carve(S), carve(S)]
        yt = carve(NB, D)
        top[0] = 0
        qa, ka, qb = carve(8, S), carve(8, S), carve(8, S)
        kb = carve(2, S)
        va = carve(NB, 512)
        vb = carve(NB, P)
        swb = carve(8, S)
        sbt = [[carve(KEYS) for _ in range(4)] for _ in range(2)]
        top[0] = 0
        qm, kmT = carve(H, S), carve(H, S)
        vm = carve(NB, D)
        cq, ckv, kr = carve(3, S), carve(2, S), carve(S)
        csq = carve(5, S)
        rstd_f = carve(2, S)
        posf, ang, rope_t, rope_q, rt = carve(S), carve(S), carve(S), carve(S), carve(2, S)
        pos_n = carve(S).bitcast(I32)

        slot_full = [sem(f"slot_full{i}") for i in range(RING)]
        unit_done = sem("unit_done")
        params_in = sem("params_in")
        row_in = sem("row_in")
        row_free = sem("row_free")
        phase = sem("phase")
        out_done = sem("out_done")
        phases = {}

        def phase_end(e):
            phases[id(e)] = phases.get(id(e), 0) + 1
            e.drain().then_inc(phase, 1)
            e.wait_ge(phase, 4 * phases[id(e)])

        def arrived(e, u, i=0, step=RING):
            assert step == RING
            e.wait_ge(slot_full[u % RING], 16 * (u // RING + 1) + 16 * i)

        norms = ["mix", "ffn0", "attn1", "ffn1", "attn2", "ffn2"]
        sq_ready = sem("sq_ready")
        root_ready = sem("root_ready")
        xn_ready = sem("xn_ready")
        tr_ready = sem("tr_ready")
        tr_free = sem("tr_free")

        n_norm = {}
        lora_mm, lora_free, staged, pair_done = map(sem, ("lora_mm", "lora_free", "staged", "pair_done"))
        lora_up, lora_out, kk2_ready, knorm = map(sem, ("lora_up", "lora_out", "kk2_ready", "knorm"))
        zs_ready, mixed, cum_ready, exp_ready = map(sem, ("zs_ready", "mixed", "cum_ready", "exp_ready"))
        nrm_ready, bkar_ready, gram, p0_ready = map(sem, ("nrm_ready", "bkar_ready", "gram", "p0_ready"))
        shift_ready = sem("shift_ready")
        q0_mm, q0_ready = sem("q0_mm"), sem("q0_ready")
        pow_mm, pq_ready, z_mm, z_ready = map(sem, ("pow_mm", "pq_ready", "z_mm", "z_ready"))
        r_mm, r_ready, u_mm, u_ready = map(sem, ("r_mm", "r_ready", "u_mm", "u_ready"))
        ds_mm, state_ready = sem("ds_mm"), sem("state_ready")
        y_mm, y_ready, mean_mm, yq_ready, var_mm = map(sem, ("y_mm", "y_ready", "mean_mm", "yq_ready", "var_mm"))
        rstd_root, rwkv_tail = sem("rstd_root"), sem("rwkv_tail")
        half_ready, bonus_ready, gate_out, vrec_ready, ln_staged, y_norm = map(
            sem, ("half_ready", "bonus_ready", "gate_out", "vrec_ready", "ln_staged", "y_norm"))
        aux_in, eps_ready, gates_tanh, lora_mix, lora_tanh, lora_ready = map(
            sem, ("aux_in", "eps_ready", "gates_tanh", "lora_mix", "lora_tanh", "lora_ready"))

        ev_lo, ev_hi, blk_ready, hid_mm, gelu_in, gelu_arg, gelu_tanh, hid_ready, kv_mm, kv_out, zeroed = map(sem, (
            "ev_lo", "ev_hi", "blk_ready", "hid_mm", "gelu_in", "gelu_arg", "gelu_tanh", "hid_ready", "kv_mm",
            "kv_out", "zeroed"))
        c_mm, c_arg, c_exp, c_tr, c_pT, c_pv, c_out = map(sem, (
            "c_mm", "c_arg", "c_exp", "c_tr", "c_pT", "c_pv", "c_out"))
        q_staged, b_staged, s_mm, pre_ready, max_ready, p_ready, t_mm, pt_ready, o_mm = map(sem, (
            "q_staged", "b_staged", "s_mm", "pre_ready", "max_ready", "p_ready", "t_mm", "pt_ready", "o_mm"))
        ga_ready, gb_done, gb_ready, m_ready, sq2_ready, sum_ready, root2_ready, post_done = map(sem, (
            "ga_ready", "gb_done", "gb_ready", "m_ready", "sq2_ready", "sum_ready", "root2_ready", "post_done"))
        ff_copied, ff_conv, ff_tanh, ff_free, ff_act = map(sem, (
            "ff_copied", "ff_conv", "ff_tanh", "ff_free", "ff_act"))
        e_lo, e_hi, v_out = map(sem, ("e_lo", "e_hi", "v_out"))
        m_ev, m_sq, m_sum, m_root, m_norm, rope_ready, q_lo, q_hi, kr_ready, k_lo, k_hi, rope_in = map(sem, (
            "m_ev", "m_sq", "m_sum", "m_root", "m_norm", "rope_ready", "q_lo", "q_hi", "kr_ready", "k_lo", "k_hi",
            "rope_in"))
        apart = sem("apart")
        swb_in, rope_pos, final_ready = map(sem, ("swb_in", "rope_pos", "final_ready"))
        HEAD0 = 2
        NSA0 = HEAD0
        SB0 = NSA0 + 2 * H
        SW0 = SB0 + SB_HEADS
        MLA0 = SW0 + SW_HEADS

        block = ctx.enter_context(nc.Block())

        @block.sync
        def _(sp):
            sp.dma_start(x[:], x_d).then_inc(params_in, 16)
            sp.dma_start(cst[:], const_d).then_inc(params_in, 16)
            sp.dma_start(sml[:], small_d).then_inc(params_in, 16)
            for u in range(RING):
                sp.dma_start(ring[:, u, :], weights[u]).then_inc(slot_full[u], 16)
            groups = N_UNITS // RING
            with sp.Fori(1, groups) as i:
                for j in range(RING):
                    sp.wait_ge(unit_done, i * RING + (j - RING + 1))
                    sp.dma_start(ring[:, j, :], weights[i * RING + j]).then_inc(slot_full[j], 16)
            for u in range(groups * RING, N_UNITS):
                sp.wait_ge(unit_done, u - RING + 1)
                sp.dma_start(ring[:, u % RING, :], weights[u]).then_inc(slot_full[u % RING], 16)

        @block.tensor
        def _(pe):
            def f_tile(dst, u, tile, rhs, keys=KT, width=P, inc=None, i=0):
                w = ring[:, u % RING, :].rearrange("p (k c) -> p k c", k=KT)
                for k in range(keys):
                    m = pe.matmul(dst, w[:, k, tile * P:tile * P + width], rhs[:, k, :],
                                  start=k == 0, stop=k == keys - 1)
                if inc is not None:
                    m.then_inc(inc, 1)

            def f_unit(bank, u, rhs, i=0):
                arrived(pe, u, i)
                f_tile(bank[:, 0:S], u, 0, rhs)
                f_tile(bank[:, S:2 * S], u, 1, rhs, inc=unit_done)

            def transposes(src):
                pe.wait_ge(xn_ready, n_norm.setdefault("pe", 0) + 1)
                n_norm["pe"] += 1
                for k in range(KT):
                    for b in range(NB):
                        m = pe.transpose(ps[4 + k // 2][:, (k % 2) * S + b * P:(k % 2) * S + b * P + P],
                                         src[:, b, k * P:(k + 1) * P], ident)
                    if k % 2:
                        m.then_inc(tr_ready, 1)

            def t_rows(u0, lhs, n_units, i=0):
                for n in range(n_units):
                    arrived(pe, u0 + n)
                    w = ring[:, (u0 + n) % RING, :].rearrange("p (k c) -> p k c", k=2)
                    for k in range(2):
                        for b in range(NB):
                            for hf in range(2):
                                m = pe.matmul(ps[4 + 2 * b + hf][:], lhs[:, 2 * n + k, b * P:(b + 1) * P],
                                              w[:, k, hf * 512:(hf + 1) * 512],
                                              start=n == 0 and k == 0, stop=n == n_units - 1 and k == 1)
                    m.then_inc(unit_done, 1)

            def attention(insts, n0):
                N = len(insts)
                for s in range(N + 2):
                    if s < N:
                        rows, keys, _ = insts[s]
                        bank = ps[s % 2]
                        pe.wait_ge(q_staged, n0 + s + 1)
                        pe.sem_inc(apart, 1)
                        q = q_st[0:rows, s % 2, :]
                        pe.matmul(bank[:, 0:P], q[:, 0:P], keys(0, P), start=True, stop=True)
                        pe.matmul(bank[:, P:KEYS], q[:, P:S], keys(0, S), start=True, stop=True).then_inc(s_mm, 1)
                    if 1 <= s <= N:
                        t = s - 1
                        pe.wait_ge(p_ready, n0 + t + 1)
                        for kt in range(3):
                            m = pe.transpose(ps[2 + t % 2][:, kt * P:(kt + 1) * P],
                                             sc[:, t % 2, kt * P:(kt + 1) * P], ident)
                        m.then_inc(t_mm, 1)
                    if s >= 2:
                        t = s - 2
                        values = insts[t][2]
                        o = ps[4 + t % 2]
                        pe.wait_ge(pt_ready, n0 + t + 1)
                        pe.matmul(o[:, 0:HD], pT[:, t % 2, 0:P], values(0), start=True, stop=True)
                        pe.matmul(o[:, HD:2 * HD], pT[:, t % 2, P:2 * P], values(0), start=True, stop=False)
                        pe.matmul(o[:, HD:2 * HD], pT[:, t % 2, 2 * P:3 * P], values(1), start=False,
                                  stop=True).then_inc(o_mm, 1)

            def ffn_up(u0, n_ffn):
                def unit(j, i):
                    pe.wait_ge(ff_act if n_ffn else ff_free, 2 + n_ffn * FT + 4 * i + j - 1)
                    f_unit(ps[j % 2], u0 + j, hT, i)

                with pe.Fori(0, FT // 4) as i:
                    for j in range(4):
                        unit(j, i)
                for j in range(FT % 4):
                    unit(j, FT // 4)

            pe.wait_ge(params_in, 48)
            pe.drain().then_inc(s_mm, HEAD0)
            pe.drain().then_inc(t_mm, HEAD0)
            pe.drain().then_inc(o_mm, HEAD0)
            transposes(xn)
            phase_end(pe)

            f_unit(ps[0], U["lora"], hT)
            for k in range(KT):
                pe.matmul(ps[1][0:32, 0:S], w_small[:, k, 0:32], hT[:, k, :], start=k == 0, stop=k == KT - 1)
            for b in range(NB):
                for k in range(KT):
                    m = pe.matmul(ps[2][:, b * 48:b * 48 + 48], hT[:, k, b * P:(b + 1) * P],
                                  w_small[:, k, 32:80], start=k == 0, stop=k == KT - 1)
            m.then_inc(lora_mm, 1)

            def rwkv_dense(i, j, tiles):
                for tile in tiles:
                    u = U["rwkv"] + 2 * j + tile // 2
                    if tile % 2 == 0:
                        arrived(pe, u, i)
                    w = ring[:, u % RING, :].rearrange("p (k c) -> p k c", k=KT)
                    dst = ps[tile // 2][:, (tile % 2) * S:(tile % 2 + 1) * S]
                    for k in range(KT):
                        m = pe.matmul(dst, w[:, k, (tile % 2) * P:(tile % 2 + 1) * P], hT[:, k, :],
                                      start=k == 0, stop=k == KT - 1)
                        if k == KT - 1 and tile % 2:
                            m.then_inc(unit_done, 1)
                        if k % 2:
                            yield

            def low_rank(m, j):
                pe.wait_ge(staged, m + 1)
                st = ast[:, j, :]
                pe.matmul(ps[2][:, 0:S], st[0:64, 0:128], lora[0:64, 0, :], start=True, stop=True)
                pe.matmul(ps[3][:, S:2 * S], st[64:128, 0:128], lora[64:128, 0, :], start=True, stop=True)
                pe.matmul(ps[2][:, S:2 * S], st[:, 128:256], lora[:, 1, :], start=True, stop=False)
                pe.matmul(ps[2][:, S:2 * S], st[0:32, 256:384], lora[0:32, 2, :], start=False,
                          stop=True).then_inc(lora_up, 1)

            def key_norm(m):
                pe.wait_ge(kk2_ready, m + 1)
                pe.wait_ge(lora_out, m + 1)
                pe.matmul(ps[3][:, 0:S], headsum, kk2, start=True, stop=True).then_inc(knorm, 1)

            def grams(m, tail=None):
                pe.wait_ge(bkar_ready, m + 1)
                for hh in range(2):
                    for c in range(NC):
                        pe.matmul(ps[4 + hh][:, c * P:(c + 1) * P],
                                  BK[hh * HD:(hh + 1) * HD, c, :, :].rearrange("p a b -> p (a b)"),
                                  AR[hh * HD:(hh + 1) * HD, c, :, :].rearrange("p a b -> p (a b)"),
                                  start=True, stop=True)
                if tail is not None:
                    tail()
                for c in range(NC):
                    pe.transpose(ps[6][:, c * P:(c + 1) * P], v_pad[:, c * CH:c * CH + P], ident)
                for c in range(NC):
                    pe.transpose(ps[7][:, c * P:(c + 1) * P],
                                 BK[:, c, :, :].rearrange("p a b -> p (a b)"), ident)
                pe.wait_ge(gate_out, m + 1)
                pe.matmul(ps[2][:, 0:S], headsum, rk, start=True, stop=True).then_inc(gram, 1)

            def mean_of(n):
                pe.wait_ge(y_ready, n + 1)
                pe.matmul(ps[3][:, 0:S], headsum, y_f, start=True, stop=True).then_inc(mean_mm, 1)

            def variance_of(n):
                pe.wait_ge(yq_ready, n + 1)
                pe.matmul(ps[3][:, S:2 * S], headsum, yq, start=True, stop=True).then_inc(var_mm, 1)

            def rwkv_pair(n, j, dense=None):
                last = dense is None and n == PAIRS - 1
                pe.wait_ge(p0_ready, n + 1)
                for g in range(4):
                    m = pe.transpose(ps[4][:, g * P:(g + 1) * P], P0[:, g, :], ident)
                m.then_inc(q0_mm, 1)
                for lvl in range(6):
                    if lvl == 0:
                        pe.wait_ge(q0_ready, n + 1)
                        p_, q_, z_ = P0, Qp[1], Zp[1]
                    else:
                        pe.wait_ge(pq_ready, 10 * n + 2 * lvl)
                        p_, q_, z_ = Pp[(lvl + 1) % 2], Qp[(lvl + 1) % 2], Zp[lvl % 2]
                    if lvl < 5:
                        for g in range(4):
                            m = pe.matmul(ps[4][:, g * P:(g + 1) * P], q_[:, g, :], p_[:, g, :], start=True, stop=True)
                        m.then_inc(pow_mm, 1)
                        for g in range(4):
                            m = pe.matmul(ps[5][:, g * P:(g + 1) * P], p_[:, g, :], q_[:, g, :], start=True, stop=True)
                        m.then_inc(pow_mm, 1)
                    if lvl > 1:
                        pe.wait_ge(z_ready, 5 * n + lvl - 1)
                    if lvl > 0:
                        for g in range(4):
                            m = pe.matmul(ps[6][:, g * P:(g + 1) * P], q_[:, g, :], z_[:, g, :], start=True, stop=True)
                        m.then_inc(z_mm, 1)
                    if not last and lvl == 0:
                        pe.wait_ge(bonus_ready, n + 1)
                        low_rank(n + 1, 1 - j)
                    if not last and lvl == 2:
                        key_norm(n + 1)
                fill = iter(())
                if dense is not None:
                    pe.wait_ge(zs_ready, n + 2)
                    fill = rwkv_dense(*dense, (0, 1, 2))
                for _ in range(3):
                    next(fill, None)
                pe.wait_ge(z_ready, 5 * n + 5)
                Z = Zp[0]
                for c in range(NC):
                    lo = (c % 2) * CH
                    if c:
                        pe.wait_ge(state_ready, 3 * n + c)
                    for hh in range(2):
                        m = pe.matmul(ps[7][lo:lo + CH, hh * HD:(hh + 1) * HD], LR[:, c, hh, :], SV[:, c, hh, :],
                                      start=True, stop=True)
                    m.then_inc(r_mm, 1)
                    next(fill, None)
                    pe.wait_ge(r_ready, 4 * n + c + 1)
                    pe.sem_inc(apart, 1)
                    for hh in range(2):
                        m = pe.matmul(ps[4][0:CH, hh * HD:(hh + 1) * HD],
                                      Z[lo:lo + CH, 2 * hh + c // 2, lo:lo + CH], Rs[lo:lo + CH, hh, :],
                                      start=True, stop=True)
                    m.then_inc(u_mm, 1)
                    next(fill, None)
                    pe.wait_ge(u_ready, 4 * n + c + 1)
                    if c < NC - 1:
                        for hh in range(2):
                            m = pe.matmul(ps[5][0:HD, hh * HD:(hh + 1) * HD], BKT[:, c, hh, :], UV[:, c, hh, :],
                                          start=True, stop=True)
                        m.then_inc(ds_mm, 1)
                    for hh in range(2):
                        dst = ps[6][hh * HD:(hh + 1) * HD, c * CH:(c + 1) * CH]
                        pe.matmul(dst, UV[:, c, hh, :], GR[:, c, hh, :], start=True, stop=False)
                        m = pe.matmul(dst, SV[0:HD, c, hh, :], RH[0:HD, c, hh, :], start=False, stop=True)
                    if c < NC - 1:
                        next(fill, None)
                m.then_inc(y_mm, 1)
                for _ in fill:
                    pass
                mean_of(n)
                if last:
                    variance_of(n)
                    return
                grams(n + 1, tail=lambda: variance_of(n))
                if dense is not None:
                    for _ in rwkv_dense(*dense, (3,)):
                        pass

            pe.wait_ge(lora_free, 2)
            pe.wait_ge(lora_ready, 1)
            for _ in rwkv_dense(0, 0, range(4)):
                pass
            low_rank(0, 0)
            key_norm(0)
            pe.wait_ge(zs_ready, 1)
            for _ in rwkv_dense(0, 1, (0, 1, 2)):
                pass
            grams(0)
            for _ in rwkv_dense(0, 1, (3,)):
                pass
            rwkv_pair(0, 0, (1, 0))
            with pe.Fori(0, PAIRS // 2 - 1) as i:
                rwkv_pair(2 * i + 1, 1, (i + 1, 1))
                rwkv_pair(2 * i + 2, 0, (i + 2, 0))
            rwkv_pair(PAIRS - 1, 1)
            phase_end(pe)

            for m in range(2, 8):
                pe.wait_ge(ev_lo, m - 1)
                pe.wait_ge(ev_hi, m - 1)
                f_unit(ps[m % 2], U["nsa_q"] + m, hT)
            for n in range(2):
                u = U["nsa_v"] + n
                arrived(pe, u)
                w = ring[:, u % RING, :].rearrange("p (k c) -> p k c", k=4)
                for k in range(4):
                    for b in range(NB):
                        m = pe.matmul(ps[2 + b][:], hT[:, 4 * n + k, b * P:(b + 1) * P], w[:, k, :],
                                      start=n == 0 and k == 0, stop=n == 1 and k == 3)
                m.then_inc(unit_done, 1)
            for w_ in range(2):
                pe.wait_ge(blk_ready, w_ + 1)
                u = U["cmp"] + w_
                arrived(pe, u)
                w = ring[:, u % RING, :].rearrange("p (k c) -> p k c", k=16)
                for k in range(16):
                    m = pe.matmul(ps[4][:, 60 * w_:60 * w_ + 60], w[:, k, :], blk[w_][:, k, :], start=k == 0, stop=k == 15)
                m.then_inc(unit_done, 1)
            pe.wait_ge(hid_ready, 1)
            pe.matmul(ps[5][0:HD, 0:60], cmp_w2[:, 0:HD], xg[:, 0, :], start=True, stop=True)
            for g in range(GROUPS):
                m = pe.matmul(ps[6][0:N_CMP, g * HD:(g + 1) * HD], xg[:, 1, g * N_CMP:(g + 1) * N_CMP],
                              cmp_w2[:, HD:P], start=True, stop=True)
            m.then_inc(kv_mm, 1)
            phase_end(pe)

            for g in range(GROUPS):
                if g >= 1:
                    pe.wait_ge(c_arg, g)
                for b in range(NB):
                    for hh in range(HPG):
                        c = (b * HPG + hh) * N_CMP
                        m = pe.matmul(ps[0][:, c:c + N_CMP], qT[0:HD, HPG * g + hh, b * P:(b + 1) * P],
                                      kcmp[0:HD, g * N_CMP:(g + 1) * N_CMP], start=True, stop=True)
                m.then_inc(c_mm, 1)
                pe.wait_ge(c_exp, g + 1)
                for b in range(NB):
                    m = pe.transpose(ps[1][:, b * P:(b + 1) * P],
                                     cp_[:, b * HPG:(b + 1) * HPG, :].rearrange("p h n -> p (h n)"), ident)
                m.then_inc(c_tr, 1)
                pe.wait_ge(c_pT, g + 1)
                for b in range(NB):
                    m = pe.matmul(ps[2][:, b * S:(b + 1) * S], cpT[:, b, :], Vblk[:, g, :], start=True, stop=True)
                m.then_inc(c_pv, 1)
            phase_end(pe)

            with pe.Fori(0, GROUPS) as g:
                attention([(HD, (lambda lo, hi, k=(ksT, kwT)[br]: k[0:HD, g, lo:hi]),
                            (lambda kt, br=br: v_sw.rearrange("p b (w g d) -> p b w g d", w=2, g=GROUPS)[:, kt, br, g, :]))
                           for hh in range(HPG) for br in range(2)], NSA0 + 8 * g)
            transposes(xn)
            phase_end(pe)

            for m in range(4):
                if m >= 2:
                    pe.wait_ge(gb_done, m - 1)
                f_unit(ps[m % 2], U["gate_b"] + m, hT)
            for m in range(KT):
                pe.wait_ge(gb_done, min(4, m + 3))
                if m >= 2:
                    pe.wait_ge(m_ready, m - 1)
                u = U["branch"] + m
                arrived(pe, u)
                f_tile(ps[m % 2][:, 0:S], u, 0, oaT)
                f_tile(ps[m % 2][:, S:2 * S], u, 1, oT, inc=unit_done)
            pe.wait_ge(m_ready, KT)
            t_rows(U["w_out"], mT, 4)
            phase_end(pe)
            transposes(xn)
            phase_end(pe)
            ffn_up(U["up0"], 0)
            pe.wait_ge(ff_act, 2 + FT)
            t_rows(U["down0"], actT, FT // 2)
            phase_end(pe)
            transposes(xn)
            phase_end(pe)

            for m in range(7):
                if m >= 2:
                    pe.wait_ge(e_lo, m - 1)
                    pe.wait_ge(e_hi, m - 1)
                u = U["even_f"] + m
                arrived(pe, u)
                f_tile(ps[m % 2][:, 0:S], u, 0, hT)
                if m < 6:
                    f_tile(ps[m % 2][:, S:2 * S], u, 1, hT, inc=unit_done)
            w = ring[:, u % RING, :].rearrange("p (k c) -> p k c", k=KT)
            for b in range(NB):
                for k in range(KT):
                    m = pe.matmul(ps[2][:, b * P:(b + 1) * P], hT[:, k, b * P:(b + 1) * P], w[:, k, P:2 * P],
                                  start=k == 0, stop=k == KT - 1)
            m.then_inc(unit_done, 1)
            for n in range(2):
                u = U["even_v"] + n
                arrived(pe, u)
                w = ring[:, u % RING, :].rearrange("p (k c) -> p k c", k=4)
                for k in range(4):
                    for b in range(NB):
                        m = pe.matmul(ps[4 + b][:], hT[:, 4 * n + k, b * P:(b + 1) * P], w[:, k, :],
                                      start=n == 0 and k == 0, stop=n == 1 and k == 3)
                m.then_inc(unit_done, 1)
            phase_end(pe)
            with pe.Fori(0, 2) as i:
                attention([(HD, (lambda lo, hi, h=h: ka[0:HD, 4 * i + h, lo:hi]),
                            (lambda kt, h=h: va.rearrange("p b (h d) -> p b h d", d=HD)[:, kt, 4 * i + h, :]))
                           for h in range(4)], SB0 + 4 * i)
            phase_end(pe)
            with pe.Fori(0, 2) as i:
                attention([(HD, (lambda lo, hi: kb[0:HD, i, lo:hi]),
                            (lambda kt: vb.rearrange("p b (h d) -> p b h d", d=HD)[:, kt, i, :]))
                           for h in range(4)], SW0 + 4 * i)
            transposes(xn)
            phase_end(pe)
            t_rows(U["even_out"], oT, 4)
            phase_end(pe)
            transposes(xn)
            phase_end(pe)
            ffn_up(U["up1"], 1)
            pe.wait_ge(ff_act, 2 + 2 * FT)
            t_rows(U["down1"], actT, FT // 2)
            phase_end(pe)
            transposes(xn)
            phase_end(pe)

            for m in range(3):
                f_unit(ps[m], U["mla_down"] + m, hT)
            pe.wait_ge(m_sq, 1)
            for k in range(3):
                pe.matmul(ps[4][:, 0:S], ones, csq[:, k, :], start=k == 0, stop=k == 2)
            for k in range(2):
                m = pe.matmul(ps[4][:, S:2 * S], ones, csq[:, 3 + k, :], start=k == 0, stop=k == 1)
            m.then_inc(m_sum, 1)
            pe.wait_ge(m_norm, 1)
            for h in range(H):
                if h >= 2:
                    pe.wait_ge(q_lo, h - 1)
                    pe.wait_ge(q_hi, h - 1)
                u = U["mla_uq"] + h // 4
                arrived(pe, u)
                w = ring[:, u % RING, 0:1536].rearrange("p (k c) -> p k c", k=3)
                for k in range(3):
                    m = pe.matmul(ps[6 + h % 2][:, 0:S], w[:, k, (h % 4) * P:(h % 4 + 1) * P], cq[:, k, :],
                                  start=k == 0, stop=k == 2)
                if h % 4 == 3:
                    m.then_inc(unit_done, 1)
                    pe.drain().then_inc(m_ev, 1)
                else:
                    m.then_inc(m_ev, 1)
            u = U["mla_uk"]
            arrived(pe, u)
            w = ring[:, u % RING, :].rearrange("p (k c) -> p k c", k=2)
            for t in range(8):
                if t >= 2:
                    pe.wait_ge(k_lo, t - 1)
                    pe.wait_ge(k_hi, t - 1)
                for k in range(2):
                    m = pe.matmul(ps[t % 2][:, 0:S], w[:, k, t * P:(t + 1) * P], ckv[:, k, :], start=k == 0, stop=k == 1)
                if t == 7:
                    m.then_inc(unit_done, 1)
                    pe.drain().then_inc(m_ev, 1)
                else:
                    m.then_inc(m_ev, 1)
            u = U["mla_uv"]
            arrived(pe, u)
            w = ring[:, u % RING, :].rearrange("p (k c) -> p k c", k=2)
            for b in range(NB):
                for hf in range(2):
                    for k in range(2):
                        m = pe.matmul(ps[2 + 2 * b + hf][:], ckv[:, k, b * P:(b + 1) * P],
                                      w[:, k, hf * 512:(hf + 1) * 512], start=k == 0, stop=k == 1)
            m.then_inc(unit_done, 1)
            phase_end(pe)
            with pe.Fori(0, 4) as i:
                attention([(HD + ROPE, (lambda lo, hi, h=h: kmT[0:HD + ROPE, 4 * i + h, lo:hi]),
                            (lambda kt, h=h: vm.rearrange("p b (h d) -> p b h d", d=HD)[:, kt, 4 * i + h, :]))
                           for h in range(4)], MLA0 + 4 * i)
            transposes(xn)
            phase_end(pe)
            t_rows(U["mla_out"], oT, 4)
            phase_end(pe)
            transposes(xn)
            phase_end(pe)
            ffn_up(U["up2"], 2)
            pe.wait_ge(ff_act, 2 + 3 * FT)
            t_rows(U["down2"], actT, FT // 2)
            phase_end(pe)

        @block.scalar
        def _(act):
            def square_rows(src):
                act.drain()
                for b in range(NB):
                    m = act.activation(xn[:, b, :], src[:, b, :], ACT.Square, accum_out=stat[:, b:b + 1])
                m.then_inc(sq_ready, 1)
                act.drain()
                act.activation(stat[:, 2:4], stat[:, 0:2], ACT.Sqrt, bias=stat[:, 7:8],
                               scale=1.0 / D).then_inc(root_ready, 1)

            def evacuate_even(dst, gain):
                n = n_norm.setdefault("act", 0)
                n_norm["act"] += 1
                for q in (0, 2):
                    act.wait_ge(tr_ready, 4 * n + q + 1)
                    for k in (2 * q, 2 * q + 1):
                        src = ps[4 + q][:, (k % 2) * S:(k % 2 + 1) * S]
                        if gain is None:
                            act.activation(dst[:, k, :], src, ACT.Copy)
                        else:
                            act.activation(dst[:, k, :], src, ACT.Copy, scale=gain[:, k:k + 1])

            def exponentials(N, n0):
                for s in range(N):
                    act.wait_ge(max_ready, n0 + s + 1)
                    act.activation(sc[:, s % 2, 0:P], sc[:, s % 2, 0:P], ACT.Exp, bias=mx[:, s % 2, 2:3],
                                   accum_out=mx[:, s % 2, 4:5])
                    act.activation(sc[:, s % 2, P:KEYS], sc[:, s % 2, P:KEYS], ACT.Exp, bias=mx[:, s % 2, 3:4],
                                   accum_out=mx[:, s % 2, 5:6]).then_inc(p_ready, 1)

            def square_post(n_post):
                for q in range(4):
                    m = act.activation(xn[:, q // 2, (q % 2) * 512:(q % 2 + 1) * 512], ps[4 + q][:], ACT.Square,
                                       accum_out=mx[:, 0, q:q + 1])
                m.then_inc(sq2_ready, 1)
                act.wait_ge(sum_ready, n_post + 1)
                act.activation(stat[:, 2:4], stat[:, 0:2], ACT.Sqrt, bias=stat[:, 7:8],
                               scale=1.0 / D).then_inc(root2_ready, 1)

            def ffn_conv():
                def body(js, i):
                    for k in range(len(js) + 1):
                        if k < len(js):
                            j = js[k]
                            m = 4 * i + j
                            act.wait_ge(unit_done, U["up0"] + 4 * i + j + 1)
                            act.wait_ge(ff_act, 2 + 4 * i + j - 1)
                            act.activation(uz[j % 2][:, :, 2:S + 2], ps[j % 2][:].rearrange("p (a t) -> p a t", a=2),
                                           ACT.Copy).then_inc(ff_free, 1)
                        if k > 0:
                            j = js[k - 1]
                            act.wait_ge(ff_conv, 4 * i + j + 1)
                            act.activation(ut[j % 2], uc[j % 2][:, 0, :], ACT.Tanh, scale=0.5).then_inc(ff_tanh, 1)

                with act.Fori(0, FT // 4) as i:
                    body(range(4), i)
                body(range(FT % 4), FT // 4)

            def ffn_tanh(u0, n_ffn):
                def body(js, i):
                    for j in js:
                        act.wait_ge(unit_done, u0 + 4 * i + j + 1)
                        act.wait_ge(ff_act, 2 + n_ffn * FT + 4 * i + j - 1)
                        act.activation(ut[j % 2], ps[j % 2][:, 0:S], ACT.Tanh, scale=0.5).then_inc(ff_tanh, 1)

                with act.Fori(0, FT // 4) as i:
                    body(range(4), i)
                body(range(FT % 4), FT // 4)

            act.wait_ge(params_in, 48)
            act.wait_ge(eps_ready, 1)
            act.drain().then_inc(p_ready, HEAD0)
            act.drain().then_inc(ff_free, 2)
            square_rows(x)
            evacuate_even(hT, small("g_mix"))
            phase_end(act)

            act.wait_ge(unit_done, U["lora"] + 1)
            act.activation(lz[:, 0:2, 1:S + 1], ps[0][:].rearrange("p (a t) -> p a t", a=2),
                           ACT.Copy).then_inc(lora_free, 1)
            act.wait_ge(lora_mm, 1)
            act.activation(lz[0:32, 2, 1:S + 1], ps[1][0:32, 0:S], ACT.Copy).then_inc(lora_free, 1)
            act.activation(gates.rearrange("p b c -> p (b c)"), ps[2][:, 0:96], ACT.Tanh,
                           scale=0.5).then_inc(gates_tanh, 1)
            act.wait_ge(lora_mix, 1)
            act.activation(lora[0:64, 0, :], lora[0:64, 0, :], ACT.Tanh)
            act.activation(lora[:, 1:3, :], lora[:, 1:3, :], ACT.Tanh, scale=0.5).then_inc(lora_tanh, 1)
            act.wait_ge(lora_ready, 1)

            def take_dense(m):
                act.wait_ge(mixed, m + 1)
                act.wait_ge(unit_done, U["rwkv"] + 2 * m + 1)
                act.activation(zs[:, 0:2, 1:S + 1], ps[0][:].rearrange("p (a t) -> p a t", a=2), ACT.Copy)
                act.wait_ge(unit_done, U["rwkv"] + 2 * m + 2)
                act.activation(zs[:, 2, 1:S + 1], ps[1][:, 0:S], ACT.Copy)
                act.activation(gaT[:, m, :], ps[1][:, S:2 * S], ACT.Tanh, scale=0.5).then_inc(zs_ready, 1)

            def low_rank(m, j):
                act.wait_ge(half_ready, m + 1)
                act.wait_ge(lora_up, m + 1)
                act.activation(th_w, ps[2][:, 0:S], ACT.Tanh, scale=0.5, bias=half[:, j, 0:1])
                act.activation(th_a, ps[3][:, S:2 * S], ACT.Tanh, scale=0.5, bias=half[:, j, 1:2]).then_inc(lora_out, 1)

            def output_gate(m, j):
                act.wait_ge(pair_done, m)
                act.activation(g_f[:, j, :], ps[2][:, S:2 * S], ACT.Copy).then_inc(gate_out, 1)

            def decays(m):
                act.wait_ge(cum_ready, m + 1)
                act.activation(e1, cum, ACT.Exp)
                act.activation(e2, cum, ACT.Exp, scale=-1.0)
                act.activation(e3, cum1, ACT.Exp).then_inc(exp_ready, 1)

            def key_norm(m):
                act.wait_ge(knorm, m + 1)
                act.activation(nrm, ps[3][:, 0:S], ACT.Sqrt).then_inc(nrm_ready, 1)

            def variance_root(n):
                act.wait_ge(var_mm, n + 1)
                act.activation(vroot, ps[3][:, S:2 * S], ACT.Sqrt, bias=stat[:, 6:7],
                               scale=1.0 / HD).then_inc(rstd_root, 1)

            def shift_rows(m, before=None):
                act.wait_ge(bkar_ready, m + 1)
                for hh in range(2):
                    rows = slice(hh * HD, (hh + 1) * HD)
                    act.activation(LR[0:HD, :, hh, :], AR[rows, :, 0, :], ACT.Copy)
                    act.activation(RH[0:HD, :, hh, :], AR[rows, :, 1, :], ACT.Copy)
                    act.activation(Wc[0:HD, :, hh], e1[rows, CH - 1:S:CH], ACT.Copy)
                if before is not None:
                    variance_root(before)
                act.wait_ge(gram, m + 1)
                act.activation(BKT.rearrange("p c h d -> p (c h d)"), ps[7][:], ACT.Copy)
                v_tm = ps[6][CH:P, :].rearrange("p (c h d) -> p c h d", c=NC, h=2)
                act.activation(UV[CH:P, :, :, :], v_tm, ACT.Copy)
                act.activation(SV[CH:P, :, :, :], v_tm, ACT.Copy).then_inc(shift_ready, 1)

            def rwkv_pair(n, j, last=False):
                if not last:
                    take_dense(n + 1)
                act.wait_ge(q0_mm, n + 1)
                act.activation(Qp[1].rearrange("p a b -> p (a b)"), ps[4][:], ACT.Copy).then_inc(q0_ready, 1)
                for lvl in range(5):
                    act.wait_ge(pow_mm, 10 * n + 2 * lvl + 1)
                    act.activation(Pp[lvl % 2].rearrange("p a b -> p (a b)"), ps[4][:], ACT.Copy).then_inc(pq_ready, 1)
                    act.wait_ge(pow_mm, 10 * n + 2 * lvl + 2)
                    act.activation(Qp[lvl % 2].rearrange("p a b -> p (a b)"), ps[5][:],
                                   ACT.Copy).then_inc(pq_ready, 1)
                    if not last:
                        if lvl == 0:
                            low_rank(n + 1, 1 - j)
                        if lvl == 2:
                            decays(n + 1)
                        if lvl == 3:
                            key_norm(n + 1)
                        if lvl == 4:
                            output_gate(n + 1, 1 - j)
                for c in range(NC):
                    act.wait_ge(u_mm, 4 * n + c + 1)
                    act.activation(UV[0:CH, c, :, :].rearrange("p h d -> p (h d)"), ps[4][0:CH, 0:P],
                                   ACT.Copy).then_inc(u_ready, 1)
                if last:
                    variance_root(n)
                    return
                act.wait_ge(y_mm, n + 1)
                shift_rows(n + 1, before=n)

            take_dense(0)
            low_rank(0, 0)
            act.activation(g_f[:, 0, :], ps[2][:, S:2 * S], ACT.Copy).then_inc(gate_out, 1)
            decays(0)
            key_norm(0)
            shift_rows(0)
            rwkv_pair(0, 0)
            with act.Fori(0, PAIRS // 2 - 1) as i:
                rwkv_pair(2 * i + 1, 1)
                rwkv_pair(2 * i + 2, 0)
            rwkv_pair(PAIRS - 1, 1, last=True)
            phase_end(act)

            for m in range(8):
                act.wait_ge(unit_done, U["nsa_q"] + m + 1)
                src = ps[m % 2][0:HD, :].rearrange("p (a t) -> p a t", a=2)
                if m < 4:
                    act.activation(qT[0:HD, 4 * m:4 * m + 4:2, :], src, ACT.Copy, scale=SCALE).then_inc(ev_lo, 1)
                else:
                    act.activation((kcT, vcT, ksT, kwT)[m - 4][0:HD, 0:4:2, :], src, ACT.Copy).then_inc(ev_lo, 1)
            act.wait_ge(unit_done, U["nsa_v"] + 2)
            act.activation(v_sw[:, 0, :], ps[2][:], ACT.Copy)
            act.wait_ge(gelu_arg, 1)
            act.activation(xg[:], xg[:], ACT.Tanh, scale=math.sqrt(2 / math.pi)).then_inc(gelu_tanh, 1)
            phase_end(act)
            for g in range(GROUPS):
                act.wait_ge(c_arg, g + 1)
                act.activation(cp_[:, :, 0:N_CMP], cs[:], ACT.Exp).then_inc(c_exp, 1)
            phase_end(act)
            with act.Fori(0, GROUPS) as g:
                exponentials(8, NSA0 + 8 * g)
            evacuate_even(oT, None)
            phase_end(act)
            for m in range(4):
                act.wait_ge(unit_done, U["gate_b"] + m + 1)
                act.activation(gbT[:, 2 * m:2 * m + 2, :].rearrange("p a t -> p (a t)"), ps[m % 2][:], ACT.Tanh,
                               scale=0.5).then_inc(gb_done, 1)
            act.wait_ge(unit_done, U["w_out"] + 4)
            square_post(0)
            phase_end(act)
            square_rows(x)
            evacuate_even(hT, small("g_ffn"))
            phase_end(act)
            ffn_conv()
            act.wait_ge(unit_done, U["down0"] + FT // 2)
            square_post(1)
            phase_end(act)
            square_rows(x)
            evacuate_even(hT, small("g_attn2")[:, 0:KT])
            phase_end(act)
            for m in range(7):
                act.wait_ge(unit_done, U["even_f"] + m + 1)
                src = ps[m % 2][0:HD, :].rearrange("p (a t) -> p a t", a=2)
                dst = (qa, qa, ka, ka, qb, qb, kb)[m]
                if m < 6:
                    act.activation(dst[0:HD, 4 * (m % 2):4 * (m % 2) + 4:2, :], src, ACT.Copy,
                                   scale=1.0 if m in (2, 3) else SCALE).then_inc(e_lo, 1)
                else:
                    act.activation(kb[0:HD, 0, :], src[:, 0, :], ACT.Copy).then_inc(e_lo, 1)
            act.activation(vb.rearrange("p b c -> p (b c)"), ps[2][:, 0:S], ACT.Copy)
            act.wait_ge(unit_done, U["even_v"] + 2)
            act.activation(va[:, 0, :], ps[4][:], ACT.Copy)
            phase_end(act)
            with act.Fori(0, 2) as i:
                for s in range(5):
                    if s < 4:
                        t0 = sbt[s % 2][0]
                        act.wait_ge(s_mm, SB0 + 4 * i + s + 1)
                        act.wait_ge(max_ready, SB0 + 4 * i + s - 1)
                        act.activation(t0, ps[s % 2][:, 0:KEYS], ACT.Abs)
                        act.drain()
                        act.activation(t0, t0, ACT.Exp, scale=-1.0)
                        act.drain()
                        act.activation(t0, t0, ACT.Ln, bias=1.0).then_inc(pre_ready, 1)
                    if s > 0:
                        act.wait_ge(max_ready, SB0 + 4 * i + s)
                        act.activation(sc[:, (s - 1) % 2, :], sc[:, (s - 1) % 2, :], ACT.Exp).then_inc(p_ready, 1)
            phase_end(act)
            def sink_exponentials(n0):
                for s in range(4):
                    act.wait_ge(max_ready, n0 + s + 1)
                    act.activation(sc[:, s % 2, 0:P], sc[:, s % 2, 0:P], ACT.Exp, bias=mx[:, s % 2, 2:3],
                                   accum_out=mx[:, s % 2, 4:5])
                    act.activation(sc[:, s % 2, P:KEYS], sc[:, s % 2, P:KEYS], ACT.Exp, bias=mx[:, s % 2, 3:4],
                                   accum_out=mx[:, s % 2, 5:6])
                    act.activation(mx[:, s % 2, 6:8], mx[:, s % 2, 2:4], ACT.Exp,
                                   bias=sink_st[:, s % 2:s % 2 + 1]).then_inc(p_ready, 1)

            with act.Fori(0, 2) as i:
                sink_exponentials(SW0 + 4 * i)
            evacuate_even(oT, None)
            phase_end(act)
            phase_end(act)
            square_rows(x)
            evacuate_even(hT, small("g_ffn2")[:, 0:KT])
            phase_end(act)
            ffn_tanh(U["up1"], 1)
            phase_end(act)
            square_rows(x)
            evacuate_even(hT, small("g_attn2")[:, KT:2 * KT])
            phase_end(act)
            for m in range(3):
                act.wait_ge(unit_done, U["mla_down"] + m + 1)
                for t in range(2):
                    k = 2 * m + t
                    if k == 5:
                        continue
                    dst = cq[:, k, :] if k < 3 else ckv[:, k - 3, :]
                    act.activation(dst, ps[m][:, t * S:(t + 1) * S], ACT.Copy)
                    e_ = act.activation(csq[:, k, :], ps[m][:, t * S:(t + 1) * S], ACT.Square)
            e_.then_inc(m_sq, 1)
            act.wait_ge(m_sum, 1)
            act.activation(rstd_f[:, 0, :], ps[4][:, 0:S], ACT.Sqrt, bias=stat[:, 7:8], scale=1.0 / Q_RANK)
            act.activation(rstd_f[:, 1, :], ps[4][:, S:2 * S], ACT.Sqrt, bias=stat[:, 7:8],
                           scale=1.0 / KV_RANK).then_inc(m_root, 1)
            act.wait_ge(rope_in, 1)
            act.activation(rope_t, ang, ACT.Sin).then_inc(rope_ready, 1)
            for h in range(H):
                act.wait_ge(m_ev, h + 1)
                act.activation(qm[0:HD, h, :], ps[6 + h % 2][0:HD, 0:S], ACT.Copy, scale=MLA_SCALE).then_inc(q_lo, 1)
            for t in range(8):
                act.wait_ge(m_ev, H + t + 1)
                act.activation(kmT[0:HD, 2 * t, :], ps[t % 2][0:HD, 0:S], ACT.Copy).then_inc(k_lo, 1)
            act.wait_ge(unit_done, U["mla_uv"] + 1)
            for hf in range(2):
                act.activation(vm[:, 0, hf * 512:(hf + 1) * 512], ps[2 + hf][:], ACT.Copy)
            phase_end(act)
            with act.Fori(0, 4) as i:
                exponentials(4, MLA0 + 4 * i)
            evacuate_even(oT, None)
            phase_end(act)
            phase_end(act)
            square_rows(x)
            evacuate_even(hT, small("g_ffn2")[:, KT:2 * KT])
            phase_end(act)
            ffn_tanh(U["up2"], 2)
            phase_end(act)
            square_rows(x)

        @block.vector
        def _(dve):
            def normalise(src):
                n = n_norm.setdefault("dve", 0)
                n_norm["dve"] += 1
                r = n_norm['root'] = n_norm.get('root', 0) + 1
                dve.wait_ge(root_ready, r)
                dve.reciprocal(stat[:, 4:6], stat[:, 2:4])
                dve.drain()
                for b in range(NB):
                    m = dve.tensor_scalar(xn[:, b, :], src[:, b, :], stat[:, 4 + b:5 + b], None, ALU.mult)
                m.then_inc(xn_ready, 1)

            def evacuate_odd(dst, gain):
                n = n_norm["dve"] - 1
                for q in (1, 3):
                    dve.wait_ge(tr_ready, 4 * n + q + 1)
                    for k in (2 * q, 2 * q + 1):
                        src = ps[4 + q][:, (k % 2) * S:(k % 2 + 1) * S]
                        if gain is None:
                            dve.tensor_copy(dst[:, k, :], src)
                        else:
                            dve.tensor_scalar(dst[:, k, :], src, gain[:, k:k + 1], None, ALU.mult)

            def attention(N, n0, finish, sink=None, middle=None):
                for s in range(N + 2):
                    if s < N:
                        j = s % 2
                        dve.wait_ge(s_mm, n0 + s + 1)
                        if middle is not None:
                            middle(s, n0)
                        else:
                            dve.wait_ge(b_staged, n0 + s + 1)
                            dve.sem_inc(apart, 1)
                            for a, b in ((0, P), (P, KEYS)):
                                dve.tensor_tensor_reduce(out=sc[:, j, a:b], in0=ps[j][:, a:b], in1=b_st[:, j, a:b],
                                                         scale=1.0, scalar=-3e38, op0=ALU.add, op1=ALU.max,
                                                         accum_out=mx[:, j, a // P:a // P + 1])
                            dve.drain()
                            if sink is not None:
                                dve.tensor_scalar(mx[:, j, 0:2], mx[:, j, 0:2], sink(s), None, ALU.max)
                                dve.drain()
                            dve.tensor_scalar(mx[:, j, 2:4], mx[:, j, 0:2], -1.0, None, ALU.mult).then_inc(max_ready, 1)
                    if 1 <= s <= N:
                        t = s - 1
                        dve.wait_ge(t_mm, n0 + t + 1)
                        dve.tensor_copy(pT[:, t % 2, :], ps[2 + t % 2][:, 0:KEYS]).then_inc(pt_ready, 1)
                        if middle is None:
                            dve.drain()
                            sums = mx[:, t % 2, 4:6]
                            if sink is not None:
                                dve.tensor_tensor(mx2[:, t % 2, 0:2], sums, mx[:, t % 2, 6:8], ALU.add)
                                dve.drain()
                                sums = mx2[:, t % 2, 0:2]
                            dve.reciprocal(mx2[:, t % 2, 0:2], sums)
                    if s >= 2:
                        t = s - 2
                        dve.drain()
                        dve.wait_ge(o_mm, n0 + t + 1)
                        finish(t, ps[4 + t % 2])
                dve.drain()

            def post_norm(n_post, n_sq):
                dve.wait_ge(sq2_ready, n_post + 1)
                dve.tensor_tensor(stat[:, 0:2], mx[:, 0, 0:4:2], mx[:, 0, 1:4:2], ALU.add).then_inc(sum_ready, 1)
                dve.wait_ge(root2_ready, n_post + 1)
                dve.reciprocal(stat[:, 4:6], stat[:, 2:4])
                dve.wait_ge(row_in, 16 * (n_post + 1))
                dve.drain()
                for q in range(4):
                    cols = slice((q % 2) * 512, (q % 2 + 1) * 512)
                    dve.scalar_tensor_tensor(xn[:, q // 2, cols], ps[4 + q][:], stat[:, 4 + q // 2:5 + q // 2],
                                             grow[:, cols], ALU.mult, ALU.mult)
                dve.drain()
                dve.tensor_tensor(x[:], x[:], xn[:], ALU.add)

            def add_rows():
                for q in range(4):
                    cols = slice((q % 2) * 512, (q % 2 + 1) * 512)
                    dve.tensor_tensor(x[:, q // 2, cols], ps[4 + q][:], x[:, q // 2, cols], ALU.add)

            def ffn_conv():
                def conv(m, j):
                    dve.drain()
                    dve.wait_ge(ff_free, 2 + m + 1)
                    for a in range(2):
                        z, c = uz[j % 2][:, a, :], uc[j % 2][:, a, :]
                        p = conv_p[:, m, 4 * a:4 * a + 4]
                        dve.tensor_scalar(c, z[:, 0:S], p[:, 0:1], p[:, 3:4], ALU.mult, ALU.add)
                    for t in (1, 2):
                        dve.drain()
                        for a in range(2):
                            z, c = uz[j % 2][:, a, :], uc[j % 2][:, a, :]
                            ins = dve.scalar_tensor_tensor(c, z[:, t:S + t], conv_p[:, m, 4 * a + t:4 * a + t + 1], c,
                                                           ALU.mult, ALU.add)
                    ins.then_inc(ff_conv, 1)

                def act_out(m, j):
                    dve.drain()
                    dve.wait_ge(ff_tanh, m + 1)
                    g, v = uc[j % 2][:, 0, :], uc[j % 2][:, 1, :]
                    dve.scalar_tensor_tensor(ut[j % 2], ut[j % 2], 1.0, g, ALU.add, ALU.mult)
                    dve.drain()
                    dve.scalar_tensor_tensor(actT[:, m, :], ut[j % 2], 0.5, v, ALU.mult, ALU.mult).then_inc(ff_act, 1)

                def body(js, i):
                    for k in range(len(js) + 1):
                        if k < len(js):
                            conv(4 * i + js[k], js[k])
                        if k > 0:
                            act_out(4 * i + js[k - 1], js[k - 1])

                with dve.Fori(0, FT // 4) as i:
                    body(range(4), i)
                body(range(FT % 4), FT // 4)

            def ffn_act(n_ffn):
                def body(js, i):
                    for j in js:
                        dve.drain()
                        dve.wait_ge(ff_tanh, n_ffn * FT + 4 * i + j + 1)
                        dve.scalar_tensor_tensor(ut[j % 2], ut[j % 2], 1.0, ps[j % 2][:, 0:S], ALU.add, ALU.mult)
                        dve.drain()
                        dve.scalar_tensor_tensor(actT[:, 4 * i + j, :], ut[j % 2], 0.5, ps[j % 2][:, S:2 * S],
                                                 ALU.mult, ALU.mult).then_inc(ff_act, 1)

                with dve.Fori(0, FT // 4) as i:
                    body(range(4), i)
                body(range(FT % 4), FT // 4)

            dve.drain().then_inc(max_ready, HEAD0)
            dve.drain().then_inc(pt_ready, HEAD0)
            dve.drain().then_inc(ff_act, 2)
            dve.memset(stat[:, 6:7], 64e-5)
            dve.memset(stat[:, 7:8], 1e-6).then_inc(eps_ready, 1)
            dve.drain().then_inc(pair_done, 1)
            dve.drain().then_inc(mixed, 1)
            dve.memset(lz, 0.0)
            dve.memset(zs, 0.0)
            dve.memset(v_pad, 0.0)
            dve.memset(P0, 0.0)
            dve.wait_ge(params_in, 48)
            normalise(x)
            evacuate_odd(hT, small("g_mix"))
            phase_end(dve)

            dve.wait_ge(lora_free, 2)
            dve.tensor_tensor(lora, lz[:, :, 0:S], lz[:, :, 1:S + 1], ALU.subtract)
            dve.drain()
            for t in range(3):
                m = dve.scalar_tensor_tensor(lora[:, t, :], lora[:, t, :], small("mu_lora")[:, t:t + 1],
                                             lz[:, t, 1:S + 1], ALU.mult, ALU.add)
            m.then_inc(lora_mix, 1)
            dve.wait_ge(gates_tanh, 1)
            dve.tensor_scalar(gates[:], gates[:], 0.5, 0.5, ALU.mult, ALU.add)
            dve.wait_ge(lora_tanh, 1)
            dve.tensor_scalar(lora[:, 1:3, :], lora[:, 1:3, :], 0.5, 0.5, ALU.mult, ALU.add)
            dve.memset(SV[0:HD, 0, :, :], 0.0)
            dve.drain().then_inc(lora_ready, 1)

            def chunks(a):
                return a.rearrange("p (c t) -> p c t", c=NC)

            def front(m, j):
                def col(c):
                    return ast[:, j, c:c + 1]

                dve.wait_ge(staged, m + 1)
                dve.wait_ge(zs_ready, m + 1)
                dve.tensor_tensor(dz, zs[:, :, 0:S], zs[:, :, 1:S + 1], ALU.subtract)
                dve.drain()
                for t, (dst, mu) in enumerate(((r_f, MU_R), (k_f, MU_K), (v_pad[:, CH:CH + S], MU_V))):
                    ins = dve.scalar_tensor_tensor(dst, dz[:, t, :], col(mu), zs[:, t, 1:S + 1], ALU.mult, ALU.add)
                ins.then_inc(mixed, 1)
                dve.drain()
                dve.tensor_scalar(kk, k_f, col(K_K), None, ALU.mult)
                dve.drain()
                dve.tensor_tensor(kk2, kk, kk, ALU.mult).then_inc(kk2_ready, 1)
                yield
                dve.drain()
                dve.wait_ge(lora_out, m + 1)
                dve.tensor_scalar(ld, th_w, -0.5 * C_DECAY, -0.5 * C_DECAY, ALU.mult, ALU.add)
                dve.tensor_scalar(th_a, th_a, 0.5, 0.5, ALU.mult, ALU.add)
                dve.drain()
                dve.tensor_tensor_scan(cum, chunk_keep, ld, 0.0, ALU.mult, ALU.add)
                dve.tensor_scalar(km, th_a, 1.0, col(K_A), ALU.subtract, ALU.mult)
                dve.drain()
                dve.tensor_tensor(cum1, cum, ld, ALU.subtract).then_inc(cum_ready, 1)
                dve.scalar_tensor_tensor(km, km, 1.0, k_f, ALU.add, ALU.mult)
                dve.drain()
                dve.scalar_tensor_tensor(rk, r_f, col(R_K), km, ALU.mult, ALU.mult)
                yield
                dve.drain()
                dve.wait_ge(exp_ready, m + 1)
                dve.tensor_tensor(BK[:, :, 1, :], chunks(km), chunks(e2), ALU.mult)
                dve.tensor_tensor(AR[:, :, 1, :], chunks(r_f), chunks(e1), ALU.mult)
                yield
                dve.drain()
                dve.wait_ge(nrm_ready, m + 1)
                dve.tensor_scalar(nrm, nrm, 1e-12, None, ALU.max)
                dve.drain()
                dve.reciprocal(nrm, nrm)
                dve.drain()
                dve.tensor_tensor(kk, kk, nrm, ALU.mult)
                dve.drain()
                dve.scalar_tensor_tensor(AR[:, :, 0, :], chunks(kk), -1.0, chunks(e3), ALU.mult, ALU.mult)
                dve.tensor_tensor(kk2, kk, th_a, ALU.mult)
                dve.drain()
                dve.tensor_tensor(BK[:, :, 0, :], chunks(kk2), chunks(e2), ALU.mult).then_inc(bkar_ready, 1)

            def masks(m, j):
                dve.wait_ge(shift_ready, m + 1)
                for hh in range(2):
                    G = ps[4 + hh][:].rearrange("p (c w t) -> p c w t", c=NC, w=2)
                    keep = tri[:, 0:CH].unsqueeze(1)
                    keep_r = tri[:, CH:P].unsqueeze(1)
                    dve.tensor_tensor(GR[:, :, hh, :], G[:, :, 1, :], keep_r.broadcast_to((P, NC, CH)), ALU.mult)
                    dve.tensor_tensor(LR[CH:P, :, hh, :], G[CH:P, :, 0, :],
                                      keep[CH:P].broadcast_to((CH, NC, CH)), ALU.mult)
                    k0 = keep[0:CH].broadcast_to((CH, 2, CH))
                    dve.tensor_tensor(P0[0:CH, 2 * hh:2 * hh + 2, 0:CH], G[0:CH, 0:NC:2, 0, :], k0, ALU.mult)
                    dve.tensor_tensor(P0[CH:P, 2 * hh:2 * hh + 2, CH:P], G[0:CH, 1:NC:2, 0, :], k0, ALU.mult)
                dve.drain()
                dve.tensor_tensor(Zp[1], P0, ident.unsqueeze(1).broadcast_to((P, 4, P)), ALU.add).then_inc(p0_ready, 1)
                dve.tensor_tensor(bonus[:, j, :], ps[2][:, 0:S], v_pad[:, CH:CH + S], ALU.mult).then_inc(bonus_ready, 1)
                dve.drain()

            def reciprocal_root(n):
                dve.wait_ge(rstd_root, n + 1)
                dve.reciprocal(vrec, vroot).then_inc(vrec_ready, 1)

            def rwkv_pair(n, j, first=False, last=False):
                steps = iter(()) if last else front(n + 1, 1 - j)
                next(steps, None)
                if not first:
                    reciprocal_root(n - 1)
                for lvl in range(1, 6):
                    dve.drain()
                    dve.wait_ge(z_mm, 5 * n + lvl)
                    dve.tensor_tensor(Zp[(lvl + 1) % 2].rearrange("p a b -> p (a b)"), ps[6][:],
                                      Zp[lvl % 2].rearrange("p a b -> p (a b)"), ALU.add).then_inc(z_ready, 1)
                    if lvl in (1, 3, 4):
                        next(steps, None)
                for c in range(NC):
                    lo = (c % 2) * CH
                    dve.wait_ge(r_mm, 4 * n + c + 1)
                    dve.tensor_copy(Rs[lo:lo + CH].rearrange("p h d -> p (h d)"),
                                    ps[7][lo:lo + CH, 0:P]).then_inc(r_ready, 1)
                    if c < NC - 1:
                        for hh in range(2):
                            dve.tensor_scalar(Sw[0:HD, hh, :], SV[0:HD, c, hh, :], Wc[0:HD, c, hh:hh + 1],
                                              None, ALU.mult)
                        dve.drain()
                        dve.wait_ge(ds_mm, 3 * n + c + 1)
                        for hh in range(2):
                            m = dve.scalar_tensor_tensor(SV[0:HD, c + 1, hh, :], ps[5][0:HD, hh * HD:(hh + 1) * HD],
                                                         Wc[0:HD, c, hh:hh + 1], Sw[0:HD, hh, :],
                                                         ALU.mult, ALU.add)
                        m.then_inc(state_ready, 1)
                        dve.drain()
                dve.wait_ge(pair_done, n + 1)
                dve.wait_ge(y_mm, n + 1)
                dve.tensor_copy(y_f, ps[6][:, 0:S]).then_inc(y_ready, 1)
                dve.drain()
                dve.wait_ge(mean_mm, n + 1)
                dve.scalar_tensor_tensor(y_f, ps[3][:, 0:S], -1.0 / HD, y_f, ALU.mult, ALU.add)
                dve.drain()
                dve.tensor_tensor(yq, y_f, y_f, ALU.mult).then_inc(yq_ready, 1)
                for _ in steps:
                    pass
                if last:
                    reciprocal_root(n)
                else:
                    masks(n + 1, 1 - j)

            for _ in front(0, 0):
                pass
            masks(0, 0)
            rwkv_pair(0, 0, first=True)
            with dve.Fori(0, PAIRS // 2 - 1) as i:
                rwkv_pair(2 * i + 1, 1)
                rwkv_pair(2 * i + 2, 0)
            rwkv_pair(PAIRS - 1, 1, last=True)
            phase_end(dve)

            dve.memset(Vblk, 0.0)
            dve.memset(cp_, 0.0)
            for m in range(8):
                dve.wait_ge(unit_done, U["nsa_q"] + m + 1)
                src = ps[m % 2][HD:P, :].rearrange("p (a t) -> p a t", a=2)
                if m < 4:
                    dve.tensor_scalar(qT[0:HD, 4 * m + 1:4 * m + 4:2, :], src, SCALE, None, ALU.mult).then_inc(ev_hi, 1)
                else:
                    dve.tensor_copy((kcT, vcT, ksT, kwT)[m - 4][0:HD, 1:4:2, :], src).then_inc(ev_hi, 1)
            dve.drain()
            dve.wait_ge(ev_lo, 6)
            for w_ in range(2):
                t = (kcT, vcT)[w_][0:HD].rearrange("p g (a l) -> p l g a", l=16)
                for par in range(2):
                    for late in range(2):
                        o = blk[w_][par * HD:(par + 1) * HD, 8 * late:8 * late + 8, :].rearrange(
                            "p l (g a) -> p l g a", g=GROUPS)
                        pos = cmp_pos[0:HD, w_, 16 * late + par:16 * late + 16:2].unsqueeze(2)
                        for lp in range(8):
                            m = dve.tensor_scalar(o[:, lp, :, :], t[:, par + 2 * lp, :, late:late + N_CMP],
                                                  pos[:, lp, 0:1], None, ALU.add)
                m.then_inc(blk_ready, 1)
            dve.wait_ge(unit_done, U["nsa_v"] + 2)
            dve.tensor_copy(v_sw[:, 1, :], ps[3][:])
            dve.wait_ge(unit_done, U["cmp"] + 2)
            hx = xg.rearrange("p a b -> p (a b)")
            hb = blk[0].rearrange("p a b -> p (a b)")[:, 0:120]
            dve.tensor_copy(hb, ps[4][:, 0:120])
            dve.drain()
            dve.tensor_tensor(hx, hb, hb, ALU.mult)
            dve.drain()
            dve.tensor_scalar(hx, hx, 0.044715, 1.0, ALU.mult, ALU.add)
            dve.drain()
            dve.tensor_tensor(hx, hx, hb, ALU.mult).then_inc(gelu_arg, 1)
            dve.wait_ge(gelu_tanh, 1)
            dve.scalar_tensor_tensor(hx, hx, 1.0, hb, ALU.add, ALU.mult)
            dve.drain()
            dve.tensor_scalar(hx, hx, 0.5, None, ALU.mult).then_inc(hid_ready, 1)
            dve.wait_ge(kv_mm, 1)
            dve.tensor_copy(kcmp[0:HD, :], ps[5][0:HD, 0:60])
            for hh in range(HPG):
                dve.tensor_copy(Vblk[32 * hh:32 * hh + N_CMP, :, hh * HD:(hh + 1) * HD],
                                ps[6][0:N_CMP, 0:S].rearrange("p (g d) -> p g d", g=GROUPS))
            phase_end(dve)

            bias = const("cmpbias").rearrange("p (g h n) -> p g h n", g=GROUPS, n=N_CMP)
            for g in range(GROUPS):
                dve.wait_ge(c_mm, g + 1)
                dve.tensor_tensor(cs, ps[0][:, 0:8 * N_CMP].rearrange("p (h n) -> p h n", n=N_CMP), bias[:, g],
                                  ALU.add)
                dve.drain()
                dve.tensor_reduce(cst8[:, 0, :], cs, AX, ALU.max)
                dve.drain()
                dve.tensor_scalar(cst8[:, 0, :], cst8[:, 0, :], -1e25, None, ALU.max)
                dve.drain()
                dve.tensor_tensor(cs, cs, cst8[:, 0, :].unsqueeze(2).broadcast_to((P, 8, N_CMP)),
                                  ALU.subtract).then_inc(c_arg, 1)
                dve.wait_ge(c_exp, g + 1)
                dve.tensor_reduce(cst8[:, 1, :], cp_[:, :, 0:N_CMP], AX, ALU.add)
                dve.drain()
                dve.tensor_scalar(cst8[:, 1, :], cst8[:, 1, :], 1e-30, None, ALU.max)
                dve.drain()
                dve.reciprocal(cst8[:, 2, :], cst8[:, 1, :])
                dve.drain()
                gate = gates[:].rearrange("p b (g h w) -> p b g h w", g=GROUPS, w=3)[:, :, g, :, 0]
                dve.tensor_tensor(cst8[:, 3, :].rearrange("p (b h) -> p b h", b=NB),
                                  cst8[:, 2, :].rearrange("p (b h) -> p b h", b=NB), gate, ALU.mult)
                dve.wait_ge(c_tr, g + 1)
                dve.tensor_copy(cpT.rearrange("p b t -> p (b t)"), ps[1][:, 0:S]).then_inc(c_pT, 1)
                dve.wait_ge(c_pv, g + 1)
                dve.drain()
                for b in range(NB):
                    dve.tensor_tensor(
                        xn[:, b, g * S:(g + 1) * S].rearrange("p (h d) -> p h d", d=HD),
                        ps[2][:, b * S:(b + 1) * S].rearrange("p (h d) -> p h d", d=HD),
                        cst8[:, 3, b * HPG:(b + 1) * HPG].unsqueeze(2).broadcast_to((P, HPG, HD)), ALU.mult)
            phase_end(dve)

            with dve.Fori(0, GROUPS) as g:
                heads = xn[:].rearrange("p b (g h d) -> p b g h d", g=GROUPS, d=HD)
                gate = gates[:].rearrange("p b (g e) -> p b g e", g=GROUPS)

                def finish(t, o):
                    j, hh, br = t % 2, t // 2, t % 2
                    dve.tensor_tensor(mx2[:, j, 2:4], mx2[:, j, 0:2], gate[:, :, g, 3 * hh + 1 + br], ALU.mult)
                    dve.drain()
                    for b in range(NB):
                        dst = heads[:, b, g, hh, :]
                        dve.scalar_tensor_tensor(dst, o[:, b * HD:(b + 1) * HD], mx2[:, j, 2 + b:3 + b], dst,
                                                 ALU.mult, ALU.add)

                attention(8, NSA0 + 8 * g, finish)
            dve.drain().then_inc(xn_ready, 1)
            n_norm["dve"] += 1
            evacuate_odd(oT, None)
            phase_end(dve)

            for m in range(KT):
                dve.wait_ge(gb_ready, 1)
                dve.wait_ge(unit_done, U["branch"] + m + 1)
                dve.tensor_tensor(mT[:, m, :], ps[m % 2][:, 0:S], gaT[:, m, :], ALU.mult)
                dve.tensor_tensor(gbT[:, m, :], ps[m % 2][:, S:2 * S], gbT[:, m, :], ALU.mult)
                dve.drain()
                dve.tensor_tensor(mT[:, m, :], mT[:, m, :], gbT[:, m, :], ALU.add).then_inc(m_ready, 1)
            post_norm(0, 0)
            phase_end(dve)
            for b in range(2):
                dve.memset(uz[b], 0.0)
            normalise(x)
            evacuate_odd(hT, small("g_ffn"))
            phase_end(dve)
            ffn_conv()
            post_norm(1, 1)
            phase_end(dve)
            normalise(x)
            evacuate_odd(hT, small("g_attn2")[:, 0:KT])
            phase_end(dve)
            for m in range(7):
                dve.wait_ge(unit_done, U["even_f"] + m + 1)
                src = ps[m % 2][HD:P, :].rearrange("p (a t) -> p a t", a=2)
                dst = (qa, qa, ka, ka, qb, qb, kb)[m]
                if m < 6:
                    dve.tensor_scalar(dst[0:HD, 4 * (m % 2) + 1:4 * (m % 2) + 4:2, :], src,
                                      1.0 if m in (2, 3) else SCALE, None, ALU.mult).then_inc(e_hi, 1)
                else:
                    dve.tensor_copy(kb[0:HD, 1, :], src[:, 0, :]).then_inc(e_hi, 1)
            dve.wait_ge(unit_done, U["even_v"] + 2)
            dve.tensor_copy(va[:, 1, :], ps[5][:])
            phase_end(dve)

            heads = xn[:].rearrange("p b (h d) -> p b h d", d=HD)
            with dve.Fori(0, 2) as i:
                def log_weights(s, n0):
                    j = s % 2
                    t0, t1, t2, t3 = sbt[j]
                    z = ps[j][:, 0:KEYS]
                    dve.wait_ge(pre_ready, 4 * i + s + 1)
                    dve.scalar_tensor_tensor(t1, z, 0.0, t0, ALU.max, ALU.add)
                    dve.tensor_tensor(t3, z, const("strict"), ALU.add)
                    dve.drain()
                    dve.tensor_tensor(t1, t1, const("nstrict"), ALU.mult)
                    dve.drain()
                    for a, b in ((0, P), (P, KEYS)):
                        dve.tensor_tensor_scan(t2[:, a:b][:, ::-1], t1[:, a:b][:, ::-1], t1[:, a:b][:, ::-1], 0.0,
                                               ALU.add, ALU.bypass)
                    dve.drain()
                    dve.tensor_tensor(sc[:, j, :], t2, t3, ALU.add).then_inc(max_ready, 1)

                def finish(t, o):
                    for b in range(NB):
                        dve.tensor_copy(heads[:, b, 4 * i + t, :], o[:, b * HD:(b + 1) * HD])

                attention(4, SB0 + 4 * i, finish, middle=log_weights)
            phase_end(dve)
            with dve.Fori(0, 2) as i:
                def finish(t, o):
                    j = t % 2
                    for b in range(NB):
                        dve.tensor_scalar(heads[:, b, SB_HEADS + 4 * i + t, :], o[:, b * HD:(b + 1) * HD],
                                          mx2[:, j, b:b + 1], None, ALU.mult)

                attention(4, SW0 + 4 * i, finish, sink=lambda s: sink_st[:, s % 2:s % 2 + 1])
            dve.drain().then_inc(xn_ready, 1)
            n_norm["dve"] += 1
            evacuate_odd(oT, None)
            phase_end(dve)
            dve.wait_ge(unit_done, U["even_out"] + 4)
            add_rows()
            phase_end(dve)
            normalise(x)
            evacuate_odd(hT, small("g_ffn2")[:, 0:KT])
            phase_end(dve)
            ffn_act(1)
            dve.wait_ge(unit_done, U["down1"] + FT // 2)
            add_rows()
            phase_end(dve)
            normalise(x)
            evacuate_odd(hT, small("g_attn2")[:, KT:2 * KT])
            phase_end(dve)

            rope = const("rope")
            dve.wait_ge(rope_pos, 16)
            dve.tensor_copy(posf, pos_i[:])
            dve.drain()
            dve.tensor_scalar(ang, posf, rope[:, 0:1], None, ALU.mult)
            dve.drain()
            dve.tensor_scalar(rope_t, ang, 1.0 / (2 * math.pi), rope[:, 1:2], ALU.mult, ALU.add)
            dve.drain()
            dve.tensor_copy(pos_n, rope_t)
            dve.drain()
            dve.tensor_copy(rope_t, pos_n)
            dve.drain()
            for part in TWO_PI:
                dve.scalar_tensor_tensor(ang, rope_t, -part, ang, ALU.mult, ALU.add)
                dve.drain()
            dve.tensor_scalar(rope_q[:, 0:1], rope[:, 1:2], 2 * math.pi, None, ALU.mult)
            dve.drain()
            dve.tensor_scalar(ang, ang, rope_q[:, 0:1], None, ALU.add)
            dve.drain()
            dve.tensor_scalar(ang, ang, 3.1415925, -3.1415925, ALU.min, ALU.max).then_inc(rope_in, 1)
            dve.wait_ge(m_root, 1)
            dve.reciprocal(rstd_f, rstd_f)
            dve.drain()
            for k in range(3):
                dve.scalar_tensor_tensor(cq[:, k, :], cq[:, k, :], small("g_q")[:, k:k + 1], rstd_f[:, 0, :],
                                         ALU.mult, ALU.mult)
            for k in range(2):
                m = dve.scalar_tensor_tensor(ckv[:, k, :], ckv[:, k, :], small("g_kv")[:, k:k + 1], rstd_f[:, 1, :],
                                             ALU.mult, ALU.mult)
            m.then_inc(m_norm, 1)
            dve.wait_ge(rope_ready, 1)
            dve.tensor_scalar(rope_t, rope_t, rope[:, 2:3], None, ALU.mult)
            dve.drain()
            dve.tensor_scalar(rope_q, rope_t, MLA_SCALE, None, ALU.mult)
            dve.drain()

            def rotate(dst, src, table):
                dve.tensor_tensor(rt[HD:HD + ROPE, 0, :], src[HD:HD + ROPE], table[HD:HD + ROPE], ALU.mult)
                dve.tensor_tensor(rt[HD:HD + ROPE, 1, :], src[HD + ROPE:P], table[HD + ROPE:P], ALU.mult)
                dve.drain()
                return dve.tensor_tensor(dst, rt[HD:HD + ROPE, 0, :], rt[HD:HD + ROPE, 1, :], ALU.add)

            rotate(kr[HD:HD + ROPE], ps[2][:, S:2 * S], rope_t).then_inc(kr_ready, 1)
            for h in range(H):
                dve.drain()
                dve.wait_ge(m_ev, h + 1)
                rotate(qm[HD:HD + ROPE, h, :], ps[6 + h % 2][:, 0:S], rope_q).then_inc(q_hi, 1)
            for t in range(8):
                dve.wait_ge(m_ev, H + t + 1)
                dve.tensor_copy(kmT[0:HD, 2 * t + 1, :], ps[t % 2][HD:P, 0:S]).then_inc(k_hi, 1)
            dve.wait_ge(unit_done, U["mla_uv"] + 1)
            for hf in range(2):
                dve.tensor_copy(vm[:, 1, hf * 512:(hf + 1) * 512], ps[4 + hf][:])
            phase_end(dve)
            with dve.Fori(0, 4) as i:
                def finish(t, o):
                    j = t % 2
                    for b in range(NB):
                        dve.tensor_scalar(heads[:, b, 4 * i + t, :], o[:, b * HD:(b + 1) * HD],
                                          mx2[:, j, b:b + 1], None, ALU.mult)

                attention(4, MLA0 + 4 * i, finish)
            dve.drain().then_inc(xn_ready, 1)
            n_norm["dve"] += 1
            evacuate_odd(oT, None)
            phase_end(dve)
            dve.wait_ge(unit_done, U["mla_out"] + 4)
            add_rows()
            phase_end(dve)
            normalise(x)
            evacuate_odd(hT, small("g_ffn2")[:, KT:2 * KT])
            phase_end(dve)
            ffn_act(2)
            dve.wait_ge(unit_done, U["down2"] + FT // 2)
            add_rows()
            phase_end(dve)
            normalise(x)
            dve.wait_ge(row_in, 48)
            dve.drain()
            for b in range(NB):
                m = dve.tensor_tensor(xn[:, b, :], xn[:, b, :], grow[:], ALU.mult)
            m.then_inc(final_ready, 1)

        @block.gpsimd
        def _(pool):
            pool.drain().then_inc(q_staged, HEAD0)
            pool.drain().then_inc(b_staged, HEAD0)
            pool.dma_start(aux, aux_d).then_inc(aux_in, 16)
            phase_end(pool)
            pool.wait_ge(aux_in, 16)

            def stage_aux(m, j):
                pool.tensor_copy(ast[:, j, :], aux[:, m, :]).then_inc(staged, 1)
                pool.wait_ge(staged, m + 1)
                pool.sem_inc(apart, 1)
                pool.tensor_scalar(half[:, j, :], ast[:, j, W0:A0 + 1], 0.5, None, ALU.mult).then_inc(half_ready, 1)

            def finish_pair(n, j):
                pool.tensor_copy(ln_st, aux[:, n, LN_W:LN_B + 1])
                pool.drain()
                pool.wait_ge(vrec_ready, n + 1)
                pool.sem_inc(apart, 1)
                pool.tensor_tensor(y_f, y_f, vrec, ALU.mult)
                pool.drain()
                pool.tensor_scalar(y_f, y_f, ln_st[:, 0:1], ln_st[:, 1:2], ALU.mult, ALU.add)
                pool.drain()
                pool.tensor_tensor(y_f, y_f, bonus[:, j, :], ALU.add)
                pool.drain()
                pool.tensor_tensor(oaT[:, n, :], y_f, g_f[:, j, :], ALU.mult)
                pool.drain().then_inc(pair_done, 1)

            stage_aux(0, 0)
            stage_aux(1, 1)
            with pool.Fori(0, PAIRS // 2 - 1) as i:
                for j in range(2):
                    pool.wait_ge(bkar_ready, 2 * i + j + 1)
                    stage_aux(2 * i + j + 2, j)
                    finish_pair(2 * i + j, j)
            for n in (PAIRS - 2, PAIRS - 1):
                finish_pair(n, n % 2)
            phase_end(pool)

            for k in range(KT):
                pool.tensor_scalar(gaT[:, k, :], gaT[:, k, :], 0.5, 0.5, ALU.mult, ALU.add)
            phase_end(pool)
            phase_end(pool)

            def stage(N, n0, query, bias):
                for s in range(N):
                    j = s % 2
                    pool.wait_ge(s_mm, n0 + s - 1)
                    pool.sem_inc(apart, 1)
                    query(s, j).then_inc(q_staged, 1)
                    pool.wait_ge(max_ready, n0 + s - 1)
                    pool.sem_inc(apart, 1)
                    bias(s, j).then_inc(b_staged, 1)

            with pool.Fori(0, GROUPS) as g:
                stage(8, NSA0 + 8 * g,
                      lambda s, j: pool.tensor_copy(q_st[0:HD, j, :], qT[0:HD, HPG * g + s // 2, :]),
                      lambda s, j: pool.tensor_tensor(b_st[:, j, :], dist, const("slope").unsqueeze(2)[:, HPG * g + s // 2, :].broadcast_to((P, KEYS)), ALU.mult))
            phase_end(pool)
            pool.dma_start(grow[:], rows_d[0:1, :].broadcast_to((P, D))).then_inc(row_in, 16)
            pool.wait_ge(gb_done, 4)
            for k in range(KT):
                m = pool.tensor_scalar(gbT[:, k, :], gbT[:, k, :], 0.5, 0.5, ALU.mult, ALU.add)
            m.then_inc(gb_ready, 1)
            phase_end(pool)
            pool.dma_start(grow[:], rows_d[1:2, :].broadcast_to((P, D))).then_inc(row_in, 16)
            phase_end(pool)
            phase_end(pool)
            pool.dma_start(grow[:], rows_d[2:3, :].broadcast_to((P, D))).then_inc(row_in, 16)
            pool.dma_start(pos_i[:], pos_d.broadcast_to((P, S))).then_inc(rope_pos, 16)
            pool.dma_start(swb, swbias_d).then_inc(swb_in, 16)
            phase_end(pool)
            phase_end(pool)
            with pool.Fori(0, 2) as i:
                for s in range(4):
                    pool.wait_ge(s_mm, SB0 + 4 * i + s - 1)
                    pool.sem_inc(apart, 1)
                    pool.tensor_copy(q_st[0:HD, s % 2, :], qa[0:HD, 4 * i + s, :]).then_inc(q_staged, 1)
            phase_end(pool)
            pool.wait_ge(swb_in, 16)
            pool.drain().then_inc(b_staged, SB_HEADS)
            with pool.Fori(0, 2) as i:
                def bias(s, j):
                    h = 4 * i + s
                    pool.tensor_copy(b_st[:, j, P:KEYS], swb[:, h, :])
                    pool.tensor_copy(b_st[:, j, 0:P], swb[:, h, P:S])
                    return pool.tensor_copy(sink_st[:, j:j + 1], small("sinks").unsqueeze(2)[:, h, :])

                for s in range(4):
                    j = s % 2
                    pool.wait_ge(s_mm, SW0 + 4 * i + s - 1)
                    pool.sem_inc(apart, 1)
                    pool.tensor_copy(q_st[0:HD, j, :], qb[0:HD, 4 * i + s, :]).then_inc(q_staged, 1)
                    pool.wait_ge(p_ready, SW0 + 4 * i + s - 1)
                    pool.sem_inc(apart, 1)
                    bias(s, j).then_inc(b_staged, 1)
            phase_end(pool)
            phase_end(pool)
            phase_end(pool)
            phase_end(pool)
            phase_end(pool)
            pool.wait_ge(kr_ready, 1)
            for h in range(H):
                pool.tensor_copy(kmT[HD:HD + ROPE, h, :], kr[HD:HD + ROPE])
            phase_end(pool)
            pool.tensor_copy(b_st[:, 0, :], const("causal"))
            pool.tensor_copy(b_st[:, 1, :], const("causal"))
            pool.drain().then_inc(b_staged, H)
            with pool.Fori(0, 4) as i:
                for s in range(4):
                    pool.wait_ge(s_mm, MLA0 + 4 * i + s - 1)
                    pool.sem_inc(apart, 1)
                    pool.tensor_copy(q_st[0:HD + ROPE, s % 2, :], qm[0:HD + ROPE, 4 * i + s, :]).then_inc(q_staged, 1)
            phase_end(pool)
            phase_end(pool)
            phase_end(pool)
            phase_end(pool)
            pool.wait_ge(final_ready, 1)
            pool.dma_start(out, xn[:]).then_inc(out_done, 16)
            pool.wait_ge(out_done, 16)


def _tiles(w, c0, c1):
    return w[:, c0:c1].reshape(w.shape[0] // P, P, c1 - c0).transpose(1, 0, 2)


def _constants():
    c = np.zeros((P, N_CONST), np.float32)

    def put(name, v):
        c[:, CO[name][0]:CO[name][1]] = v

    p = np.arange(P)
    put("ident", np.eye(P))
    put("headsum", (p[:, None] // HD == p[None, :] // HD))
    put("ones", 1.0)
    put("chunk", (np.arange(S) % CH != 0)[None, :])
    s = p[:, None] % CH
    put("tri", np.concatenate([s < np.arange(CH)[None, :], s <= np.arange(CH)[None, :]], 1))
    rel = np.concatenate([p[:, None] - p[None, :], P + p[:, None] - np.arange(S)[None, :]], 1)
    put("dist", np.where(rel >= 0, rel, BIG))
    put("causal", np.where(rel >= 0, 0.0, -BIG))
    put("strict", np.where(rel > 0, 0.0, -BIG))
    put("nstrict", np.where(rel > 0, -1.0, 0.0))
    slopes = np.exp2(-8.0 * np.arange(1, H + 1) / H)
    put("slope", -slopes[None, :])
    t = (np.arange(NB)[None, :] * P + p[:, None]).reshape(P, 1, NB, 1, 1)
    mid = (np.arange(N_CMP) * 16 + 15.5).reshape(1, 1, 1, 1, N_CMP)
    end = (np.arange(N_CMP) * 16 + 31).reshape(1, 1, 1, 1, N_CMP)
    sl = slopes.reshape(1, GROUPS, 1, HPG, 1)
    put("cmpbias", np.where(end <= t, -sl * (t - mid), -BIG).reshape(P, -1))
    half = ROPE // 2
    freq = (10000.0 ** (-np.arange(half, dtype=np.float32) / np.float32(half))).astype(np.float32)
    rope = np.zeros((P, 3), np.float32)
    rope[HD:, 0] = np.tile(freq, 4)
    rope[HD:HD + ROPE, 1] = 0.25
    rope[:, 2] = 1.0
    rope[HD + ROPE:HD + ROPE + half, 2] = -1.0
    put("rope", rope)
    return c


def _bucket(rel):
    rel = np.maximum(rel, 0)
    relf = np.maximum(rel, 1).astype(np.float32)
    large = 16 + (np.log(relf / np.float32(16)) / np.float32(math.log(8.0)) * np.float32(16)).astype(np.int32)
    return np.where(rel < 16, rel, np.minimum(large, 31))


def _layout(v):
    cols = lambda a: a.reshape(-1, P).T
    w_in = v["w_in"][0]
    q0 = 3360
    kc, vc, ks, vs, kw, vw, gl, ga, gb = 4384, 4640, 4896, 5152, 5408, 5664, 5920, 5968, 6992
    units = []

    def fm(w, *ranges):
        units.append(np.concatenate([_tiles(w, a, b) for a, b in ranges], 2).reshape(P, UNIT))

    def tm(w, c0, c1, per):
        t = _tiles(w, c0, c1)
        for k in range(0, t.shape[1], per):
            units.append(t[:, k:k + per].reshape(P, -1))

    fm(w_in, (3072, 3328))
    for n in range(PAIRS):
        a, b = n * P, (n + 1) * P
        fm(w_in, (a, b), (D + a, D + b))
        fm(w_in, (2 * D + a, 2 * D + b), (ga + a, ga + b))
    for n in range(4):
        fm(w_in, (q0 + n * 256, q0 + (n + 1) * 256))
    for c in (kc, vc, ks, kw):
        fm(w_in, (c, c + 256))
    vsw = np.concatenate([w_in[:, vs:vs + 256], w_in[:, vw:vw + 256]], 1)
    tm(vsw, 0, 512, 4)
    for name in ("cmp_w1_k", "cmp_w1_v"):
        units.append(v[name][0].reshape(16, P, 128).transpose(1, 0, 2).reshape(P, UNIT))
    for n in range(4):
        fm(w_in, (gb + n * 256, gb + (n + 1) * 256))
    both = np.concatenate([v["w_branch_rwkv"][0], v["w_branch_nsa"][0]], 1)
    for n in range(KT):
        fm(both, (n * P, (n + 1) * P), (D + n * P, D + (n + 1) * P))
    tm(v["w_out"][0], 0, D, 2)

    def ffn(up, off, down):
        for n in range(FT):
            fm(up, (n * P, (n + 1) * P), (off + n * P, off + (n + 1) * P))
        tm(down, 0, D, 2)

    ffn(v["ffn_up"][0], F_FF, v["ffn_down"][0])
    w = v["even_w_in_2"][0]
    for c in (0, 256, 512, 768, 1536, 1792):
        fm(w, (c, c + 256))
    fm(w, (2048, 2304))
    tm(w, 1024, 1536, 4)
    tm(v["even_w_out_2"][0], 0, D, 2)
    up = [np.concatenate([v["ffn_w_gate_2"][n], v["ffn_w_up_2"][n]], 1) for n in range(2)]
    ffn(up[0], F_FF, v["ffn_w_down_2"][0])
    w = v["mla_w_down_2"][0]
    r0 = Q_RANK + KV_RANK
    half = ROPE // 2
    swap = np.concatenate([w[:, :r0], np.zeros((D, HD), np.float32), w[:, r0:],
                           w[:, r0 + half:], w[:, r0:r0 + half]], 1)
    for n in range(3):
        fm(swap, (n * 256, (n + 1) * 256))
    w = v["mla_w_uq_2"][0].reshape(Q_RANK, H, HD + ROPE)
    w = np.concatenate([w, w[:, :, HD + half:], w[:, :, HD:HD + half]], 2).reshape(Q_RANK, H * P)
    for n in range(4):
        t = _tiles(w, n * 512, (n + 1) * 512).reshape(P, -1)
        units.append(np.concatenate([t, np.zeros((P, UNIT - t.shape[1]), np.float32)], 1))
    w = v["mla_w_ukv_2"][0].reshape(KV_RANK, H, 2 * HD)
    units.append(_tiles(w[:, :, :HD].reshape(KV_RANK, D), 0, D).reshape(P, UNIT))
    units.append(_tiles(w[:, :, HD:].reshape(KV_RANK, D), 0, D).reshape(P, UNIT))
    tm(v["mla_w_o_2"][0], 0, D, 2)
    ffn(up[1], F_FF, v["ffn_w_down_2"][1])
    weights = np.stack(units)
    assert weights.shape == (N_UNITS, P, UNIT), weights.shape

    aux = np.zeros((P, PAIRS, AUX), np.float32)
    heads = lambda a: a.reshape(-1, PAIRS, P)
    aux[0:64, :, 0:128] = heads(v["rwkv_w2"][0])
    aux[64:128, :, 0:128] = heads(v["rwkv_a2"][0])
    aux[:, :, 128:256] = heads(v["rwkv_g2"][0][:P])
    aux[0:32, :, 256:384] = heads(v["rwkv_g2"][0][P:])
    mu = v["rwkv_mu"][0]
    for c, a in ((MU_R, mu[:D]), (MU_K, mu[D:2 * D]), (MU_V, mu[2 * D:3 * D]), (W0, v["rwkv_w0"]),
                 (A0, v["rwkv_a0"]), (K_K, v["rwkv_k_k"]), (K_A, v["rwkv_k_a"]), (R_K, v["rwkv_r_k"]),
                 (LN_W, v["rwkv_ln_w"]), (LN_B, v["rwkv_ln_b"])):
        aux[:, :, c] = cols(a)

    small = np.zeros((P, N_SMALL), np.float32)

    def put(name, a, rows=P):
        small[:rows, SO[name][0]:SO[name][0] + a.reshape(rows, -1).shape[1]] = a.reshape(rows, -1)

    put("w_small", np.concatenate([_tiles(w_in, 3328, 3360), _tiles(w_in, gl, gl + 48)], 2))
    mu_l = np.zeros((3, P), np.float32)
    mu_l[0], mu_l[1], mu_l[2, :32] = mu[3072:3200], mu[3200:3328], mu[3328:]
    put("mu_lora", mu_l.T)
    put("g_mix", cols(v["norm_mix_pre"]))
    put("g_ffn", cols(v["norm_ffn_pre"]))
    put("g_attn2", cols(v["attn_norm_2"]))
    put("g_ffn2", cols(v["ffn_norm_2"]))
    put("g_q", cols(v["mla_q_norm_2"]))
    put("g_kv", cols(v["mla_kv_norm_2"]))
    taps = np.concatenate([v["ffn_conv_w"][0], v["ffn_conv_b"]], 0)
    put("conv", taps.reshape(4, 2, FT, P).transpose(3, 2, 1, 0))
    put("cmp_w2", np.concatenate([v["cmp_w2_k"][0], v["cmp_w2_v"][0]], 1))
    put("cmp_pos", np.stack([v["cmp_pos_k"][0].T, v["cmp_pos_v"][0].T], 1), HD)
    put("sinks", np.repeat(v["even_sinks_2"], P, 0))

    rel = P + np.arange(P)[:, None] - np.arange(S)[None, :]
    table = v["rel_bias_table_2"][_bucket(rel)]
    swb = np.where(((rel >= 0) & (rel < 128))[:, :, None], table, np.float32(-BIG))
    swb = np.ascontiguousarray(swb.transpose(0, 2, 1))
    rows = np.stack([v["norm_mix_post"][0], v["norm_ffn_post"][0], v["final_norm_2"]])
    return {
        "weights": weights, "aux": aux, "consts": _constants(), "small": small, "rows": rows,
        "swbias": swb.astype(np.float32),
        "x": np.ascontiguousarray(v["x"][0].reshape(NB, P, D).transpose(1, 0, 2)),
        "positions": np.ascontiguousarray(v["positions_2"]),
    }


def kernel(**inputs):
    import concourse.bacc as _bacc
    from concourse.bass_utils import run_bass_kernel_spmd as _run

    arrays = _layout({k: np.asarray(a) for k, a in inputs.items()})
    nc = _bacc.Bacc("TRN2", target_bir_lowering=False, num_devices=1)
    args = [nc.dram_tensor("in_" + k, a.shape, mybir.dt.from_np(a.dtype), kind="ExternalInput").ap()
            for k, a in arrays.items()]
    out = nc.dram_tensor("out_0", (P, NB, D), F32, kind="ExternalOutput").ap()
    build(nc, args, out)
    r = _run(nc, [{"in_" + k: a for k, a in arrays.items()}], core_ids=[0])
    y = np.asarray(r.results[0]["out_0"])
    return np.ascontiguousarray(y.transpose(1, 0, 2)).reshape(1, S, D)
```

```python
from contextlib import ExitStack
import math

import numpy as np
import concourse.bass as bass
from concourse import mybir

F32 = mybir.dt.float32
F32R = mybir.dt.float32r
I32 = mybir.dt.int32
ALU = mybir.AluOpType
ACT = mybir.ActivationFunctionType
AX = mybir.AxisListType.X

P = 128
S = 256
D = 1024
KT = D // P
NB = S // P
HD = 64
H = D // HD
PAIRS = H // 2
CH = 64
NC = S // CH
GROUPS = 4
HPG = H // GROUPS
N_CMP = (S - 32) // 16 + 1
SB_HEADS = 8
SW_HEADS = 8
Q_RANK, KV_RANK, ROPE = 384, 256, 32
F_FF = 2816
FT = F_FF // P
RING = 4
UNIT = 2048
BIG = 1e30
ARENA = 28400
C_DECAY = math.exp(-0.5)
SCALE = HD ** -0.5
MLA_SCALE = (HD + ROPE) ** -0.5
KEYS = P + S

PLAN = [("lora", 1), ("rwkv", 16), ("nsa_q", 4), ("nsa_k", 4), ("nsa_v", 2), ("cmp", 2),
        ("gate_b", 4), ("branch_a", 4), ("branch_b", 4), ("w_out", 4), ("up0", FT), ("down0", FT // 2),
        ("even_f", 6), ("even_kv", 1), ("even_v", 2), ("even_out", 4),
        ("up1", FT), ("down1", FT // 2),
        ("mla_down", 3), ("mla_uq", 4), ("mla_uk", 1), ("mla_uv", 1), ("mla_out", 4),
        ("up2", FT), ("down2", FT // 2)]
U = {}
N_UNITS = 0
for _name, _n in PLAN:
    U[_name] = N_UNITS
    N_UNITS += _n

CONST = [("ident", 128), ("headsum", 128), ("ones", 128), ("chunk", 256), ("tri", 128),
         ("dist", KEYS), ("causal", KEYS), ("strict", KEYS), ("nstrict", KEYS),
         ("cmpbias", GROUPS * 8 * N_CMP), ("slope", H), ("rope", 3)]
CO = {}
N_CONST = 0
for _name, _n in CONST:
    CO[_name] = (N_CONST, N_CONST + _n)
    N_CONST += _n

SMALL = [("w_small", KT * 80), ("mu_lora", 3), ("g_mix", KT), ("g_ffn", KT), ("g_attn2", 2 * KT),
         ("g_ffn2", 2 * KT), ("g_q", 3), ("g_kv", 2), ("conv", FT * 8), ("cmp_w2", 128),
         ("cmp_pos", 64), ("sinks", 8)]
SO = {}
N_SMALL = 0
for _name, _n in SMALL:
    SO[_name] = (N_SMALL, N_SMALL + _n)
    N_SMALL += _n

_P1 = float(np.float32(6.28125))
_P2 = float(np.float32(round((2 * math.pi - _P1) * 2 ** 20) / 2 ** 20))
TWO_PI = (_P1, _P2, 2 * math.pi - _P1 - _P2)

AUX = 384 + 16
(MU_R, MU_K, MU_V, W0, A0, K_K, K_A, R_K, LN_W, LN_B) = range(384, 394)


def build(nc, ins, out):
    weights, aux_d, const_d, small_d, rows_d, swbias_d, x_d, pos_d = ins
    with ExitStack() as ctx:
        def sb(name, shape, dt=F32):
            return ctx.enter_context(nc.sbuf_tensor(name, shape, dt))

        def sem(name):
            return ctx.enter_context(nc.semaphore(name))

        ps = [ctx.enter_context(nc.psum_tensor(f"ps{i}", [P, 512], F32)) for i in range(8)]
        ring = sb("ring", [P, RING, UNIT])
        x = sb("x", [P, NB, D])
        xn = sb("xn", [P, NB, D])
        hT = sb("hT", [P, KT, S])
        oT = sb("oT", [P, KT, S])
        cst = sb("cst", [P, N_CONST])
        sml = sb("sml", [P, N_SMALL])
        grow = sb("grow", [P, D])
        pos_i = sb("pos_i", [P, S], I32)
        stat = sb("stat", [P, 8])
        gates = sb("gates", [P, NB, 48])
        q_st = sb("q_st", [P, 2, S])
        b_st = sb("b_st", [P, 2, KEYS])
        sc = sb("sc", [P, 2, KEYS])
        pT = sb("pT", [P, 2, KEYS])
        mx = sb("mx", [P, 2, 8])
        mx2 = sb("mx2", [P, 2, 8])
        sink_st = sb("sink_st", [P, 2])
        with ExitStack() as region:
            arena = region.enter_context(nc.sbuf_tensor("arena", [P, ARENA], F32))
        w_hi, w_lo = sb("w_hi", [P, 2, UNIT], F32R), sb("w_lo", [P, 2, UNIT], F32R)
        h_hi, h_lo = sb("h_hi", [P, KT, S], F32R), sb("h_lo", [P, KT, S], F32R)
        a_hi, a_lo = sb("a_hi", [P, FT, S], F32R), sb("a_lo", [P, FT, S], F32R)
        top = [0]

        def carve(*shape):
            n = int(np.prod(shape))
            a = arena[:, top[0]:top[0] + n]
            top[0] += n
            assert top[0] <= ARENA, top[0]
            if len(shape) == 1:
                return a
            names = "abcd"[:len(shape)]
            pat = f"p ({' '.join(names)}) -> p {' '.join(names)}"
            return a.rearrange(pat, **{k: v for k, v in zip(names, shape)})

        def const(name):
            return cst[:, CO[name][0]:CO[name][1]]

        def small(name):
            return sml[:, SO[name][0]:SO[name][1]]

        ident = const("ident")
        headsum = const("headsum")
        ones = const("ones")
        chunk_keep = const("chunk")
        tri = const("tri")
        dist = const("dist")
        w_small = small("w_small").rearrange("p (k c) -> p k c", k=KT)
        conv_p = small("conv").rearrange("p (f c) -> p f c", f=FT)
        cmp_w2 = small("cmp_w2")
        cmp_pos = small("cmp_pos").rearrange("p (w l) -> p w l", w=2)

        oaT = carve(PAIRS, S)
        gaT = carve(KT, S)
        gbT = carve(KT, S)
        mT = carve(KT, S)
        first_top = top[0]
        aux = carve(PAIRS, AUX)
        ast = carve(2, AUX)
        half = carve(2, 2)
        lz = carve(3, S + 1)
        lora = carve(3, S)
        zs = carve(3, S + 1)
        dz = carve(3, S)
        r_f, k_f = carve(S), carve(S)
        v_pad = carve(CH + S)
        th_w, th_a = carve(S), carve(S)
        g_f, bonus = carve(2, S), q_st
        ln_st = carve(2)
        ld, cum, cum1 = carve(S), carve(S), carve(S)
        e1, e2, e3 = carve(S), carve(S), carve(S)
        kk, kk2, km, rk, nrm = carve(S), carve(S), carve(S), carve(S), carve(S)
        BK = carve(NC, 2, CH)
        AR = carve(NC, 2, CH)
        RH = carve(NC, 2, CH)
        LR = carve(NC, 2, CH)
        GR = carve(NC, 2, CH)
        UV = carve(NC, 2, CH)
        SV = carve(NC, 2, CH)
        BKT = carve(NC, 2, CH)
        Rs = carve(2, CH)
        Sw = carve(2, CH)
        Wc = carve(NC, 2)
        P0 = carve(4, P)
        Pp = [carve(4, P), carve(4, P)]
        Qp = [carve(4, P), carve(4, P)]
        Zp = [carve(4, P), carve(4, P)]
        y_f, yq = pT[:, 0, 0:S], pT[:, 1, 0:S]
        vroot, vrec = sc[:, 0, 0:S], sc[:, 1, 0:S]
        top[0] = first_top
        qT = carve(H, S)
        kcT, vcT, ksT, kwT = (carve(GROUPS, S) for _ in range(4))
        v_sw = carve(NB, 512)
        blk = [carve(16, GROUPS * N_CMP), carve(16, GROUPS * N_CMP)]
        hid = [carve(GROUPS * N_CMP) for _ in range(2)]
        ga_, gb_ = carve(GROUPS * N_CMP), carve(GROUPS * N_CMP)
        xg = carve(2, GROUPS * N_CMP)
        kcmp = carve(GROUPS * N_CMP)
        Vblk = carve(GROUPS, 4 * HD)
        cs = carve(8, N_CMP)
        cp_ = carve(8, 32)
        cpT = carve(NB, P)
        cst8 = carve(4, 8)
        top[0] = 4 * UNIT + 2 * (KT + FT) * S
        act_f = carve(2, S)
        uz = [carve(2, S + 2), carve(2, S + 2)]
        uc = [carve(2, S), carve(2, S)]
        ut = [carve(S), carve(S)]
        top[0] = 4 * UNIT + 2 * KT * S
        qa, ka, qb = carve(8, S), carve(8, S), carve(8, S)
        kb = carve(2, S)
        va = carve(NB, 512)
        vb = carve(NB, P)
        swb = carve(8, S)
        sbt = [[carve(KEYS) for _ in range(4)] for _ in range(2)]
        top[0] = 4 * UNIT + 2 * KT * S
        qm, kmT = carve(H, S), carve(H, S)
        vm = carve(NB, D)
        cq, ckv, kr = carve(3, S), carve(2, S), carve(S)
        csq = carve(5, S)
        rstd_f = carve(2, S)
        posf, ang, rope_t, rope_q, rt = carve(S), carve(S), carve(S), carve(S), carve(2, S)
        pos_n = carve(S).bitcast(I32)

        slot_full = [sem(f"slot_full{i}") for i in range(RING)]
        unit_done = sem("unit_done")
        params_in = sem("params_in")
        row_in = sem("row_in")
        row_free = sem("row_free")
        phase = sem("phase")
        out_done = sem("out_done")
        phases = {}

        def phase_end(e):
            phases[id(e)] = phases.get(id(e), 0) + 1
            e.drain().then_inc(phase, 1)
            e.wait_ge(phase, 4 * phases[id(e)])

        def arrived(e, u, i=0, step=RING):
            assert step == RING
            e.wait_ge(slot_full[u % RING], 16 * (u // RING + 1) + 16 * i)

        norms = ["mix", "ffn0", "attn1", "ffn1", "attn2", "ffn2"]
        sq_ready = sem("sq_ready")
        root_ready = sem("root_ready")
        xn_ready = sem("xn_ready")
        tr_ready = sem("tr_ready")
        tr_free = sem("tr_free")

        n_norm = {}
        lora_mm, lora_free, staged, pair_done = map(sem, ("lora_mm", "lora_free", "staged", "pair_done"))
        lora_up, lora_out, kk2_ready, knorm = map(sem, ("lora_up", "lora_out", "kk2_ready", "knorm"))
        zs_ready, mixed, cum_ready, exp_ready = map(sem, ("zs_ready", "mixed", "cum_ready", "exp_ready"))
        nrm_ready, bkar_ready, gram, p0_ready = map(sem, ("nrm_ready", "bkar_ready", "gram", "p0_ready"))
        shift_ready = sem("shift_ready")
        q0_mm, q0_ready = sem("q0_mm"), sem("q0_ready")
        pow_mm, pq_ready, z_mm, z_ready = map(sem, ("pow_mm", "pq_ready", "z_mm", "z_ready"))
        r_mm, r_ready, u_mm, u_ready = map(sem, ("r_mm", "r_ready", "u_mm", "u_ready"))
        ds_mm, state_ready = sem("ds_mm"), sem("state_ready")
        y_mm, y_ready, mean_mm, yq_ready, var_mm = map(sem, ("y_mm", "y_ready", "mean_mm", "yq_ready", "var_mm"))
        rstd_root, rwkv_tail = sem("rstd_root"), sem("rwkv_tail")
        half_ready, bonus_ready, gate_out, vrec_ready, ln_staged, y_norm = map(
            sem, ("half_ready", "bonus_ready", "gate_out", "vrec_ready", "ln_staged", "y_norm"))
        aux_in, eps_ready, gates_tanh, lora_mix, lora_tanh, lora_ready = map(
            sem, ("aux_in", "eps_ready", "gates_tanh", "lora_mix", "lora_tanh", "lora_ready"))

        ev_lo, ev_hi, blk_ready, hid_mm, gelu_in, gelu_arg, gelu_tanh, hid_ready, kv_mm, kv_out, zeroed = map(sem, (
            "ev_lo", "ev_hi", "blk_ready", "hid_mm", "gelu_in", "gelu_arg", "gelu_tanh", "hid_ready", "kv_mm",
            "kv_out", "zeroed"))
        c_mm, c_arg, c_exp, c_tr, c_pT, c_pv, c_out = map(sem, (
            "c_mm", "c_arg", "c_exp", "c_tr", "c_pT", "c_pv", "c_out"))
        q_staged, b_staged, s_mm, pre_ready, max_ready, p_ready, t_mm, pt_ready, o_mm = map(sem, (
            "q_staged", "b_staged", "s_mm", "pre_ready", "max_ready", "p_ready", "t_mm", "pt_ready", "o_mm"))
        ga_ready, gb_done, gb_ready, m_ready, sq2_ready, sum_ready, root2_ready, post_done = map(sem, (
            "ga_ready", "gb_done", "gb_ready", "m_ready", "sq2_ready", "sum_ready", "root2_ready", "post_done"))
        ff_copied, ff_conv, ff_tanh, ff_free, ff_act = map(sem, (
            "ff_copied", "ff_conv", "ff_tanh", "ff_free", "ff_act"))
        w_hi_d, w_hi_p, w_lo_d, w_lo_p, h_hi_ready, act_split = map(sem, (
            "w_hi_d", "w_hi_p", "w_lo_d", "w_lo_p", "h_hi_ready", "act_split"))
        FU = FT + FT // 2
        SPLIT = {}
        n_split = 0
        for name, n in (("ffn0", FU), ("even", 9), ("even_out", 4), ("ffn1", FU), ("mla", 3), ("mla_out", 4),
                        ("ffn2", FU)):
            SPLIT[name] = n_split
            n_split += n

        def in_steps(e, step, tail=None):
            step(0, 0)
            with e.Fori(0, (FT - 2) // 4) as i:
                for j in range(1, 5):
                    step(j, i)
                    if tail:
                        tail(j - 1, i)
            step(FT - 1, 0)
            if tail:
                tail(FT - 2, 0)
                tail(FT - 1, 0)

        WH = UNIT // 2
        e_lo, e_hi, v_out = map(sem, ("e_lo", "e_hi", "v_out"))
        m_ev, m_sq, m_sum, m_root, m_norm, rope_ready, q_lo, q_hi, kr_ready, k_lo, k_hi, rope_in = map(sem, (
            "m_ev", "m_sq", "m_sum", "m_root", "m_norm", "rope_ready", "q_lo", "q_hi", "kr_ready", "k_lo", "k_hi",
            "rope_in"))
        apart = sem("apart")
        swb_in, rope_pos, final_ready = map(sem, ("swb_in", "rope_pos", "final_ready"))
        HEAD0 = 2
        NSA0 = HEAD0
        SB0 = NSA0 + 2 * H
        SW0 = SB0 + SB_HEADS
        MLA0 = SW0 + SW_HEADS

        block = ctx.enter_context(nc.Block())

        @block.sync
        def _(sp):
            sp.dma_start(x[:], x_d).then_inc(params_in, 16)
            sp.dma_start(cst[:], const_d).then_inc(params_in, 16)
            sp.dma_start(sml[:], small_d).then_inc(params_in, 16)
            for u in range(RING):
                sp.dma_start(ring[:, u, :], weights[u]).then_inc(slot_full[u], 16)
            groups = N_UNITS // RING
            with sp.Fori(1, groups) as i:
                for j in range(RING):
                    sp.wait_ge(unit_done, i * RING + (j - RING + 1))
                    sp.dma_start(ring[:, j, :], weights[i * RING + j]).then_inc(slot_full[j], 16)
            for u in range(groups * RING, N_UNITS):
                sp.wait_ge(unit_done, u - RING + 1)
                sp.dma_start(ring[:, u % RING, :], weights[u]).then_inc(slot_full[u % RING], 16)

        @block.tensor
        def _(pe):
            def f_tile(dst, u, tile, rhs, keys=KT, width=P, inc=None, i=0):
                w = ring[:, u % RING, :].rearrange("p (k c) -> p k c", k=KT)
                for k in range(keys):
                    m = pe.matmul(dst, w[:, k, tile * P:tile * P + width], rhs[:, k, :],
                                  start=k == 0, stop=k == keys - 1)
                if inc is not None:
                    m.then_inc(inc, 1)

            def f_unit(bank, u, rhs, i=0):
                arrived(pe, u, i)
                f_tile(bank[:, 0:S], u, 0, rhs)
                f_tile(bank[:, S:2 * S], u, 1, rhs, inc=unit_done)

            def transposes(src):
                pe.wait_ge(xn_ready, n_norm.setdefault("pe", 0) + 1)
                n_norm["pe"] += 1
                for k in range(KT):
                    for b in range(NB):
                        m = pe.transpose(ps[4 + k // 2][:, (k % 2) * S + b * P:(k % 2) * S + b * P + P],
                                         src[:, b, k * P:(k + 1) * P], ident)
                    if k % 2:
                        m.then_inc(tr_ready, 1)

            def t_rows(u0, lhs, n_units, i=0):
                for n in range(n_units):
                    arrived(pe, u0 + n)
                    w = ring[:, (u0 + n) % RING, :].rearrange("p (k c) -> p k c", k=2)
                    for k in range(2):
                        for b in range(NB):
                            for hf in range(2):
                                m = pe.matmul(ps[4 + 2 * b + hf][:], lhs[:, 2 * n + k, b * P:(b + 1) * P],
                                              w[:, k, hf * 512:(hf + 1) * 512],
                                              start=n == 0 and k == 0, stop=n == n_units - 1 and k == 1)
                    m.then_inc(unit_done, 1)

            def mixer_dense():
                for n in range(8):
                    if n >= 2:
                        pe.wait_ge(gb_done, n - 1)
                    u = U["gate_b"] + n
                    arrived(pe, u)
                    w = ring[:, u % RING, :].rearrange("p (k c) -> p k c", k=KT)
                    for tile in range(2):
                        for k in range(KT):
                            m = pe.matmul(ps[6 + n % 2][:, tile * S:(tile + 1) * S], w[:, k, tile * P:(tile + 1) * P],
                                          (hT if n < 4 else oaT)[:, k, :], start=k == 0, stop=k == KT - 1)
                            if tile == 1 and k == KT - 1:
                                m.then_inc(unit_done, 1)
                            if k % 2:
                                yield

            def attention(insts, n0, fill=iter(()), rate=(0, 0)):
                N = len(insts)
                for s in range(N + 2):
                    if s < N:
                        rows, keys, _ = insts[s]
                        bank = ps[s % 2]
                        pe.wait_ge(q_staged, n0 + s + 1)
                        pe.sem_inc(apart, 1)
                        q = q_st[0:rows, s % 2, :]
                        pe.matmul(bank[:, 0:P], q[:, 0:P], keys(0, P), start=True, stop=True)
                        pe.matmul(bank[:, P:KEYS], q[:, P:S], keys(0, S), start=True, stop=True).then_inc(s_mm, 1)
                    for _ in range(rate[s % 2]):
                        next(fill, None)
                    if 1 <= s <= N:
                        t = s - 1
                        pe.wait_ge(p_ready, n0 + t + 1)
                        for kt in range(3):
                            m = pe.transpose(ps[2 + t % 2][:, kt * P:(kt + 1) * P],
                                             sc[:, t % 2, kt * P:(kt + 1) * P], ident)
                        m.then_inc(t_mm, 1)
                    if s >= 2:
                        t = s - 2
                        values = insts[t][2]
                        o = ps[4 + t % 2]
                        pe.wait_ge(pt_ready, n0 + t + 1)
                        pe.matmul(o[:, 0:HD], pT[:, t % 2, 0:P], values(0), start=True, stop=True)
                        pe.matmul(o[:, HD:2 * HD], pT[:, t % 2, P:2 * P], values(0), start=True, stop=False)
                        pe.matmul(o[:, HD:2 * HD], pT[:, t % 2, 2 * P:3 * P], values(1), start=False,
                                  stop=True).then_inc(o_mm, 1)

            def split_product(dst, pairs, first=True, last=True):
                terms = [(l[a], r[b]) for a, b in ((0, 0), (0, 1), (1, 0)) for l, r in pairs]
                for n, (l, r) in enumerate(terms):
                    m = pe.matmul(dst, l, r, start=first and n == 0, stop=last and n == len(terms) - 1)
                return m

            def ffn_up(u0, n_ffn):
                w = [t[:].rearrange("p s (k c) -> p s k c", k=KT) for t in (w_hi, w_lo)]
                h = (h_hi, h_lo)

                def unit(j, i):
                    pe.wait_ge(ff_act if n_ffn else ff_free, 4 + n_ffn * FT + 4 * i + j - 3)
                    pe.wait_ge(w_lo_d, SPLIT[f"ffn{n_ffn}"] + 4 * i + j + 1)
                    pe.wait_ge(w_lo_p, SPLIT[f"ffn{n_ffn}"] + 4 * i + j + 1)
                    for tile in range(2):
                        m = split_product(ps[j][:, tile * S:(tile + 1) * S],
                                          [([t[:, j % 2, k, tile * P:(tile + 1) * P] for t in w],
                                            [t[:, k, :] for t in h]) for k in range(KT)])
                    m.then_inc(unit_done, 1)

                with pe.Fori(0, FT // 4) as i:
                    for j in range(4):
                        unit(j, i)
                for j in range(FT % 4):
                    unit(j, FT // 4)

            def unit_split(name, m):
                pe.wait_ge(w_lo_d, SPLIT[name] + m + 1)
                pe.wait_ge(w_lo_p, SPLIT[name] + m + 1)

            def split_f_unit(bank, name, m):
                unit_split(name, m)
                w = [t[:].rearrange("p s (k c) -> p s k c", k=KT) for t in (w_hi, w_lo)]
                for tile in range(2):
                    ins = split_product(bank[:, tile * S:(tile + 1) * S],
                                        [([t[:, m % 2, k, tile * P:(tile + 1) * P] for t in w],
                                          [t[:, k, :] for t in (h_hi, h_lo)]) for k in range(KT)])
                ins.then_inc(unit_done, 1)

            def split_rows(name, m0, lhs, n_units, before=lambda n: None):
                w = [t[:].rearrange("p s (k c) -> p s k c", k=2) for t in (w_hi, w_lo)]
                for n in range(n_units):
                    before(n)
                    unit_split(name, m0 + n)
                    for b in range(NB):
                        for hf in range(2):
                            m = split_product(ps[4 + 2 * b + hf][:],
                                              [([t[:, 2 * n + k, b * P:(b + 1) * P] for t in lhs],
                                                [t[:, n % 2, k, hf * 512:(hf + 1) * 512] for t in w])
                                               for k in range(2)], first=n == 0, last=n == n_units - 1)
                    m.then_inc(unit_done, 1)

            def ffn_down(n_ffn):
                split_rows(f"ffn{n_ffn}", FT, (a_hi, a_lo), FT // 2,
                           lambda n: pe.wait_ge(act_split, 2 + n_ffn * FT + 2 * n + 2))

            pe.wait_ge(params_in, 48)
            pe.drain().then_inc(s_mm, HEAD0)
            pe.drain().then_inc(t_mm, HEAD0)
            pe.drain().then_inc(o_mm, HEAD0)
            transposes(xn)
            phase_end(pe)

            f_unit(ps[0], U["lora"], hT)
            for k in range(KT):
                pe.matmul(ps[1][0:32, 0:S], w_small[:, k, 0:32], hT[:, k, :], start=k == 0, stop=k == KT - 1)
            for b in range(NB):
                for k in range(KT):
                    m = pe.matmul(ps[2][:, b * 48:b * 48 + 48], hT[:, k, b * P:(b + 1) * P],
                                  w_small[:, k, 32:80], start=k == 0, stop=k == KT - 1)
            m.then_inc(lora_mm, 1)

            def rwkv_dense(i, j, tiles):
                for tile in tiles:
                    u = U["rwkv"] + 2 * j + tile // 2
                    if tile % 2 == 0:
                        arrived(pe, u, i)
                    w = ring[:, u % RING, :].rearrange("p (k c) -> p k c", k=KT)
                    dst = ps[tile // 2][:, (tile % 2) * S:(tile % 2 + 1) * S]
                    for k in range(KT):
                        m = pe.matmul(dst, w[:, k, (tile % 2) * P:(tile % 2 + 1) * P], hT[:, k, :],
                                      start=k == 0, stop=k == KT - 1)
                        if k == KT - 1 and tile % 2:
                            m.then_inc(unit_done, 1)
                        if k % 2:
                            yield

            def low_rank(m, j):
                pe.wait_ge(staged, m + 1)
                st = ast[:, j, :]
                pe.matmul(ps[2][:, 0:S], st[0:64, 0:128], lora[0:64, 0, :], start=True, stop=True)
                pe.matmul(ps[3][:, S:2 * S], st[64:128, 0:128], lora[64:128, 0, :], start=True, stop=True)
                pe.matmul(ps[2][:, S:2 * S], st[:, 128:256], lora[:, 1, :], start=True, stop=False)
                pe.matmul(ps[2][:, S:2 * S], st[0:32, 256:384], lora[0:32, 2, :], start=False,
                          stop=True).then_inc(lora_up, 1)

            def key_norm(m):
                pe.wait_ge(kk2_ready, m + 1)
                pe.wait_ge(lora_out, m + 1)
                pe.matmul(ps[3][:, 0:S], headsum, kk2, start=True, stop=True).then_inc(knorm, 1)

            def grams(m, tail=None):
                pe.wait_ge(bkar_ready, m + 1)
                for hh in range(2):
                    for c in range(NC):
                        pe.matmul(ps[4 + hh][:, c * P:(c + 1) * P],
                                  BK[hh * HD:(hh + 1) * HD, c, :, :].rearrange("p a b -> p (a b)"),
                                  AR[hh * HD:(hh + 1) * HD, c, :, :].rearrange("p a b -> p (a b)"),
                                  start=True, stop=True)
                if tail is not None:
                    tail()
                for c in range(NC):
                    pe.transpose(ps[6][:, c * P:(c + 1) * P], v_pad[:, c * CH:c * CH + P], ident)
                for c in range(NC):
                    pe.transpose(ps[7][:, c * P:(c + 1) * P],
                                 BK[:, c, :, :].rearrange("p a b -> p (a b)"), ident)
                pe.wait_ge(gate_out, m + 1)
                pe.matmul(ps[2][:, 0:S], headsum, rk, start=True, stop=True).then_inc(gram, 1)

            def mean_of(n):
                pe.wait_ge(y_ready, n + 1)
                pe.matmul(ps[3][:, 0:S], headsum, y_f, start=True, stop=True).then_inc(mean_mm, 1)

            def variance_of(n):
                pe.wait_ge(yq_ready, n + 1)
                pe.matmul(ps[3][:, S:2 * S], headsum, yq, start=True, stop=True).then_inc(var_mm, 1)

            def rwkv_pair(n, j, dense=None):
                last = dense is None and n == PAIRS - 1
                pe.wait_ge(p0_ready, n + 1)
                for g in range(4):
                    m = pe.transpose(ps[4][:, g * P:(g + 1) * P], P0[:, g, :], ident)
                m.then_inc(q0_mm, 1)
                for lvl in range(6):
                    if lvl == 0:
                        pe.wait_ge(q0_ready, n + 1)
                        p_, q_, z_ = P0, Qp[1], Zp[1]
                    else:
                        pe.wait_ge(pq_ready, 10 * n + 2 * lvl)
                        p_, q_, z_ = Pp[(lvl + 1) % 2], Qp[(lvl + 1) % 2], Zp[lvl % 2]
                    if lvl < 5:
                        for g in range(4):
                            m = pe.matmul(ps[4][:, g * P:(g + 1) * P], q_[:, g, :], p_[:, g, :], start=True, stop=True)
                        m.then_inc(pow_mm, 1)
                        for g in range(4):
                            m = pe.matmul(ps[5][:, g * P:(g + 1) * P], p_[:, g, :], q_[:, g, :], start=True, stop=True)
                        m.then_inc(pow_mm, 1)
                    if lvl > 1:
                        pe.wait_ge(z_ready, 5 * n + lvl - 1)
                    if lvl > 0:
                        for g in range(4):
                            m = pe.matmul(ps[6][:, g * P:(g + 1) * P], q_[:, g, :], z_[:, g, :], start=True, stop=True)
                        m.then_inc(z_mm, 1)
                    if not last and lvl == 0:
                        pe.wait_ge(bonus_ready, n + 1)
                        low_rank(n + 1, 1 - j)
                    if not last and lvl == 2:
                        key_norm(n + 1)
                fill = iter(())
                if dense is not None:
                    pe.wait_ge(zs_ready, n + 2)
                    fill = rwkv_dense(*dense, (0, 1, 2))
                for _ in range(3):
                    next(fill, None)
                pe.wait_ge(z_ready, 5 * n + 5)
                Z = Zp[0]
                for c in range(NC):
                    lo = (c % 2) * CH
                    if c:
                        pe.wait_ge(state_ready, 3 * n + c)
                    for hh in range(2):
                        m = pe.matmul(ps[7][lo:lo + CH, hh * HD:(hh + 1) * HD], LR[:, c, hh, :], SV[:, c, hh, :],
                                      start=True, stop=True)
                    m.then_inc(r_mm, 1)
                    next(fill, None)
                    pe.wait_ge(r_ready, 4 * n + c + 1)
                    pe.sem_inc(apart, 1)
                    for hh in range(2):
                        m = pe.matmul(ps[4][0:CH, hh * HD:(hh + 1) * HD],
                                      Z[lo:lo + CH, 2 * hh + c // 2, lo:lo + CH], Rs[lo:lo + CH, hh, :],
                                      start=True, stop=True)
                    m.then_inc(u_mm, 1)
                    next(fill, None)
                    pe.wait_ge(u_ready, 4 * n + c + 1)
                    if c < NC - 1:
                        for hh in range(2):
                            m = pe.matmul(ps[5][0:HD, hh * HD:(hh + 1) * HD], BKT[:, c, hh, :], UV[:, c, hh, :],
                                          start=True, stop=True)
                        m.then_inc(ds_mm, 1)
                    for hh in range(2):
                        dst = ps[6][hh * HD:(hh + 1) * HD, c * CH:(c + 1) * CH]
                        pe.matmul(dst, UV[:, c, hh, :], GR[:, c, hh, :], start=True, stop=False)
                        m = pe.matmul(dst, SV[0:HD, c, hh, :], RH[0:HD, c, hh, :], start=False, stop=True)
                    if c < NC - 1:
                        next(fill, None)
                m.then_inc(y_mm, 1)
                for _ in fill:
                    pass
                mean_of(n)
                if last:
                    variance_of(n)
                    return
                grams(n + 1, tail=lambda: variance_of(n))
                if dense is not None:
                    for _ in rwkv_dense(*dense, (3,)):
                        pass

            pe.wait_ge(lora_free, 2)
            pe.wait_ge(lora_ready, 1)
            for _ in rwkv_dense(0, 0, range(4)):
                pass
            low_rank(0, 0)
            key_norm(0)
            pe.wait_ge(zs_ready, 1)
            for _ in rwkv_dense(0, 1, (0, 1, 2)):
                pass
            grams(0)
            for _ in rwkv_dense(0, 1, (3,)):
                pass
            rwkv_pair(0, 0, (1, 0))
            with pe.Fori(0, PAIRS // 2 - 1) as i:
                rwkv_pair(2 * i + 1, 1, (i + 1, 1))
                rwkv_pair(2 * i + 2, 0, (i + 2, 0))
            rwkv_pair(PAIRS - 1, 1)
            phase_end(pe)

            for m in range(2, 8):
                pe.wait_ge(ev_lo, m - 1)
                pe.wait_ge(ev_hi, m - 1)
                f_unit(ps[m % 2], U["nsa_q"] + m, hT)
            for n in range(2):
                u = U["nsa_v"] + n
                arrived(pe, u)
                w = ring[:, u % RING, :].rearrange("p (k c) -> p k c", k=4)
                for k in range(4):
                    for b in range(NB):
                        m = pe.matmul(ps[2 + b][:], hT[:, 4 * n + k, b * P:(b + 1) * P], w[:, k, :],
                                      start=n == 0 and k == 0, stop=n == 1 and k == 3)
                m.then_inc(unit_done, 1)
            for w_ in range(2):
                pe.wait_ge(blk_ready, w_ + 1)
                u = U["cmp"] + w_
                arrived(pe, u)
                w = ring[:, u % RING, :].rearrange("p (k c) -> p k c", k=16)
                for k in range(16):
                    m = pe.matmul(ps[4][:, 60 * w_:60 * w_ + 60], w[:, k, :], blk[w_][:, k, :], start=k == 0, stop=k == 15)
                m.then_inc(unit_done, 1)
            pe.wait_ge(hid_ready, 1)
            pe.matmul(ps[5][0:HD, 0:60], cmp_w2[:, 0:HD], xg[:, 0, :], start=True, stop=True)
            for g in range(GROUPS):
                m = pe.matmul(ps[6][0:N_CMP, g * HD:(g + 1) * HD], xg[:, 1, g * N_CMP:(g + 1) * N_CMP],
                              cmp_w2[:, HD:P], start=True, stop=True)
            m.then_inc(kv_mm, 1)
            phase_end(pe)

            dense = mixer_dense()
            for g in range(GROUPS):
                if g >= 1:
                    pe.wait_ge(c_arg, g)
                for b in range(NB):
                    for hh in range(HPG):
                        c = (b * HPG + hh) * N_CMP
                        m = pe.matmul(ps[0][:, c:c + N_CMP], qT[0:HD, HPG * g + hh, b * P:(b + 1) * P],
                                      kcmp[0:HD, g * N_CMP:(g + 1) * N_CMP], start=True, stop=True)
                m.then_inc(c_mm, 1)
                for _ in range(2):
                    next(dense)
                pe.wait_ge(c_exp, g + 1)
                for b in range(NB):
                    m = pe.transpose(ps[1][:, b * P:(b + 1) * P],
                                     cp_[:, b * HPG:(b + 1) * HPG, :].rearrange("p h n -> p (h n)"), ident)
                m.then_inc(c_tr, 1)
                for _ in range(2):
                    next(dense)
                pe.wait_ge(c_pT, g + 1)
                for b in range(NB):
                    m = pe.matmul(ps[2][:, b * S:(b + 1) * S], cpT[:, b, :], Vblk[:, g, :], start=True, stop=True)
                m.then_inc(c_pv, 1)
            phase_end(pe)

            attention([(HD, (lambda lo, hi, g=g, k=(ksT, kwT)[br]: k[0:HD, g, lo:hi]),
                        (lambda kt, g=g, br=br: v_sw.rearrange("p b (w g d) -> p b w g d", w=2, g=GROUPS)[:, kt, br, g, :]))
                       for g in range(GROUPS) for hh in range(HPG) for br in range(2)], NSA0, dense, (2, 1))
            for _ in dense:
                pass
            pe.wait_ge(gb_done, 8)
            transposes(xn)
            phase_end(pe)

            for m in range(4):
                if m >= 2:
                    pe.wait_ge(m_ready, m - 1)
                f_unit(ps[m % 2], U["branch_b"] + m, oT)
            pe.wait_ge(m_ready, 4)
            t_rows(U["w_out"], mT, 4)
            phase_end(pe)
            transposes(xn)
            phase_end(pe)
            ffn_up(U["up0"], 0)
            ffn_down(0)
            phase_end(pe)
            transposes(xn)
            phase_end(pe)

            for m in range(6):
                if m >= 2:
                    pe.wait_ge(e_lo, m - 1)
                    pe.wait_ge(e_hi, m - 1)
                split_f_unit(ps[m % 2], "even", m)
            pe.wait_ge(e_lo, 5)
            pe.wait_ge(e_hi, 5)
            unit_split("even", 6)
            w = [t[:, 0, :].rearrange("p (k c) -> p k c", k=KT) for t in (w_hi, w_lo)]
            h = (h_hi, h_lo)
            split_product(ps[0][:, 0:S], [([t[:, k, 0:P] for t in w], [t[:, k, :] for t in h]) for k in range(KT)])
            for b in range(NB):
                m = split_product(ps[2][:, b * P:(b + 1) * P],
                                  [([t[:, k, b * P:(b + 1) * P] for t in h], [t[:, k, P:2 * P] for t in w])
                                   for k in range(KT)])
            m.then_inc(unit_done, 1)
            for n in range(2):
                unit_split("even", 7 + n)
                w = [t[:, 1 - n, :].rearrange("p (k c) -> p k c", k=4) for t in (w_hi, w_lo)]
                for b in range(NB):
                    m = split_product(ps[4 + b][:], [([t[:, 4 * n + k, b * P:(b + 1) * P] for t in h],
                                                      [t[:, k, :] for t in w]) for k in range(4)],
                                      first=n == 0, last=n == 1)
                m.then_inc(unit_done, 1)
            phase_end(pe)
            with pe.Fori(0, 2) as i:
                attention([(HD, (lambda lo, hi, h=h: ka[0:HD, 4 * i + h, lo:hi]),
                            (lambda kt, h=h: va.rearrange("p b (h d) -> p b h d", d=HD)[:, kt, 4 * i + h, :]))
                           for h in range(4)], SB0 + 4 * i)
            phase_end(pe)
            with pe.Fori(0, 2) as i:
                attention([(HD, (lambda lo, hi: kb[0:HD, i, lo:hi]),
                            (lambda kt: vb.rearrange("p b (h d) -> p b h d", d=HD)[:, kt, i, :]))
                           for h in range(4)], SW0 + 4 * i)
            transposes(xn)
            phase_end(pe)
            split_rows("even_out", 0, (h_hi, h_lo), 4)
            phase_end(pe)
            transposes(xn)
            phase_end(pe)
            ffn_up(U["up1"], 1)
            ffn_down(1)
            phase_end(pe)
            transposes(xn)
            phase_end(pe)

            for m in range(3):
                split_f_unit(ps[m], "mla", m)
            pe.wait_ge(m_sq, 1)
            for k in range(3):
                pe.matmul(ps[4][:, 0:S], ones, csq[:, k, :], start=k == 0, stop=k == 2)
            for k in range(2):
                m = pe.matmul(ps[4][:, S:2 * S], ones, csq[:, 3 + k, :], start=k == 0, stop=k == 1)
            m.then_inc(m_sum, 1)
            pe.wait_ge(m_norm, 1)
            for h in range(H):
                if h >= 2:
                    pe.wait_ge(q_lo, h - 1)
                    pe.wait_ge(q_hi, h - 1)
                u = U["mla_uq"] + h // 4
                arrived(pe, u)
                w = ring[:, u % RING, 0:1536].rearrange("p (k c) -> p k c", k=3)
                for k in range(3):
                    m = pe.matmul(ps[6 + h % 2][:, 0:S], w[:, k, (h % 4) * P:(h % 4 + 1) * P], cq[:, k, :],
                                  start=k == 0, stop=k == 2)
                if h % 4 == 3:
                    m.then_inc(unit_done, 1)
                    pe.drain().then_inc(m_ev, 1)
                else:
                    m.then_inc(m_ev, 1)
            u = U["mla_uk"]
            arrived(pe, u)
            w = ring[:, u % RING, :].rearrange("p (k c) -> p k c", k=2)
            for t in range(8):
                if t >= 2:
                    pe.wait_ge(k_lo, t - 1)
                    pe.wait_ge(k_hi, t - 1)
                for k in range(2):
                    m = pe.matmul(ps[t % 2][:, 0:S], w[:, k, t * P:(t + 1) * P], ckv[:, k, :], start=k == 0, stop=k == 1)
                if t == 7:
                    m.then_inc(unit_done, 1)
                    pe.drain().then_inc(m_ev, 1)
                else:
                    m.then_inc(m_ev, 1)
            u = U["mla_uv"]
            arrived(pe, u)
            w = ring[:, u % RING, :].rearrange("p (k c) -> p k c", k=2)
            for b in range(NB):
                for hf in range(2):
                    for k in range(2):
                        m = pe.matmul(ps[2 + 2 * b + hf][:], ckv[:, k, b * P:(b + 1) * P],
                                      w[:, k, hf * 512:(hf + 1) * 512], start=k == 0, stop=k == 1)
            m.then_inc(unit_done, 1)
            phase_end(pe)
            with pe.Fori(0, 4) as i:
                attention([(HD + ROPE, (lambda lo, hi, h=h: kmT[0:HD + ROPE, 4 * i + h, lo:hi]),
                            (lambda kt, h=h: vm.rearrange("p b (h d) -> p b h d", d=HD)[:, kt, 4 * i + h, :]))
                           for h in range(4)], MLA0 + 4 * i)
            transposes(xn)
            phase_end(pe)
            split_rows("mla_out", 0, (h_hi, h_lo), 4)
            phase_end(pe)
            transposes(xn)
            phase_end(pe)
            ffn_up(U["up2"], 2)
            ffn_down(2)
            phase_end(pe)

        @block.scalar
        def _(act):
            def square_rows(src):
                act.drain()
                for b in range(NB):
                    m = act.activation(xn[:, b, :], src[:, b, :], ACT.Square, accum_out=stat[:, b:b + 1])
                m.then_inc(sq_ready, 1)
                act.drain()
                act.activation(stat[:, 2:4], stat[:, 0:2], ACT.Sqrt, bias=stat[:, 7:8],
                               scale=1.0 / D).then_inc(root_ready, 1)

            def evacuate_even(dst, gain):
                n = n_norm.setdefault("act", 0)
                n_norm["act"] += 1
                for q in (0, 2):
                    act.wait_ge(tr_ready, 4 * n + q + 1)
                    for k in (2 * q, 2 * q + 1):
                        src = ps[4 + q][:, (k % 2) * S:(k % 2 + 1) * S]
                        if gain is None:
                            act.activation(dst[:, k, :], src, ACT.Copy)
                        else:
                            act.activation(dst[:, k, :], src, ACT.Copy, scale=gain[:, k:k + 1])

            def take_mixer(n):
                act.wait_ge(unit_done, U["gate_b"] + n + 1)
                dst, f = (gbT, ACT.Tanh) if n < 4 else (mT, ACT.Copy)
                act.activation(dst[:, 2 * (n % 4):2 * (n % 4) + 2, :].rearrange("p a t -> p (a t)"), ps[6 + n % 2][:], f,
                               scale=0.5 if n < 4 else 1.0).then_inc(gb_done, 1)

            def exponentials(N, n0, before=lambda s: None):
                for s in range(N):
                    before(s)
                    act.wait_ge(max_ready, n0 + s + 1)
                    act.activation(sc[:, s % 2, 0:P], sc[:, s % 2, 0:P], ACT.Exp, bias=mx[:, s % 2, 2:3],
                                   accum_out=mx[:, s % 2, 4:5])
                    act.activation(sc[:, s % 2, P:KEYS], sc[:, s % 2, P:KEYS], ACT.Exp, bias=mx[:, s % 2, 3:4],
                                   accum_out=mx[:, s % 2, 5:6]).then_inc(p_ready, 1)

            def square_post(n_post):
                for q in range(4):
                    m = act.activation(xn[:, q // 2, (q % 2) * 512:(q % 2 + 1) * 512], ps[4 + q][:], ACT.Square,
                                       accum_out=mx[:, 0, q:q + 1])
                m.then_inc(sq2_ready, 1)
                act.wait_ge(sum_ready, n_post + 1)
                act.activation(stat[:, 2:4], stat[:, 0:2], ACT.Sqrt, bias=stat[:, 7:8],
                               scale=1.0 / D).then_inc(root2_ready, 1)

            def split_input(gain):
                n = n_norm.setdefault("act", 0)
                n_norm["act"] += 1
                for q in range(4):
                    act.wait_ge(tr_ready, 4 * n + q + 1)
                    for k in (2 * q, 2 * q + 1):
                        m = act.activation(h_hi[:, k, :], ps[4 + q][:, (k % 2) * S:(k % 2 + 1) * S],
                                           ACT.Copy, scale=1.0 if gain is None else gain[:, k:k + 1])
                    m.then_inc(h_hi_ready, 1)

            def split_unit(u0, m, i=0):
                arrived(act, u0 + m, i)
                act.activation(w_hi[:, m % 2, WH:], ring[:, (u0 + m) % RING, WH:],
                               ACT.Copy).then_inc(w_hi_p, 1)
                act.activation(w_hi[:, m % 2, 0:WH], ring[:, (u0 + m) % RING, 0:WH],
                               ACT.Copy).then_inc(w_hi_d, 1)

            def prepare_out(u0):
                split_unit(u0, 0)
                split_unit(u0, 1)
                split_input(None)

            def rest_of(u0, n):
                for m in range(n - 2):
                    act.wait_ge(unit_done, u0 + m + 1)
                    split_unit(u0, m + 2)

            def ffn_units(u0, body, tail=None):
                def step(j, i):
                    act.wait_ge(unit_done, u0 + 4 * i + j + 1)
                    split_unit(u0, j + 2, i)
                    body(j, i)

                in_steps(act, step, tail)
                for m in range(FT, FU - 2):
                    act.wait_ge(unit_done, u0 + m + 1)
                    split_unit(u0, m + 2)

            def ffn_conv(u0):
                def tanh(j, i):
                    act.wait_ge(ff_conv, 4 * i + j + 1)
                    act.activation(ut[j % 2], uc[j % 2][:, 0, :], ACT.Tanh, scale=0.5).then_inc(ff_tanh, 1)

                def body(j, i):
                    act.wait_ge(ff_act, 4 + 4 * i + j - 1)
                    act.activation(uz[j % 2][:, :, 2:S + 2], ps[j % 4][:].rearrange("p (a t) -> p a t", a=2),
                                   ACT.Copy).then_inc(ff_free, 1)
                    act.drain()
                    for a in range(2):
                        p = conv_p[:, 4 * i + j, 4 * a:4 * a + 4]
                        ins = act.activation(uc[j % 2][:, a, :], uz[j % 2][:, a, 0:S], ACT.Identity,
                                             scale=p[:, 0:1], bias=p[:, 3:4])
                    ins.then_inc(ff_copied, 1)

                ffn_units(u0, body, tail=tanh)

            def ffn_tanh(u0, n_ffn):
                def body(j, i):
                    act.wait_ge(ff_act, 4 + n_ffn * FT + 4 * i + j - 1)
                    act.activation(ut[j % 2], ps[j % 4][:, 0:S], ACT.Tanh, scale=0.5).then_inc(ff_tanh, 1)

                ffn_units(u0, body)

            act.wait_ge(params_in, 48)
            act.wait_ge(eps_ready, 1)
            act.drain().then_inc(p_ready, HEAD0)
            act.drain().then_inc(ff_free, 4)
            square_rows(x)
            evacuate_even(hT, small("g_mix"))
            phase_end(act)

            act.wait_ge(unit_done, U["lora"] + 1)
            act.activation(lz[:, 0:2, 1:S + 1], ps[0][:].rearrange("p (a t) -> p a t", a=2),
                           ACT.Copy).then_inc(lora_free, 1)
            act.wait_ge(lora_mm, 1)
            act.activation(lz[0:32, 2, 1:S + 1], ps[1][0:32, 0:S], ACT.Copy).then_inc(lora_free, 1)
            act.activation(gates.rearrange("p b c -> p (b c)"), ps[2][:, 0:96], ACT.Tanh,
                           scale=0.5).then_inc(gates_tanh, 1)
            act.wait_ge(lora_mix, 1)
            act.activation(lora[0:64, 0, :], lora[0:64, 0, :], ACT.Tanh)
            act.activation(lora[:, 1:3, :], lora[:, 1:3, :], ACT.Tanh, scale=0.5).then_inc(lora_tanh, 1)
            act.wait_ge(lora_ready, 1)

            def take_dense(m):
                act.wait_ge(mixed, m + 1)
                act.wait_ge(unit_done, U["rwkv"] + 2 * m + 1)
                act.activation(zs[:, 0:2, 1:S + 1], ps[0][:].rearrange("p (a t) -> p a t", a=2), ACT.Copy)
                act.wait_ge(unit_done, U["rwkv"] + 2 * m + 2)
                act.activation(zs[:, 2, 1:S + 1], ps[1][:, 0:S], ACT.Copy)
                act.activation(gaT[:, m, :], ps[1][:, S:2 * S], ACT.Tanh, scale=0.5).then_inc(zs_ready, 1)

            def low_rank(m, j):
                act.wait_ge(half_ready, m + 1)
                act.wait_ge(lora_up, m + 1)
                act.activation(th_w, ps[2][:, 0:S], ACT.Tanh, scale=0.5, bias=half[:, j, 0:1])
                act.activation(th_a, ps[3][:, S:2 * S], ACT.Tanh, scale=0.5, bias=half[:, j, 1:2]).then_inc(lora_out, 1)

            def output_gate(m, j):
                act.wait_ge(pair_done, m)
                act.activation(g_f[:, j, :], ps[2][:, S:2 * S], ACT.Copy).then_inc(gate_out, 1)

            def decays(m):
                act.wait_ge(cum_ready, m + 1)
                act.activation(e1, cum, ACT.Exp)
                act.activation(e2, cum, ACT.Exp, scale=-1.0)
                act.activation(e3, cum1, ACT.Exp).then_inc(exp_ready, 1)

            def key_norm(m):
                act.wait_ge(knorm, m + 1)
                act.activation(nrm, ps[3][:, 0:S], ACT.Sqrt).then_inc(nrm_ready, 1)

            def variance_root(n):
                act.wait_ge(var_mm, n + 1)
                act.activation(vroot, ps[3][:, S:2 * S], ACT.Sqrt, bias=stat[:, 6:7],
                               scale=1.0 / HD).then_inc(rstd_root, 1)

            def shift_rows(m, before=None):
                act.wait_ge(bkar_ready, m + 1)
                for hh in range(2):
                    rows = slice(hh * HD, (hh + 1) * HD)
                    act.activation(LR[0:HD, :, hh, :], AR[rows, :, 0, :], ACT.Copy)
                    act.activation(RH[0:HD, :, hh, :], AR[rows, :, 1, :], ACT.Copy)
                    act.activation(Wc[0:HD, :, hh], e1[rows, CH - 1:S:CH], ACT.Copy)
                if before is not None:
                    variance_root(before)
                act.wait_ge(gram, m + 1)
                act.activation(BKT.rearrange("p c h d -> p (c h d)"), ps[7][:], ACT.Copy)
                v_tm = ps[6][CH:P, :].rearrange("p (c h d) -> p c h d", c=NC, h=2)
                act.activation(UV[CH:P, :, :, :], v_tm, ACT.Copy)
                act.activation(SV[CH:P, :, :, :], v_tm, ACT.Copy).then_inc(shift_ready, 1)

            def rwkv_pair(n, j, last=False):
                if not last:
                    take_dense(n + 1)
                act.wait_ge(q0_mm, n + 1)
                act.activation(Qp[1].rearrange("p a b -> p (a b)"), ps[4][:], ACT.Copy).then_inc(q0_ready, 1)
                for lvl in range(5):
                    act.wait_ge(pow_mm, 10 * n + 2 * lvl + 1)
                    act.activation(Pp[lvl % 2].rearrange("p a b -> p (a b)"), ps[4][:], ACT.Copy).then_inc(pq_ready, 1)
                    act.wait_ge(pow_mm, 10 * n + 2 * lvl + 2)
                    act.activation(Qp[lvl % 2].rearrange("p a b -> p (a b)"), ps[5][:],
                                   ACT.Copy).then_inc(pq_ready, 1)
                    if not last:
                        if lvl == 0:
                            low_rank(n + 1, 1 - j)
                        if lvl == 2:
                            decays(n + 1)
                        if lvl == 3:
                            key_norm(n + 1)
                        if lvl == 4:
                            output_gate(n + 1, 1 - j)
                for c in range(NC):
                    act.wait_ge(u_mm, 4 * n + c + 1)
                    act.activation(UV[0:CH, c, :, :].rearrange("p h d -> p (h d)"), ps[4][0:CH, 0:P],
                                   ACT.Copy).then_inc(u_ready, 1)
                if last:
                    variance_root(n)
                    return
                act.wait_ge(y_mm, n + 1)
                shift_rows(n + 1, before=n)

            take_dense(0)
            low_rank(0, 0)
            act.activation(g_f[:, 0, :], ps[2][:, S:2 * S], ACT.Copy).then_inc(gate_out, 1)
            decays(0)
            key_norm(0)
            shift_rows(0)
            rwkv_pair(0, 0)
            with act.Fori(0, PAIRS // 2 - 1) as i:
                rwkv_pair(2 * i + 1, 1)
                rwkv_pair(2 * i + 2, 0)
            rwkv_pair(PAIRS - 1, 1, last=True)
            phase_end(act)

            for m in range(8):
                act.wait_ge(unit_done, U["nsa_q"] + m + 1)
                src = ps[m % 2][0:HD, :].rearrange("p (a t) -> p a t", a=2)
                if m < 4:
                    act.activation(qT[0:HD, 4 * m:4 * m + 4:2, :], src, ACT.Copy, scale=SCALE).then_inc(ev_lo, 1)
                else:
                    act.activation((kcT, vcT, ksT, kwT)[m - 4][0:HD, 0:4:2, :], src, ACT.Copy).then_inc(ev_lo, 1)
            act.wait_ge(unit_done, U["nsa_v"] + 2)
            act.activation(v_sw[:, 0, :], ps[2][:], ACT.Copy)
            act.wait_ge(gelu_arg, 1)
            act.activation(xg[:], xg[:], ACT.Tanh, scale=math.sqrt(2 / math.pi)).then_inc(gelu_tanh, 1)
            phase_end(act)
            for g in range(GROUPS):
                act.wait_ge(c_arg, g + 1)
                act.activation(cp_[:, :, 0:N_CMP], cs[:], ACT.Exp).then_inc(c_exp, 1)
            phase_end(act)
            due = {0: [0], 1: [1]}
            for n in range(2, 8):
                due.setdefault(-(-16 * (n - 1) // 3) + 1, []).append(n)
            exponentials(4 * HPG * 2, NSA0, lambda s: [take_mixer(n) for n in due.get(s, ())])
            for s in sorted(due):
                if s >= 4 * HPG * 2:
                    for n in due[s]:
                        take_mixer(n)
            evacuate_even(oT, None)
            phase_end(act)
            act.wait_ge(unit_done, U["w_out"] + 4)
            square_post(0)
            phase_end(act)
            square_rows(x)
            split_input(small("g_ffn"))
            phase_end(act)
            ffn_conv(U["up0"])
            act.wait_ge(unit_done, U["down0"] + FT // 2)
            square_post(1)
            phase_end(act)
            square_rows(x)
            split_input(small("g_attn2")[:, 0:KT])
            phase_end(act)
            for m in range(7):
                act.wait_ge(unit_done, U["even_f"] + m + 1)
                split_unit(U["even_f"], m + 2)
                src = ps[m % 2][0:HD, :].rearrange("p (a t) -> p a t", a=2)
                dst = (qa, qa, ka, ka, qb, qb, kb)[m]
                if m < 6:
                    act.activation(dst[0:HD, 4 * (m % 2):4 * (m % 2) + 4:2, :], src, ACT.Copy,
                                   scale=1.0 if m in (2, 3) else SCALE).then_inc(e_lo, 1)
                else:
                    act.activation(kb[0:HD, 0, :], src[:, 0, :], ACT.Copy).then_inc(e_lo, 1)
            act.activation(vb.rearrange("p b c -> p (b c)"), ps[2][:, 0:S], ACT.Copy)
            act.wait_ge(unit_done, U["even_v"] + 2)
            act.activation(va[:, 0, :], ps[4][:], ACT.Copy)
            phase_end(act)
            with act.Fori(0, 2) as i:
                for s in range(5):
                    if s < 4:
                        t0 = sbt[s % 2][0]
                        act.wait_ge(s_mm, SB0 + 4 * i + s + 1)
                        act.wait_ge(max_ready, SB0 + 4 * i + s - 1)
                        act.activation(t0, ps[s % 2][:, 0:KEYS], ACT.Abs)
                        act.drain()
                        act.activation(t0, t0, ACT.Exp, scale=-1.0)
                        act.drain()
                        act.activation(t0, t0, ACT.Ln, bias=1.0).then_inc(pre_ready, 1)
                    if s > 0:
                        act.wait_ge(max_ready, SB0 + 4 * i + s)
                        act.activation(sc[:, (s - 1) % 2, :], sc[:, (s - 1) % 2, :], ACT.Exp).then_inc(p_ready, 1)
            phase_end(act)
            def sink_exponentials(n0):
                for s in range(4):
                    act.wait_ge(max_ready, n0 + s + 1)
                    act.activation(sc[:, s % 2, 0:P], sc[:, s % 2, 0:P], ACT.Exp, bias=mx[:, s % 2, 2:3],
                                   accum_out=mx[:, s % 2, 4:5])
                    act.activation(sc[:, s % 2, P:KEYS], sc[:, s % 2, P:KEYS], ACT.Exp, bias=mx[:, s % 2, 3:4],
                                   accum_out=mx[:, s % 2, 5:6])
                    act.activation(mx[:, s % 2, 6:8], mx[:, s % 2, 2:4], ACT.Exp,
                                   bias=sink_st[:, s % 2:s % 2 + 1]).then_inc(p_ready, 1)

            with act.Fori(0, 2) as i:
                sink_exponentials(SW0 + 4 * i)
            prepare_out(U["even_out"])
            phase_end(act)
            rest_of(U["even_out"], 4)
            phase_end(act)
            square_rows(x)
            split_input(small("g_ffn2")[:, 0:KT])
            phase_end(act)
            ffn_tanh(U["up1"], 1)
            phase_end(act)
            square_rows(x)
            split_input(small("g_attn2")[:, KT:2 * KT])
            phase_end(act)
            for m in range(3):
                act.wait_ge(unit_done, U["mla_down"] + m + 1)
                if m == 0:
                    split_unit(U["mla_down"], 2)
                for t in range(2):
                    k = 2 * m + t
                    if k == 5:
                        continue
                    dst = cq[:, k, :] if k < 3 else ckv[:, k - 3, :]
                    act.activation(dst, ps[m][:, t * S:(t + 1) * S], ACT.Copy)
                    e_ = act.activation(csq[:, k, :], ps[m][:, t * S:(t + 1) * S], ACT.Square)
            e_.then_inc(m_sq, 1)
            act.wait_ge(m_sum, 1)
            act.activation(rstd_f[:, 0, :], ps[4][:, 0:S], ACT.Sqrt, bias=stat[:, 7:8], scale=1.0 / Q_RANK)
            act.activation(rstd_f[:, 1, :], ps[4][:, S:2 * S], ACT.Sqrt, bias=stat[:, 7:8],
                           scale=1.0 / KV_RANK).then_inc(m_root, 1)
            act.wait_ge(rope_in, 1)
            act.activation(rope_t, ang, ACT.Sin).then_inc(rope_ready, 1)
            for h in range(H):
                act.wait_ge(m_ev, h + 1)
                act.activation(qm[0:HD, h, :], ps[6 + h % 2][0:HD, 0:S], ACT.Copy, scale=MLA_SCALE).then_inc(q_lo, 1)
            for t in range(8):
                act.wait_ge(m_ev, H + t + 1)
                act.activation(kmT[0:HD, 2 * t, :], ps[t % 2][0:HD, 0:S], ACT.Copy).then_inc(k_lo, 1)
            act.wait_ge(unit_done, U["mla_uv"] + 1)
            for hf in range(2):
                act.activation(vm[:, 0, hf * 512:(hf + 1) * 512], ps[2 + hf][:], ACT.Copy)
            phase_end(act)
            with act.Fori(0, 4) as i:
                exponentials(4, MLA0 + 4 * i)
            prepare_out(U["mla_out"])
            phase_end(act)
            rest_of(U["mla_out"], 4)
            phase_end(act)
            square_rows(x)
            split_input(small("g_ffn2")[:, KT:2 * KT])
            phase_end(act)
            ffn_tanh(U["up2"], 2)
            phase_end(act)
            square_rows(x)

        @block.vector
        def _(dve):
            def normalise(src):
                n = n_norm.setdefault("dve", 0)
                n_norm["dve"] += 1
                r = n_norm['root'] = n_norm.get('root', 0) + 1
                dve.wait_ge(root_ready, r)
                dve.reciprocal(stat[:, 4:6], stat[:, 2:4])
                dve.drain()
                for b in range(NB):
                    m = dve.tensor_scalar(xn[:, b, :], src[:, b, :], stat[:, 4 + b:5 + b], None, ALU.mult)
                m.then_inc(xn_ready, 1)

            def evacuate_odd(dst, gain):
                n = n_norm["dve"] - 1
                for q in (1, 3):
                    dve.wait_ge(tr_ready, 4 * n + q + 1)
                    for k in (2 * q, 2 * q + 1):
                        src = ps[4 + q][:, (k % 2) * S:(k % 2 + 1) * S]
                        if gain is None:
                            dve.tensor_copy(dst[:, k, :], src)
                        else:
                            dve.tensor_scalar(dst[:, k, :], src, gain[:, k:k + 1], None, ALU.mult)

            def attention(N, n0, finish, sink=None, middle=None):
                for s in range(N + 2):
                    if s < N:
                        j = s % 2
                        dve.wait_ge(s_mm, n0 + s + 1)
                        if middle is not None:
                            middle(s, n0)
                        else:
                            dve.wait_ge(b_staged, n0 + s + 1)
                            dve.sem_inc(apart, 1)
                            for a, b in ((0, P), (P, KEYS)):
                                dve.tensor_tensor_reduce(out=sc[:, j, a:b], in0=ps[j][:, a:b], in1=b_st[:, j, a:b],
                                                         scale=1.0, scalar=-3e38, op0=ALU.add, op1=ALU.max,
                                                         accum_out=mx[:, j, a // P:a // P + 1])
                            dve.drain()
                            if sink is not None:
                                dve.tensor_scalar(mx[:, j, 0:2], mx[:, j, 0:2], sink(s), None, ALU.max)
                                dve.drain()
                            dve.tensor_scalar(mx[:, j, 2:4], mx[:, j, 0:2], -1.0, None, ALU.mult).then_inc(max_ready, 1)
                    if 1 <= s <= N:
                        t = s - 1
                        dve.wait_ge(t_mm, n0 + t + 1)
                        dve.tensor_copy(pT[:, t % 2, :], ps[2 + t % 2][:, 0:KEYS]).then_inc(pt_ready, 1)
                        if middle is None:
                            dve.drain()
                            sums = mx[:, t % 2, 4:6]
                            if sink is not None:
                                dve.tensor_tensor(mx2[:, t % 2, 0:2], sums, mx[:, t % 2, 6:8], ALU.add)
                                dve.drain()
                                sums = mx2[:, t % 2, 0:2]
                            dve.reciprocal(mx2[:, t % 2, 0:2], sums)
                    if s >= 2:
                        t = s - 2
                        dve.drain()
                        dve.wait_ge(o_mm, n0 + t + 1)
                        finish(t, ps[4 + t % 2])
                dve.drain()

            def post_norm(n_post, n_sq):
                dve.wait_ge(sq2_ready, n_post + 1)
                dve.tensor_tensor(stat[:, 0:2], mx[:, 0, 0:4:2], mx[:, 0, 1:4:2], ALU.add).then_inc(sum_ready, 1)
                dve.wait_ge(root2_ready, n_post + 1)
                dve.reciprocal(stat[:, 4:6], stat[:, 2:4])
                dve.wait_ge(row_in, 16 * (n_post + 1))
                dve.drain()
                for q in range(4):
                    cols = slice((q % 2) * 512, (q % 2 + 1) * 512)
                    dve.scalar_tensor_tensor(xn[:, q // 2, cols], ps[4 + q][:], stat[:, 4 + q // 2:5 + q // 2],
                                             grow[:, cols], ALU.mult, ALU.mult)
                dve.drain()
                dve.tensor_tensor(x[:], x[:], xn[:], ALU.add)

            def add_rows():
                for q in range(4):
                    cols = slice((q % 2) * 512, (q % 2 + 1) * 512)
                    dve.tensor_tensor(x[:, q // 2, cols], ps[4 + q][:], x[:, q // 2, cols], ALU.add)

            def split_input(gain):
                n = n_norm["dve_split"] = n_norm.get("dve_split", 0) + 1
                for q in range(4):
                    dve.wait_ge(h_hi_ready, 4 * (n - 1) + q + 1)
                    for k in (2 * q, 2 * q + 1):
                        src = ps[4 + q][:, (k % 2) * S:(k % 2 + 1) * S]
                        if gain is None:
                            dve.tensor_tensor(h_lo[:, k, :], src, h_hi[:, k, :].bitcast(F32), ALU.subtract)
                        else:
                            dve.scalar_tensor_tensor(h_lo[:, k, :], src, gain[:, k:k + 1],
                                                     h_hi[:, k, :].bitcast(F32), ALU.mult, ALU.subtract)

            def split_unit(u0, name, m, i=0):
                dve.wait_ge(w_hi_d, SPLIT[name] + 4 * i + m + 1)
                dve.tensor_tensor(w_lo[:, m % 2, 0:WH], ring[:, (u0 + m) % RING, 0:WH],
                                  w_hi[:, m % 2, 0:WH].bitcast(F32), ALU.subtract).then_inc(w_lo_d, 1)

            def first_units(u0):
                for m in range(2):
                    arrived(dve, u0 + m)
                    dve.tensor_copy(w_hi[:, m, WH:], ring[:, (u0 + m) % RING, WH:]).then_inc(w_hi_p, 1)
                    dve.tensor_copy(w_hi[:, m, 0:WH], ring[:, (u0 + m) % RING, 0:WH]).then_inc(w_hi_d, 1)

            def prepare_out(u0, name):
                split_unit(u0, name, 0)
                split_unit(u0, name, 1)
                split_input(None)

            def ffn_units(u0, n_ffn, body, tail=None):
                def step(j, i):
                    split_unit(u0, f"ffn{n_ffn}", j + 2, i)
                    body(j, i)

                in_steps(dve, step, tail)
                for m in range(FT, FU - 2):
                    split_unit(u0, f"ffn{n_ffn}", m + 2)

            def gated(n_ffn, j, i, g, v):
                m = n_ffn * FT + 4 * i + j
                dve.drain()
                dve.wait_ge(ff_tanh, m + 1)
                dve.scalar_tensor_tensor(ut[j % 2], ut[j % 2], 1.0, g, ALU.add, ALU.mult)
                dve.drain()
                dve.wait_ge(act_split, 2 + m - 1)
                dve.sem_inc(apart, 1)
                dve.scalar_tensor_tensor(act_f[:, j % 2, :], ut[j % 2], 0.5, v, ALU.mult, ALU.mult).then_inc(ff_act, 1)

            def ffn_conv(u0):
                def body(j, i):
                    m = 4 * i + j
                    dve.drain()
                    dve.wait_ge(ff_copied, m + 1)
                    for t in (1, 2):
                        if t == 2:
                            dve.drain()
                        for a in range(2):
                            z, c = uz[j % 2][:, a, :], uc[j % 2][:, a, :]
                            ins = dve.scalar_tensor_tensor(c, z[:, t:S + t], conv_p[:, m, 4 * a + t:4 * a + t + 1], c,
                                                           ALU.mult, ALU.add)
                    ins.then_inc(ff_conv, 1)

                ffn_units(u0, 0, body, tail=lambda j, i: gated(0, j, i, uc[j % 2][:, 0, :], uc[j % 2][:, 1, :]))

            def ffn_act(u0, n_ffn):
                ffn_units(u0, n_ffn, lambda j, i: gated(n_ffn, j, i, ps[j % 4][:, 0:S], ps[j % 4][:, S:2 * S]))

            dve.drain().then_inc(max_ready, HEAD0)
            dve.drain().then_inc(pt_ready, HEAD0)
            dve.drain().then_inc(ff_act, 4)
            dve.memset(stat[:, 6:7], 64e-5)
            dve.memset(stat[:, 7:8], 1e-6).then_inc(eps_ready, 1)
            dve.drain().then_inc(pair_done, 1)
            dve.drain().then_inc(mixed, 1)
            dve.memset(lz, 0.0)
            dve.memset(zs, 0.0)
            dve.memset(v_pad, 0.0)
            dve.memset(P0, 0.0)
            dve.wait_ge(params_in, 48)
            normalise(x)
            evacuate_odd(hT, small("g_mix"))
            phase_end(dve)

            dve.wait_ge(lora_free, 2)
            dve.tensor_tensor(lora, lz[:, :, 0:S], lz[:, :, 1:S + 1], ALU.subtract)
            dve.drain()
            for t in range(3):
                m = dve.scalar_tensor_tensor(lora[:, t, :], lora[:, t, :], small("mu_lora")[:, t:t + 1],
                                             lz[:, t, 1:S + 1], ALU.mult, ALU.add)
            m.then_inc(lora_mix, 1)
            dve.wait_ge(gates_tanh, 1)
            dve.tensor_scalar(gates[:], gates[:], 0.5, 0.5, ALU.mult, ALU.add)
            dve.wait_ge(lora_tanh, 1)
            dve.tensor_scalar(lora[:, 1:3, :], lora[:, 1:3, :], 0.5, 0.5, ALU.mult, ALU.add)
            dve.memset(SV[0:HD, 0, :, :], 0.0)
            dve.drain().then_inc(lora_ready, 1)

            def chunks(a):
                return a.rearrange("p (c t) -> p c t", c=NC)

            def front(m, j):
                def col(c):
                    return ast[:, j, c:c + 1]

                dve.wait_ge(staged, m + 1)
                dve.wait_ge(zs_ready, m + 1)
                dve.tensor_tensor(dz, zs[:, :, 0:S], zs[:, :, 1:S + 1], ALU.subtract)
                dve.drain()
                for t, (dst, mu) in enumerate(((r_f, MU_R), (k_f, MU_K), (v_pad[:, CH:CH + S], MU_V))):
                    ins = dve.scalar_tensor_tensor(dst, dz[:, t, :], col(mu), zs[:, t, 1:S + 1], ALU.mult, ALU.add)
                ins.then_inc(mixed, 1)
                dve.drain()
                dve.tensor_scalar(kk, k_f, col(K_K), None, ALU.mult)
                dve.drain()
                dve.tensor_tensor(kk2, kk, kk, ALU.mult).then_inc(kk2_ready, 1)
                yield
                dve.drain()
                dve.wait_ge(lora_out, m + 1)
                dve.tensor_scalar(ld, th_w, -0.5 * C_DECAY, -0.5 * C_DECAY, ALU.mult, ALU.add)
                dve.tensor_scalar(th_a, th_a, 0.5, 0.5, ALU.mult, ALU.add)
                dve.drain()
                dve.tensor_tensor_scan(cum, chunk_keep, ld, 0.0, ALU.mult, ALU.add)
                dve.tensor_scalar(km, th_a, 1.0, col(K_A), ALU.subtract, ALU.mult)
                dve.drain()
                dve.tensor_tensor(cum1, cum, ld, ALU.subtract).then_inc(cum_ready, 1)
                dve.scalar_tensor_tensor(km, km, 1.0, k_f, ALU.add, ALU.mult)
                dve.drain()
                dve.scalar_tensor_tensor(rk, r_f, col(R_K), km, ALU.mult, ALU.mult)
                yield
                dve.drain()
                dve.wait_ge(exp_ready, m + 1)
                dve.tensor_tensor(BK[:, :, 1, :], chunks(km), chunks(e2), ALU.mult)
                dve.tensor_tensor(AR[:, :, 1, :], chunks(r_f), chunks(e1), ALU.mult)
                yield
                dve.drain()
                dve.wait_ge(nrm_ready, m + 1)
                dve.tensor_scalar(nrm, nrm, 1e-12, None, ALU.max)
                dve.drain()
                dve.reciprocal(nrm, nrm)
                dve.drain()
                dve.tensor_tensor(kk, kk, nrm, ALU.mult)
                dve.drain()
                dve.scalar_tensor_tensor(AR[:, :, 0, :], chunks(kk), -1.0, chunks(e3), ALU.mult, ALU.mult)
                dve.tensor_tensor(kk2, kk, th_a, ALU.mult)
                dve.drain()
                dve.tensor_tensor(BK[:, :, 0, :], chunks(kk2), chunks(e2), ALU.mult).then_inc(bkar_ready, 1)

            def masks(m, j):
                dve.wait_ge(shift_ready, m + 1)
                for hh in range(2):
                    G = ps[4 + hh][:].rearrange("p (c w t) -> p c w t", c=NC, w=2)
                    keep = tri[:, 0:CH].unsqueeze(1)
                    keep_r = tri[:, CH:P].unsqueeze(1)
                    dve.tensor_tensor(GR[:, :, hh, :], G[:, :, 1, :], keep_r.broadcast_to((P, NC, CH)), ALU.mult)
                    dve.tensor_tensor(LR[CH:P, :, hh, :], G[CH:P, :, 0, :],
                                      keep[CH:P].broadcast_to((CH, NC, CH)), ALU.mult)
                    k0 = keep[0:CH].broadcast_to((CH, 2, CH))
                    dve.tensor_tensor(P0[0:CH, 2 * hh:2 * hh + 2, 0:CH], G[0:CH, 0:NC:2, 0, :], k0, ALU.mult)
                    dve.tensor_tensor(P0[CH:P, 2 * hh:2 * hh + 2, CH:P], G[0:CH, 1:NC:2, 0, :], k0, ALU.mult)
                dve.drain()
                dve.tensor_tensor(Zp[1], P0, ident.unsqueeze(1).broadcast_to((P, 4, P)), ALU.add).then_inc(p0_ready, 1)
                dve.tensor_tensor(bonus[:, j, :], ps[2][:, 0:S], v_pad[:, CH:CH + S], ALU.mult).then_inc(bonus_ready, 1)
                dve.drain()

            def reciprocal_root(n):
                dve.wait_ge(rstd_root, n + 1)
                dve.reciprocal(vrec, vroot).then_inc(vrec_ready, 1)

            def rwkv_pair(n, j, first=False, last=False):
                steps = iter(()) if last else front(n + 1, 1 - j)
                next(steps, None)
                if not first:
                    reciprocal_root(n - 1)
                for lvl in range(1, 6):
                    dve.drain()
                    dve.wait_ge(z_mm, 5 * n + lvl)
                    dve.tensor_tensor(Zp[(lvl + 1) % 2].rearrange("p a b -> p (a b)"), ps[6][:],
                                      Zp[lvl % 2].rearrange("p a b -> p (a b)"), ALU.add).then_inc(z_ready, 1)
                    if lvl in (1, 3, 4):
                        next(steps, None)
                for c in range(NC):
                    lo = (c % 2) * CH
                    dve.wait_ge(r_mm, 4 * n + c + 1)
                    dve.tensor_copy(Rs[lo:lo + CH].rearrange("p h d -> p (h d)"),
                                    ps[7][lo:lo + CH, 0:P]).then_inc(r_ready, 1)
                    if c < NC - 1:
                        for hh in range(2):
                            dve.tensor_scalar(Sw[0:HD, hh, :], SV[0:HD, c, hh, :], Wc[0:HD, c, hh:hh + 1],
                                              None, ALU.mult)
                        dve.drain()
                        dve.wait_ge(ds_mm, 3 * n + c + 1)
                        for hh in range(2):
                            m = dve.scalar_tensor_tensor(SV[0:HD, c + 1, hh, :], ps[5][0:HD, hh * HD:(hh + 1) * HD],
                                                         Wc[0:HD, c, hh:hh + 1], Sw[0:HD, hh, :],
                                                         ALU.mult, ALU.add)
                        m.then_inc(state_ready, 1)
                        dve.drain()
                dve.wait_ge(pair_done, n + 1)
                dve.wait_ge(y_mm, n + 1)
                dve.tensor_copy(y_f, ps[6][:, 0:S]).then_inc(y_ready, 1)
                dve.drain()
                dve.wait_ge(mean_mm, n + 1)
                dve.scalar_tensor_tensor(y_f, ps[3][:, 0:S], -1.0 / HD, y_f, ALU.mult, ALU.add)
                dve.drain()
                dve.tensor_tensor(yq, y_f, y_f, ALU.mult).then_inc(yq_ready, 1)
                for _ in steps:
                    pass
                if last:
                    reciprocal_root(n)
                else:
                    masks(n + 1, 1 - j)

            for _ in front(0, 0):
                pass
            masks(0, 0)
            rwkv_pair(0, 0, first=True)
            with dve.Fori(0, PAIRS // 2 - 1) as i:
                rwkv_pair(2 * i + 1, 1)
                rwkv_pair(2 * i + 2, 0)
            rwkv_pair(PAIRS - 1, 1, last=True)
            phase_end(dve)

            dve.memset(Vblk, 0.0)
            dve.memset(cp_, 0.0)
            for m in range(8):
                dve.wait_ge(unit_done, U["nsa_q"] + m + 1)
                src = ps[m % 2][HD:P, :].rearrange("p (a t) -> p a t", a=2)
                if m < 4:
                    dve.tensor_scalar(qT[0:HD, 4 * m + 1:4 * m + 4:2, :], src, SCALE, None, ALU.mult).then_inc(ev_hi, 1)
                else:
                    dve.tensor_copy((kcT, vcT, ksT, kwT)[m - 4][0:HD, 1:4:2, :], src).then_inc(ev_hi, 1)
            dve.drain()
            dve.wait_ge(ev_lo, 6)
            for w_ in range(2):
                t = (kcT, vcT)[w_][0:HD].rearrange("p g (a l) -> p l g a", l=16)
                for par in range(2):
                    for late in range(2):
                        o = blk[w_][par * HD:(par + 1) * HD, 8 * late:8 * late + 8, :].rearrange(
                            "p l (g a) -> p l g a", g=GROUPS)
                        pos = cmp_pos[0:HD, w_, 16 * late + par:16 * late + 16:2].unsqueeze(2)
                        for lp in range(8):
                            m = dve.tensor_scalar(o[:, lp, :, :], t[:, par + 2 * lp, :, late:late + N_CMP],
                                                  pos[:, lp, 0:1], None, ALU.add)
                m.then_inc(blk_ready, 1)
            dve.wait_ge(unit_done, U["nsa_v"] + 2)
            dve.tensor_copy(v_sw[:, 1, :], ps[3][:])
            dve.wait_ge(unit_done, U["cmp"] + 2)
            hx = xg.rearrange("p a b -> p (a b)")
            hb = blk[0].rearrange("p a b -> p (a b)")[:, 0:120]
            dve.tensor_copy(hb, ps[4][:, 0:120])
            dve.drain()
            dve.tensor_tensor(hx, hb, hb, ALU.mult)
            dve.drain()
            dve.tensor_scalar(hx, hx, 0.044715, 1.0, ALU.mult, ALU.add)
            dve.drain()
            dve.tensor_tensor(hx, hx, hb, ALU.mult).then_inc(gelu_arg, 1)
            dve.wait_ge(gelu_tanh, 1)
            dve.scalar_tensor_tensor(hx, hx, 1.0, hb, ALU.add, ALU.mult)
            dve.drain()
            dve.tensor_scalar(hx, hx, 0.5, None, ALU.mult).then_inc(hid_ready, 1)
            dve.wait_ge(kv_mm, 1)
            dve.tensor_copy(kcmp[0:HD, :], ps[5][0:HD, 0:60])
            for hh in range(HPG):
                dve.tensor_copy(Vblk[32 * hh:32 * hh + N_CMP, :, hh * HD:(hh + 1) * HD],
                                ps[6][0:N_CMP, 0:S].rearrange("p (g d) -> p g d", g=GROUPS))
            phase_end(dve)

            bias = const("cmpbias").rearrange("p (g h n) -> p g h n", g=GROUPS, n=N_CMP)
            for g in range(GROUPS):
                dve.wait_ge(c_mm, g + 1)
                dve.tensor_tensor(cs, ps[0][:, 0:8 * N_CMP].rearrange("p (h n) -> p h n", n=N_CMP), bias[:, g],
                                  ALU.add)
                dve.drain()
                dve.tensor_reduce(cst8[:, 0, :], cs, AX, ALU.max)
                dve.drain()
                dve.tensor_scalar(cst8[:, 0, :], cst8[:, 0, :], -1e25, None, ALU.max)
                dve.drain()
                dve.tensor_tensor(cs, cs, cst8[:, 0, :].unsqueeze(2).broadcast_to((P, 8, N_CMP)),
                                  ALU.subtract).then_inc(c_arg, 1)
                dve.wait_ge(c_exp, g + 1)
                dve.tensor_reduce(cst8[:, 1, :], cp_[:, :, 0:N_CMP], AX, ALU.add)
                dve.drain()
                dve.tensor_scalar(cst8[:, 1, :], cst8[:, 1, :], 1e-30, None, ALU.max)
                dve.drain()
                dve.reciprocal(cst8[:, 2, :], cst8[:, 1, :])
                dve.drain()
                gate = gates[:].rearrange("p b (g h w) -> p b g h w", g=GROUPS, w=3)[:, :, g, :, 0]
                dve.tensor_tensor(cst8[:, 3, :].rearrange("p (b h) -> p b h", b=NB),
                                  cst8[:, 2, :].rearrange("p (b h) -> p b h", b=NB), gate, ALU.mult)
                dve.wait_ge(c_tr, g + 1)
                dve.tensor_copy(cpT.rearrange("p b t -> p (b t)"), ps[1][:, 0:S]).then_inc(c_pT, 1)
                dve.wait_ge(c_pv, g + 1)
                dve.drain()
                for b in range(NB):
                    dve.tensor_tensor(
                        xn[:, b, g * S:(g + 1) * S].rearrange("p (h d) -> p h d", d=HD),
                        ps[2][:, b * S:(b + 1) * S].rearrange("p (h d) -> p h d", d=HD),
                        cst8[:, 3, b * HPG:(b + 1) * HPG].unsqueeze(2).broadcast_to((P, HPG, HD)), ALU.mult)
            phase_end(dve)

            heads = xn[:].rearrange("p b (g h d) -> p b g h d", g=GROUPS, d=HD)
            gate = gates[:].rearrange("p b (g e) -> p b g e", g=GROUPS)

            def finish(t, o):
                j, g, hh, br = t % 2, t // 8, t % 8 // 2, t % 2
                dve.tensor_tensor(mx2[:, j, 2:4], mx2[:, j, 0:2], gate[:, :, g, 3 * hh + 1 + br], ALU.mult)
                dve.drain()
                for b in range(NB):
                    dst = heads[:, b, g, hh, :]
                    dve.scalar_tensor_tensor(dst, o[:, b * HD:(b + 1) * HD], mx2[:, j, 2 + b:3 + b], dst,
                                             ALU.mult, ALU.add)

            attention(2 * H, NSA0, finish)
            dve.drain().then_inc(xn_ready, 1)
            n_norm["dve"] += 1
            evacuate_odd(oT, None)
            phase_end(dve)

            for k in range(KT):
                dve.tensor_tensor(mT[:, k, :], mT[:, k, :], gaT[:, k, :], ALU.mult)
            dve.wait_ge(gb_ready, 1)
            for m in range(4):
                dve.wait_ge(unit_done, U["branch_b"] + m + 1)
                two = slice(2 * m, 2 * m + 2)
                dve.tensor_tensor(gbT[:, two, :], ps[m % 2][:].rearrange("p (a t) -> p a t", a=2), gbT[:, two, :], ALU.mult)
                dve.drain()
                dve.tensor_tensor(mT[:, two, :], mT[:, two, :], gbT[:, two, :], ALU.add).then_inc(m_ready, 1)
            post_norm(0, 0)
            phase_end(dve)
            for b in range(2):
                dve.memset(uz[b], 0.0)
            first_units(U["up0"])
            normalise(x)
            split_unit(U["up0"], "ffn0", 0)
            split_unit(U["up0"], "ffn0", 1)
            split_input(small("g_ffn"))
            phase_end(dve)
            ffn_conv(U["up0"])
            post_norm(1, 1)
            phase_end(dve)
            first_units(U["even_f"])
            normalise(x)
            split_unit(U["even_f"], "even", 0)
            split_unit(U["even_f"], "even", 1)
            split_input(small("g_attn2")[:, 0:KT])
            phase_end(dve)
            for m in range(7):
                split_unit(U["even_f"], "even", m + 2)
                dve.wait_ge(unit_done, U["even_f"] + m + 1)
                src = ps[m % 2][HD:P, :].rearrange("p (a t) -> p a t", a=2)
                dst = (qa, qa, ka, ka, qb, qb, kb)[m]
                if m < 6:
                    dve.tensor_scalar(dst[0:HD, 4 * (m % 2) + 1:4 * (m % 2) + 4:2, :], src,
                                      1.0 if m in (2, 3) else SCALE, None, ALU.mult).then_inc(e_hi, 1)
                else:
                    dve.tensor_copy(kb[0:HD, 1, :], src[:, 0, :]).then_inc(e_hi, 1)
            dve.wait_ge(unit_done, U["even_v"] + 2)
            dve.tensor_copy(va[:, 1, :], ps[5][:])
            phase_end(dve)

            heads = xn[:].rearrange("p b (h d) -> p b h d", d=HD)
            with dve.Fori(0, 2) as i:
                def log_weights(s, n0):
                    j = s % 2
                    t0, t1, t2, t3 = sbt[j]
                    z = ps[j][:, 0:KEYS]
                    dve.wait_ge(pre_ready, 4 * i + s + 1)
                    dve.scalar_tensor_tensor(t1, z, 0.0, t0, ALU.max, ALU.add)
                    dve.tensor_tensor(t3, z, const("strict"), ALU.add)
                    dve.drain()
                    dve.tensor_tensor(t1, t1, const("nstrict"), ALU.mult)
                    dve.drain()
                    for a, b in ((0, P), (P, KEYS)):
                        dve.tensor_tensor_scan(t2[:, a:b][:, ::-1], t1[:, a:b][:, ::-1], t1[:, a:b][:, ::-1], 0.0,
                                               ALU.add, ALU.bypass)
                    dve.drain()
                    dve.tensor_tensor(sc[:, j, :], t2, t3, ALU.add).then_inc(max_ready, 1)

                def finish(t, o):
                    for b in range(NB):
                        dve.tensor_copy(heads[:, b, 4 * i + t, :], o[:, b * HD:(b + 1) * HD])

                attention(4, SB0 + 4 * i, finish, middle=log_weights)
            phase_end(dve)
            with dve.Fori(0, 2) as i:
                def finish(t, o):
                    j = t % 2
                    for b in range(NB):
                        dve.tensor_scalar(heads[:, b, SB_HEADS + 4 * i + t, :], o[:, b * HD:(b + 1) * HD],
                                          mx2[:, j, b:b + 1], None, ALU.mult)

                attention(4, SW0 + 4 * i, finish, sink=lambda s: sink_st[:, s % 2:s % 2 + 1])
            dve.drain().then_inc(xn_ready, 1)
            n_norm["dve"] += 1
            prepare_out(U["even_out"], "even_out")
            phase_end(dve)
            for m in (2, 3):
                split_unit(U["even_out"], "even_out", m)
            dve.wait_ge(unit_done, U["even_out"] + 4)
            add_rows()
            phase_end(dve)
            first_units(U["up1"])
            normalise(x)
            split_unit(U["up1"], "ffn1", 0)
            split_unit(U["up1"], "ffn1", 1)
            split_input(small("g_ffn2")[:, 0:KT])
            phase_end(dve)
            ffn_act(U["up1"], 1)
            dve.wait_ge(unit_done, U["down1"] + FT // 2)
            add_rows()
            phase_end(dve)
            first_units(U["mla_down"])
            normalise(x)
            split_unit(U["mla_down"], "mla", 0)
            split_unit(U["mla_down"], "mla", 1)
            split_input(small("g_attn2")[:, KT:2 * KT])
            phase_end(dve)

            rope = const("rope")
            dve.wait_ge(rope_pos, 16)
            dve.tensor_copy(posf, pos_i[:])
            dve.drain()
            dve.tensor_scalar(ang, posf, rope[:, 0:1], None, ALU.mult)
            dve.drain()
            dve.tensor_scalar(rope_t, ang, 1.0 / (2 * math.pi), rope[:, 1:2], ALU.mult, ALU.add)
            dve.drain()
            dve.tensor_copy(pos_n, rope_t)
            dve.drain()
            dve.tensor_copy(rope_t, pos_n)
            dve.drain()
            for part in TWO_PI:
                dve.scalar_tensor_tensor(ang, rope_t, -part, ang, ALU.mult, ALU.add)
                dve.drain()
            dve.tensor_scalar(rope_q[:, 0:1], rope[:, 1:2], 2 * math.pi, None, ALU.mult)
            dve.drain()
            dve.tensor_scalar(ang, ang, rope_q[:, 0:1], None, ALU.add)
            dve.drain()
            dve.tensor_scalar(ang, ang, 3.1415925, -3.1415925, ALU.min, ALU.max).then_inc(rope_in, 1)
            split_unit(U["mla_down"], "mla", 2)
            dve.wait_ge(m_root, 1)
            dve.reciprocal(rstd_f, rstd_f)
            dve.drain()
            for k in range(3):
                dve.scalar_tensor_tensor(cq[:, k, :], cq[:, k, :], small("g_q")[:, k:k + 1], rstd_f[:, 0, :],
                                         ALU.mult, ALU.mult)
            for k in range(2):
                m = dve.scalar_tensor_tensor(ckv[:, k, :], ckv[:, k, :], small("g_kv")[:, k:k + 1], rstd_f[:, 1, :],
                                             ALU.mult, ALU.mult)
            m.then_inc(m_norm, 1)
            dve.wait_ge(rope_ready, 1)
            dve.tensor_scalar(rope_t, rope_t, rope[:, 2:3], None, ALU.mult)
            dve.drain()
            dve.tensor_scalar(rope_q, rope_t, MLA_SCALE, None, ALU.mult)
            dve.drain()

            def rotate(dst, src, table):
                dve.tensor_tensor(rt[HD:HD + ROPE, 0, :], src[HD:HD + ROPE], table[HD:HD + ROPE], ALU.mult)
                dve.tensor_tensor(rt[HD:HD + ROPE, 1, :], src[HD + ROPE:P], table[HD + ROPE:P], ALU.mult)
                dve.drain()
                return dve.tensor_tensor(dst, rt[HD:HD + ROPE, 0, :], rt[HD:HD + ROPE, 1, :], ALU.add)

            rotate(kr[HD:HD + ROPE], ps[2][:, S:2 * S], rope_t).then_inc(kr_ready, 1)
            for h in range(H):
                dve.drain()
                dve.wait_ge(m_ev, h + 1)
                rotate(qm[HD:HD + ROPE, h, :], ps[6 + h % 2][:, 0:S], rope_q).then_inc(q_hi, 1)
            for t in range(8):
                dve.wait_ge(m_ev, H + t + 1)
                dve.tensor_copy(kmT[0:HD, 2 * t + 1, :], ps[t % 2][HD:P, 0:S]).then_inc(k_hi, 1)
            dve.wait_ge(unit_done, U["mla_uv"] + 1)
            for hf in range(2):
                dve.tensor_copy(vm[:, 1, hf * 512:(hf + 1) * 512], ps[4 + hf][:])
            phase_end(dve)
            with dve.Fori(0, 4) as i:
                def finish(t, o):
                    j = t % 2
                    for b in range(NB):
                        dve.tensor_scalar(heads[:, b, 4 * i + t, :], o[:, b * HD:(b + 1) * HD],
                                          mx2[:, j, b:b + 1], None, ALU.mult)

                attention(4, MLA0 + 4 * i, finish)
            dve.drain().then_inc(xn_ready, 1)
            n_norm["dve"] += 1
            prepare_out(U["mla_out"], "mla_out")
            phase_end(dve)
            for m in (2, 3):
                split_unit(U["mla_out"], "mla_out", m)
            dve.wait_ge(unit_done, U["mla_out"] + 4)
            add_rows()
            phase_end(dve)
            first_units(U["up2"])
            normalise(x)
            split_unit(U["up2"], "ffn2", 0)
            split_unit(U["up2"], "ffn2", 1)
            split_input(small("g_ffn2")[:, KT:2 * KT])
            phase_end(dve)
            ffn_act(U["up2"], 2)
            dve.wait_ge(unit_done, U["down2"] + FT // 2)
            add_rows()
            phase_end(dve)
            normalise(x)
            dve.wait_ge(row_in, 48)
            dve.drain()
            for b in range(NB):
                m = dve.tensor_tensor(xn[:, b, :], xn[:, b, :], grow[:], ALU.mult)
            m.then_inc(final_ready, 1)

        @block.gpsimd
        def _(pool):
            def split_unit(u0, name, m, i=0):
                pool.wait_ge(w_hi_p, SPLIT[name] + 4 * i + m + 1)
                pool.sem_inc(apart, 1)
                pool.tensor_tensor(w_lo[:, m % 2, WH:], ring[:, (u0 + m) % RING, WH:],
                                   w_hi[:, m % 2, WH:].bitcast(F32), ALU.subtract).then_inc(w_lo_p, 1)

            def ffn_units(u0, n_ffn):
                def split_act(j, i):
                    m = 4 * i + j
                    pool.wait_ge(ff_act, 4 + n_ffn * FT + m + 1)
                    pool.sem_inc(apart, 1)
                    pool.tensor_copy(a_hi[:, m, :], act_f[:, j % 2, :])
                    pool.drain()
                    pool.tensor_tensor(a_lo[:, m, :], act_f[:, j % 2, :], a_hi[:, m, :].bitcast(F32),
                                       ALU.subtract).then_inc(act_split, 1)

                if n_ffn == 0:
                    in_steps(pool, lambda j, i: split_unit(u0, f"ffn{n_ffn}", j + 2, i), split_act)
                else:
                    def step(j, i):
                        split_unit(u0, f"ffn{n_ffn}", j + 2, i)
                        split_act(j, i)

                    in_steps(pool, step)
                for m in range(FT, FU - 2):
                    split_unit(u0, f"ffn{n_ffn}", m + 2)

            def split_units(u0, name, *units):
                for m in units:
                    split_unit(u0, name, m)

            pool.drain().then_inc(act_split, 2)
            pool.drain().then_inc(q_staged, HEAD0)
            pool.drain().then_inc(b_staged, HEAD0)
            pool.dma_start(aux, aux_d).then_inc(aux_in, 16)
            phase_end(pool)
            pool.wait_ge(aux_in, 16)

            def stage_aux(m, j):
                pool.tensor_copy(ast[:, j, :], aux[:, m, :]).then_inc(staged, 1)
                pool.wait_ge(staged, m + 1)
                pool.sem_inc(apart, 1)
                pool.tensor_scalar(half[:, j, :], ast[:, j, W0:A0 + 1], 0.5, None, ALU.mult).then_inc(half_ready, 1)

            def finish_pair(n, j):
                pool.tensor_copy(ln_st, aux[:, n, LN_W:LN_B + 1])
                pool.drain()
                pool.wait_ge(vrec_ready, n + 1)
                pool.sem_inc(apart, 1)
                pool.tensor_tensor(y_f, y_f, vrec, ALU.mult)
                pool.drain()
                pool.tensor_scalar(y_f, y_f, ln_st[:, 0:1], ln_st[:, 1:2], ALU.mult, ALU.add)
                pool.drain()
                pool.tensor_tensor(y_f, y_f, bonus[:, j, :], ALU.add)
                pool.drain()
                pool.tensor_tensor(oaT[:, n, :], y_f, g_f[:, j, :], ALU.mult)
                pool.drain().then_inc(pair_done, 1)

            stage_aux(0, 0)
            stage_aux(1, 1)
            with pool.Fori(0, PAIRS // 2 - 1) as i:
                for j in range(2):
                    pool.wait_ge(bkar_ready, 2 * i + j + 1)
                    stage_aux(2 * i + j + 2, j)
                    finish_pair(2 * i + j, j)
            for n in (PAIRS - 2, PAIRS - 1):
                finish_pair(n, n % 2)
            phase_end(pool)

            for k in range(KT):
                pool.tensor_scalar(gaT[:, k, :], gaT[:, k, :], 0.5, 0.5, ALU.mult, ALU.add)
            phase_end(pool)
            phase_end(pool)

            def stage(N, n0, query, bias):
                for s in range(N):
                    j = s % 2
                    pool.wait_ge(s_mm, n0 + s - 1)
                    pool.sem_inc(apart, 1)
                    query(s, j).then_inc(q_staged, 1)
                    pool.wait_ge(max_ready, n0 + s - 1)
                    pool.sem_inc(apart, 1)
                    bias(s, j).then_inc(b_staged, 1)

            stage(2 * H, NSA0, lambda s, j: pool.tensor_copy(q_st[0:HD, j, :], qT[0:HD, s // 2, :]),
                  lambda s, j: pool.tensor_tensor(
                      b_st[:, j, :], dist, const("slope")[:, s // 2:s // 2 + 1].broadcast_to((P, KEYS)), ALU.mult))
            phase_end(pool)
            pool.dma_start(grow[:], rows_d[0:1, :].broadcast_to((P, D))).then_inc(row_in, 16)
            pool.wait_ge(gb_done, 8)
            for k in range(KT):
                m = pool.tensor_scalar(gbT[:, k, :], gbT[:, k, :], 0.5, 0.5, ALU.mult, ALU.add)
            m.then_inc(gb_ready, 1)
            phase_end(pool)
            split_units(U["up0"], "ffn0", 0, 1)
            pool.dma_start(grow[:], rows_d[1:2, :].broadcast_to((P, D))).then_inc(row_in, 16)
            phase_end(pool)
            ffn_units(U["up0"], 0)
            phase_end(pool)
            split_units(U["even_f"], "even", 0, 1)
            pool.dma_start(grow[:], rows_d[2:3, :].broadcast_to((P, D))).then_inc(row_in, 16)
            pool.dma_start(pos_i[:], pos_d.broadcast_to((P, S))).then_inc(rope_pos, 16)
            pool.dma_start(swb, swbias_d).then_inc(swb_in, 16)
            phase_end(pool)
            split_units(U["even_f"], "even", *range(2, 9))
            phase_end(pool)
            with pool.Fori(0, 2) as i:
                for s in range(4):
                    pool.wait_ge(s_mm, SB0 + 4 * i + s - 1)
                    pool.sem_inc(apart, 1)
                    pool.tensor_copy(q_st[0:HD, s % 2, :], qa[0:HD, 4 * i + s, :]).then_inc(q_staged, 1)
            phase_end(pool)
            pool.wait_ge(swb_in, 16)
            pool.drain().then_inc(b_staged, SB_HEADS)
            with pool.Fori(0, 2) as i:
                def bias(s, j):
                    h = 4 * i + s
                    pool.tensor_copy(b_st[:, j, P:KEYS], swb[:, h, :])
                    pool.tensor_copy(b_st[:, j, 0:P], swb[:, h, P:S])
                    return pool.tensor_copy(sink_st[:, j:j + 1], small("sinks").unsqueeze(2)[:, h, :])

                for s in range(4):
                    j = s % 2
                    pool.wait_ge(s_mm, SW0 + 4 * i + s - 1)
                    pool.sem_inc(apart, 1)
                    pool.tensor_copy(q_st[0:HD, j, :], qb[0:HD, 4 * i + s, :]).then_inc(q_staged, 1)
                    pool.wait_ge(p_ready, SW0 + 4 * i + s - 1)
                    pool.sem_inc(apart, 1)
                    bias(s, j).then_inc(b_staged, 1)
            split_units(U["even_out"], "even_out", 0, 1)
            phase_end(pool)
            split_units(U["even_out"], "even_out", 2, 3)
            phase_end(pool)
            split_units(U["up1"], "ffn1", 0, 1)
            phase_end(pool)
            ffn_units(U["up1"], 1)
            phase_end(pool)
            split_units(U["mla_down"], "mla", 0, 1)
            phase_end(pool)
            split_units(U["mla_down"], "mla", 2)
            pool.wait_ge(kr_ready, 1)
            for h in range(H):
                pool.tensor_copy(kmT[HD:HD + ROPE, h, :], kr[HD:HD + ROPE])
            phase_end(pool)
            pool.tensor_copy(b_st[:, 0, :], const("causal"))
            pool.tensor_copy(b_st[:, 1, :], const("causal"))
            pool.drain().then_inc(b_staged, H)
            with pool.Fori(0, 4) as i:
                for s in range(4):
                    pool.wait_ge(s_mm, MLA0 + 4 * i + s - 1)
                    pool.sem_inc(apart, 1)
                    pool.tensor_copy(q_st[0:HD + ROPE, s % 2, :], qm[0:HD + ROPE, 4 * i + s, :]).then_inc(q_staged, 1)
            split_units(U["mla_out"], "mla_out", 0, 1)
            phase_end(pool)
            split_units(U["mla_out"], "mla_out", 2, 3)
            phase_end(pool)
            split_units(U["up2"], "ffn2", 0, 1)
            phase_end(pool)
            ffn_units(U["up2"], 2)
            phase_end(pool)
            pool.wait_ge(final_ready, 1)
            pool.dma_start(out, xn[:]).then_inc(out_done, 16)
            pool.wait_ge(out_done, 16)


def _tiles(w, c0, c1):
    return w[:, c0:c1].reshape(w.shape[0] // P, P, c1 - c0).transpose(1, 0, 2)


def _constants():
    c = np.zeros((P, N_CONST), np.float32)

    def put(name, v):
        c[:, CO[name][0]:CO[name][1]] = v

    p = np.arange(P)
    put("ident", np.eye(P))
    put("headsum", (p[:, None] // HD == p[None, :] // HD))
    put("ones", 1.0)
    put("chunk", (np.arange(S) % CH != 0)[None, :])
    s = p[:, None] % CH
    put("tri", np.concatenate([s < np.arange(CH)[None, :], s <= np.arange(CH)[None, :]], 1))
    rel = np.concatenate([p[:, None] - p[None, :], P + p[:, None] - np.arange(S)[None, :]], 1)
    put("dist", np.where(rel >= 0, rel, BIG))
    put("causal", np.where(rel >= 0, 0.0, -BIG))
    put("strict", np.where(rel > 0, 0.0, -BIG))
    put("nstrict", np.where(rel > 0, -1.0, 0.0))
    slopes = np.exp2(-8.0 * np.arange(1, H + 1) / H)
    put("slope", -slopes[None, :])
    t = (np.arange(NB)[None, :] * P + p[:, None]).reshape(P, 1, NB, 1, 1)
    mid = (np.arange(N_CMP) * 16 + 15.5).reshape(1, 1, 1, 1, N_CMP)
    end = (np.arange(N_CMP) * 16 + 31).reshape(1, 1, 1, 1, N_CMP)
    sl = slopes.reshape(1, GROUPS, 1, HPG, 1)
    put("cmpbias", np.where(end <= t, -sl * (t - mid), -BIG).reshape(P, -1))
    half = ROPE // 2
    freq = (10000.0 ** (-np.arange(half, dtype=np.float32) / np.float32(half))).astype(np.float32)
    rope = np.zeros((P, 3), np.float32)
    rope[HD:, 0] = np.tile(freq, 4)
    rope[HD:HD + ROPE, 1] = 0.25
    rope[:, 2] = 1.0
    rope[HD + ROPE:HD + ROPE + half, 2] = -1.0
    put("rope", rope)
    return c


def _bucket(rel):
    rel = np.maximum(rel, 0)
    relf = np.maximum(rel, 1).astype(np.float32)
    large = 16 + (np.log(relf / np.float32(16)) / np.float32(math.log(8.0)) * np.float32(16)).astype(np.int32)
    return np.where(rel < 16, rel, np.minimum(large, 31))


def _layout(v):
    cols = lambda a: a.reshape(-1, P).T
    w_in = v["w_in"][0]
    q0 = 3360
    kc, vc, ks, vs, kw, vw, gl, ga, gb = 4384, 4640, 4896, 5152, 5408, 5664, 5920, 5968, 6992
    units = []

    def fm(w, *ranges):
        units.append(np.concatenate([_tiles(w, a, b) for a, b in ranges], 2).reshape(P, UNIT))

    def tm(w, c0, c1, per):
        t = _tiles(w, c0, c1)
        for k in range(0, t.shape[1], per):
            units.append(t[:, k:k + per].reshape(P, -1))

    fm(w_in, (3072, 3328))
    for n in range(PAIRS):
        a, b = n * P, (n + 1) * P
        fm(w_in, (a, b), (D + a, D + b))
        fm(w_in, (2 * D + a, 2 * D + b), (ga + a, ga + b))
    for n in range(4):
        fm(w_in, (q0 + n * 256, q0 + (n + 1) * 256))
    for c in (kc, vc, ks, kw):
        fm(w_in, (c, c + 256))
    vsw = np.concatenate([w_in[:, vs:vs + 256], w_in[:, vw:vw + 256]], 1)
    tm(vsw, 0, 512, 4)
    for name in ("cmp_w1_k", "cmp_w1_v"):
        units.append(v[name][0].reshape(16, P, 128).transpose(1, 0, 2).reshape(P, UNIT))
    for n in range(4):
        fm(w_in, (gb + n * 256, gb + (n + 1) * 256))
    for w in (v["w_branch_rwkv"][0], v["w_branch_nsa"][0]):
        for n in range(4):
            fm(w, (n * 256, (n + 1) * 256))
    tm(v["w_out"][0], 0, D, 2)

    def ffn(up, off, down):
        for n in range(FT):
            fm(up, (n * P, (n + 1) * P), (off + n * P, off + (n + 1) * P))
        tm(down, 0, D, 2)

    ffn(v["ffn_up"][0], F_FF, v["ffn_down"][0])
    w = v["even_w_in_2"][0]
    for c in (0, 256, 512, 768, 1536, 1792):
        fm(w, (c, c + 256))
    fm(w, (2048, 2304))
    tm(w, 1024, 1536, 4)
    tm(v["even_w_out_2"][0], 0, D, 2)
    up = [np.concatenate([v["ffn_w_gate_2"][n], v["ffn_w_up_2"][n]], 1) for n in range(2)]
    ffn(up[0], F_FF, v["ffn_w_down_2"][0])
    w = v["mla_w_down_2"][0]
    r0 = Q_RANK + KV_RANK
    half = ROPE // 2
    swap = np.concatenate([w[:, :r0], np.zeros((D, HD), np.float32), w[:, r0:],
                           w[:, r0 + half:], w[:, r0:r0 + half]], 1)
    for n in range(3):
        fm(swap, (n * 256, (n + 1) * 256))
    w = v["mla_w_uq_2"][0].reshape(Q_RANK, H, HD + ROPE)
    w = np.concatenate([w, w[:, :, HD + half:], w[:, :, HD:HD + half]], 2).reshape(Q_RANK, H * P)
    for n in range(4):
        t = _tiles(w, n * 512, (n + 1) * 512).reshape(P, -1)
        units.append(np.concatenate([t, np.zeros((P, UNIT - t.shape[1]), np.float32)], 1))
    w = v["mla_w_ukv_2"][0].reshape(KV_RANK, H, 2 * HD)
    units.append(_tiles(w[:, :, :HD].reshape(KV_RANK, D), 0, D).reshape(P, UNIT))
    units.append(_tiles(w[:, :, HD:].reshape(KV_RANK, D), 0, D).reshape(P, UNIT))
    tm(v["mla_w_o_2"][0], 0, D, 2)
    ffn(up[1], F_FF, v["ffn_w_down_2"][1])
    weights = np.stack(units)
    assert weights.shape == (N_UNITS, P, UNIT), weights.shape

    aux = np.zeros((P, PAIRS, AUX), np.float32)
    heads = lambda a: a.reshape(-1, PAIRS, P)
    aux[0:64, :, 0:128] = heads(v["rwkv_w2"][0])
    aux[64:128, :, 0:128] = heads(v["rwkv_a2"][0])
    aux[:, :, 128:256] = heads(v["rwkv_g2"][0][:P])
    aux[0:32, :, 256:384] = heads(v["rwkv_g2"][0][P:])
    mu = v["rwkv_mu"][0]
    for c, a in ((MU_R, mu[:D]), (MU_K, mu[D:2 * D]), (MU_V, mu[2 * D:3 * D]), (W0, v["rwkv_w0"]),
                 (A0, v["rwkv_a0"]), (K_K, v["rwkv_k_k"]), (K_A, v["rwkv_k_a"]), (R_K, v["rwkv_r_k"]),
                 (LN_W, v["rwkv_ln_w"]), (LN_B, v["rwkv_ln_b"])):
        aux[:, :, c] = cols(a)

    small = np.zeros((P, N_SMALL), np.float32)

    def put(name, a, rows=P):
        small[:rows, SO[name][0]:SO[name][0] + a.reshape(rows, -1).shape[1]] = a.reshape(rows, -1)

    put("w_small", np.concatenate([_tiles(w_in, 3328, 3360), _tiles(w_in, gl, gl + 48)], 2))
    mu_l = np.zeros((3, P), np.float32)
    mu_l[0], mu_l[1], mu_l[2, :32] = mu[3072:3200], mu[3200:3328], mu[3328:]
    put("mu_lora", mu_l.T)
    put("g_mix", cols(v["norm_mix_pre"]))
    put("g_ffn", cols(v["norm_ffn_pre"]))
    put("g_attn2", cols(v["attn_norm_2"]))
    put("g_ffn2", cols(v["ffn_norm_2"]))
    put("g_q", cols(v["mla_q_norm_2"]))
    put("g_kv", cols(v["mla_kv_norm_2"]))
    taps = np.concatenate([v["ffn_conv_w"][0], v["ffn_conv_b"]], 0)
    put("conv", taps.reshape(4, 2, FT, P).transpose(3, 2, 1, 0))
    put("cmp_w2", np.concatenate([v["cmp_w2_k"][0], v["cmp_w2_v"][0]], 1))
    put("cmp_pos", np.stack([v["cmp_pos_k"][0].T, v["cmp_pos_v"][0].T], 1), HD)
    put("sinks", np.repeat(v["even_sinks_2"], P, 0))

    rel = P + np.arange(P)[:, None] - np.arange(S)[None, :]
    table = v["rel_bias_table_2"][_bucket(rel)]
    swb = np.where(((rel >= 0) & (rel < 128))[:, :, None], table, np.float32(-BIG))
    swb = np.ascontiguousarray(swb.transpose(0, 2, 1))
    rows = np.stack([v["norm_mix_post"][0], v["norm_ffn_post"][0], v["final_norm_2"]])
    return {
        "weights": weights, "aux": aux, "consts": _constants(), "small": small, "rows": rows,
        "swbias": swb.astype(np.float32),
        "x": np.ascontiguousarray(v["x"][0].reshape(NB, P, D).transpose(1, 0, 2)),
        "positions": np.ascontiguousarray(v["positions_2"]),
    }


def kernel(**inputs):
    import concourse.bacc as _bacc
    from concourse.bass_utils import run_bass_kernel_spmd as _run

    arrays = _layout({k: np.asarray(a) for k, a in inputs.items()})
    nc = _bacc.Bacc("TRN2", target_bir_lowering=False, num_devices=1)
    args = [nc.dram_tensor("in_" + k, a.shape, mybir.dt.from_np(a.dtype), kind="ExternalInput").ap()
            for k, a in arrays.items()]
    out = nc.dram_tensor("out_0", (P, NB, D), F32, kind="ExternalOutput").ap()
    build(nc, args, out)
    r = _run(nc, [{"in_" + k: a for k, a in arrays.items()}], core_ids=[0])
    y = np.asarray(r.results[0]["out_0"])
    return np.ascontiguousarray(y.transpose(1, 0, 2)).reshape(1, S, D)
```
